# Optimizing a Trainium2 kernel written in Bass

```python
import math
import jax, jax.numpy as jnp
from jax import lax
import numpy as np

D_MODEL = 1024
BATCH = 1
SEQ = 512
DEPTH = 1

CTX_LEN = 256
GRID_W = 64
EPS = 1e-6
MIX_WIDTH = D_MODEL
GLA_WIDTH = MIX_WIDTH // 2
DIFF_WIDTH = MIX_WIDTH - GLA_WIDTH
GLA_HEADS = 4
GLA_DV = GLA_WIDTH // GLA_HEADS
GLA_DK = GLA_DV // 2
GLA_QK = GLA_HEADS * GLA_DK
GLA_GATE_RANK = 16
GLA_GATE_NORM = 16.0
GLA_CHUNK = 64
DIFF_HEADS = 4
DIFF_DV = DIFF_WIDTH // DIFF_HEADS
DIFF_DH = DIFF_DV // 2
ROPE_BASE = 10000.0
ROPE_AXIS_DIM = DIFF_DH // 2
Q_BLOCK = 128
FFN_HIDDEN = ((8 * D_MODEL // 3 + 255) // 256) * 256
IN_SIZES = (GLA_QK, GLA_QK, GLA_WIDTH, GLA_WIDTH, 2 * GLA_GATE_RANK, DIFF_WIDTH, DIFF_WIDTH, DIFF_WIDTH)
W_IN_COLS = sum(IN_SIZES)


def rmsnorm(x, g):
    xf = x.astype(jnp.float32)
    y = xf * lax.rsqrt(jnp.mean(xf * xf, axis=-1, keepdims=True) + EPS)
    return (y * g.astype(jnp.float32)).astype(x.dtype)

def modulate(x, g, shift, scale):
    return rmsnorm(x, g) * (1 + scale) + shift

def split_heads(t, n_heads):
    b, n, _ = t.shape
    return t.reshape(b, n, n_heads, -1).transpose(0, 2, 1, 3)

def merge_heads(t):
    b, h, n, d = t.shape
    return t.transpose(0, 2, 1, 3).reshape(b, n, h * d)

def adaln_params(cond, w_mod, b_mod):
    return jnp.split(jax.nn.silu(cond) @ w_mod + b_mod, 6, axis=-1)

def axial_rope_tables(n_tokens):
    rows = n_tokens // GRID_W
    t = jnp.arange(rows * GRID_W)
    row = (t // GRID_W).astype(jnp.float32)
    col = (t % GRID_W).astype(jnp.float32)
    n_freq = ROPE_AXIS_DIM // 2
    inv_freq = ROPE_BASE ** (-jnp.arange(n_freq, dtype=jnp.float32) / n_freq)
    ang = jnp.stack([row[:, None] * inv_freq, col[:, None] * inv_freq], axis=1)
    return jnp.cos(ang), jnp.sin(ang)

def apply_axial_rope(x, cos, sin):
    xr = x.reshape(x.shape[:-1] + (2, 2, ROPE_AXIS_DIM // 2))
    x1, x2 = xr[..., 0, :], xr[..., 1, :]
    cs = cos[:, None].astype(x.dtype)
    sn = sin[:, None].astype(x.dtype)
    out = jnp.stack([x1 * cs - x2 * sn, x2 * cs + x1 * sn], axis=-2)
    return out.reshape(x.shape)

def project(h, w_in):
    points = np.cumsum(IN_SIZES)[:-1].tolist()
    return jnp.split(h @ w_in, points, axis=-1)

def gla_inputs(parts, gate_up, gate_bias):
    gq, gk, gv, gr, gdown = parts[:5]
    q = split_heads(gq, GLA_HEADS) * (GLA_DK ** -0.5)
    k = split_heads(gk, GLA_HEADS)
    v = split_heads(gv, GLA_HEADS)
    down = gdown.astype(jnp.float32).reshape(gdown.shape[:-1] + (2, GLA_GATE_RANK))
    logits = jnp.einsum('bnzr,zrk->bnzk', down, gate_up.astype(jnp.float32)) + gate_bias.astype(jnp.float32)
    log_alpha = jax.nn.log_sigmoid(logits) / GLA_GATE_NORM
    g_f = split_heads(log_alpha[:, :, 0], GLA_HEADS)
    g_b = split_heads(log_alpha[:, :, 1], GLA_HEADS)
    return q, k, v, gr, g_f, g_b

def gla_chunk_scan(q, k, v, g, s0):
    b, h, n, dk = q.shape
    dv = v.shape[-1]
    nc = n // GLA_CHUNK

    def chunks(t):
        return jnp.moveaxis(t.astype(jnp.float32).reshape(b, h, nc, GLA_CHUNK, t.shape[-1]), 2, 0)

    mask = jnp.tril(jnp.ones((GLA_CHUNK, GLA_CHUNK), dtype=bool))

    def step(state, inp):
        qc, kc, vc, gc = inp
        cum = jnp.cumsum(gc, axis=2)
        o_inter = jnp.einsum('bhcd,bhde->bhce', qc * jnp.exp(cum), state)
        rel = cum[:, :, :, None, :] - cum[:, :, None, :, :]
        decay = jnp.exp(jnp.where(mask[:, :, None], rel, -jnp.inf))
        attn = jnp.einsum('bhid,bhjd,bhijd->bhij', qc, kc, decay)
        o = o_inter + jnp.einsum('bhij,bhje->bhie', attn, vc)
        last = cum[:, :, -1:, :]
        state = jnp.exp(last[:, :, 0, :, None]) * state + jnp.einsum('bhcd,bhce->bhde', kc * jnp.exp(last - cum), vc)
        return state, o

    s_final, o = lax.scan(step, s0, (chunks(q), chunks(k), chunks(v), chunks(g)))
    o = jnp.moveaxis(o, 0, 2).reshape(b, h, n, dv)
    return s_final, o.astype(v.dtype)

def gla_bidir(q, k, v, g_f, g_b, s0_f, s0_b):
    flip = lambda t: jnp.flip(t, axis=2)
    s_f, o_f = gla_chunk_scan(q, k, v, g_f, s0_f)
    s_b, o_b = gla_chunk_scan(flip(q), flip(k), flip(v), flip(g_b), s0_b)
    return s_f, s_b, o_f + flip(o_b)

def gla_merge(o, r, norm_g):
    return merge_heads(rmsnorm(o, norm_g)) * jax.nn.silu(r)

def diff_qkv(parts, q_norm_g, k_norm_g):
    dq, dk, dv = parts[5:]
    b, n, _ = dq.shape
    q = rmsnorm(dq.reshape(b, n, DIFF_HEADS, 2, DIFF_DH).transpose(0, 2, 1, 3, 4), q_norm_g)
    k = rmsnorm(dk.reshape(b, n, DIFF_HEADS, 2, DIFF_DH).transpose(0, 2, 1, 3, 4), k_norm_g)
    v = split_heads(dv, DIFF_HEADS)
    return q, k, v

def diff_attend(q, k_all, v_all, lam):
    b, h, n = q.shape[:3]
    nb = n // Q_BLOCK
    q_blocks = jnp.moveaxis(q.reshape(b, h, nb, Q_BLOCK, 2, DIFF_DH), 2, 0)

    def one_block(qb):
        s = jnp.einsum('bhqcd,bhkcd->bhcqk', qb, k_all).astype(jnp.float32) * (DIFF_DH ** -0.5)
        p = jax.nn.softmax(s, axis=-1)
        a = (p[:, :, 0] - lam.astype(jnp.float32) * p[:, :, 1]).astype(v_all.dtype)
        return jnp.einsum('bhqk,bhkd->bhqd', a, v_all)

    o = lax.map(one_block, q_blocks)
    return jnp.moveaxis(o, 0, 2).reshape(b, h, n, DIFF_DV)

def diff_merge(o, norm_g, lam_init):
    return merge_heads(rmsnorm(o, norm_g) * (1.0 - lam_init))

def swiglu(h, w_in, w_out):
    gate, up = jnp.split(h @ w_in, 2, axis=-1)
    return (jax.nn.silu(gate) * up) @ w_out

def first_inputs(seed: int = 0) -> dict:
    key = jax.random.key(seed)
    ks = jax.random.split(key, 20)
    f32 = jnp.float32
    nrm = lambda k, shape, s: jax.random.normal(k, shape, f32) * s
    return {
        "x": nrm(ks[0], (BATCH, SEQ, D_MODEL), 1.0),
        "c": nrm(ks[1], (BATCH, D_MODEL), 1.0),
        "ctx": nrm(ks[2], (BATCH, CTX_LEN, D_MODEL), 1.0),
        "c_ctx": nrm(ks[3], (D_MODEL,), 1.0),
        "w_mod": nrm(ks[4], (DEPTH, D_MODEL, 6 * D_MODEL), 0.5 * D_MODEL ** -0.5),
        "b_mod": nrm(ks[5], (DEPTH, 6 * D_MODEL), 0.01),
        "norm1_g": 1.0 + nrm(ks[6], (DEPTH, D_MODEL), 0.02),
        "w_in": nrm(ks[7], (DEPTH, D_MODEL, W_IN_COLS), D_MODEL ** -0.5),
        "gla_gate_up": nrm(ks[8], (DEPTH, 2, GLA_GATE_RANK, GLA_QK), GLA_GATE_RANK ** -0.5),
        "gla_gate_bias": nrm(ks[9], (DEPTH, 2, GLA_QK), 0.1),
        "gla_norm_g": 1.0 + nrm(ks[10], (DEPTH, GLA_DV), 0.02),
        "diff_q_norm_g": 1.0 + nrm(ks[11], (DEPTH, DIFF_DH), 0.02),
        "diff_k_norm_g": 1.0 + nrm(ks[12], (DEPTH, DIFF_DH), 0.02),
        "diff_lambda_q": nrm(ks[13], (DEPTH, 2, DIFF_DH), 0.1),
        "diff_lambda_k": nrm(ks[14], (DEPTH, 2, DIFF_DH), 0.1),
        "diff_norm_g": 1.0 + nrm(ks[15], (DEPTH, DIFF_DV), 0.02),
        "w_out": nrm(ks[16], (DEPTH, MIX_WIDTH, D_MODEL), MIX_WIDTH ** -0.5),
        "norm2_g": 1.0 + nrm(ks[17], (DEPTH, D_MODEL), 0.02),
        "w_ffn_in": nrm(ks[18], (DEPTH, D_MODEL, 2 * FFN_HIDDEN), D_MODEL ** -0.5),
        "w_ffn_out": nrm(ks[19], (DEPTH, FFN_HIDDEN, D_MODEL), FFN_HIDDEN ** -0.5),
    }

def first_block(x, c, ctx, c_ctx, w_mod, b_mod, norm1_g, w_in, gla_gate_up, gla_gate_bias, gla_norm_g,
              diff_q_norm_g, diff_k_norm_g, diff_lambda_q, diff_lambda_k, diff_norm_g, w_out, norm2_g,
              w_ffn_in, w_ffn_out):
    b = x.shape[0]
    cos, sin = axial_rope_tables(x.shape[1])
    zero_state = jnp.zeros((b, GLA_HEADS, GLA_DK, GLA_DV), jnp.float32)
    for l in range(DEPTH):
        lam_init = 0.8 - 0.6 * math.exp(-0.3 * l)
        lam = (jnp.exp(jnp.sum(diff_lambda_q[l, 0] * diff_lambda_k[l, 0]))
               - jnp.exp(jnp.sum(diff_lambda_q[l, 1] * diff_lambda_k[l, 1])) + lam_init)
        sh1, sc1, gt1, sh2, sc2, gt2 = [m[:, None, :] for m in adaln_params(c, w_mod[l], b_mod[l])]
        csh1, csc1, cgt1, csh2, csc2, cgt2 = adaln_params(c_ctx, w_mod[l], b_mod[l])

        pc = project(modulate(ctx, norm1_g[l], csh1, csc1), w_in[l])
        qg_c, kg_c, vg_c, r_c, gf_c, gb_c = gla_inputs(pc, gla_gate_up[l], gla_gate_bias[l])
        s_f, s_b, og_c = gla_bidir(qg_c, kg_c, vg_c, gf_c, gb_c, zero_state, zero_state)
        qd_c, kd_c, vd_c = diff_qkv(pc, diff_q_norm_g[l], diff_k_norm_g[l])

        px = project(modulate(x, norm1_g[l], sh1, sc1), w_in[l])
        qg, kg, vg, r, gf, gb = gla_inputs(px, gla_gate_up[l], gla_gate_bias[l])
        _, _, og = gla_bidir(qg, kg, vg, gf, gb, s_f, s_b)
        qd, kd, vd = diff_qkv(px, diff_q_norm_g[l], diff_k_norm_g[l])
        qd = apply_axial_rope(qd, cos, sin)
        kd = apply_axial_rope(kd, cos, sin)
        od = diff_attend(qd, jnp.concatenate([kd_c, kd], axis=2), jnp.concatenate([vd_c, vd], axis=2), lam)
        mix = jnp.concatenate([gla_merge(og, r, gla_norm_g[l]), diff_merge(od, diff_norm_g[l], lam_init)], axis=-1) @ w_out[l]
        x = x + gt1 * mix
        x = x + gt2 * swiglu(modulate(x, norm2_g[l], sh2, sc2), w_ffn_in[l], w_ffn_out[l])

        if l < DEPTH - 1:
            od_c = diff_attend(qd_c, kd_c, vd_c, lam)
            mix_c = jnp.concatenate([gla_merge(og_c, r_c, gla_norm_g[l]), diff_merge(od_c, diff_norm_g[l], lam_init)], axis=-1) @ w_out[l]
            ctx = ctx + cgt1 * mix_c
            ctx = ctx + cgt2 * swiglu(modulate(ctx, norm2_g[l], csh2, csc2), w_ffn_in[l], w_ffn_out[l])
    return x


CHUNK = 64
D_FF = 2816
A_HEADS = 8
A_HEAD_DIM = 64
A_Q_W = A_HEADS * A_HEAD_DIM
IDX_HEADS = 8
IDX_DIM = 64
TOPK_MAX = 256
B_HEADS = 8
QK_NOPE = 64
QK_ROPE = 32
V_DIM = 64
Q_LORA = 384
KV_LORA = 256
B_V_W = B_HEADS * V_DIM
ROPE_THETA = 10000.0
NUM_BUCKETS = 32
MAX_DISTANCE = 128
IN_SIZES_2 = (A_Q_W, A_HEAD_DIM, A_HEAD_DIM, IDX_HEADS * IDX_DIM, IDX_DIM, IDX_HEADS,
            Q_LORA, KV_LORA, QK_ROPE, 2 * D_MODEL)
IN_COLS = sum(IN_SIZES_2)
N_ADA = 9


def rmsnorm_2(x, g):
    xf = x.astype(jnp.float32)
    y = xf * lax.rsqrt(jnp.mean(xf * xf, axis=-1, keepdims=True) + EPS)
    return (y * g.astype(jnp.float32)).astype(x.dtype)

def modulate_2(h, shift, scale):
    return h * (1 + scale[:, None, :]) + shift[:, None, :]

def swiglu_2(h, w_in, w_down):
    g, u = jnp.split(h @ w_in, 2, axis=-1)
    return (jax.nn.silu(g) * u) @ w_down

def rope_angles(positions):
    half = QK_ROPE // 2
    freqs = ROPE_THETA ** (-2.0 * jnp.arange(half, dtype=jnp.float32) / QK_ROPE)
    ang = positions.astype(jnp.float32)[..., None] * freqs
    return jnp.cos(ang), jnp.sin(ang)

def apply_rope(x, cos, sin):
    cos = cos.astype(x.dtype)
    sin = sin.astype(x.dtype)
    x1, x2 = jnp.split(x, 2, axis=-1)
    return jnp.concatenate([x1 * cos - x2 * sin, x2 * cos + x1 * sin], axis=-1)

def t5_bucket(rel):
    half = NUM_BUCKETS // 2
    max_exact = half // 2
    ret = jnp.where(rel > 0, half, 0)
    n = jnp.abs(rel)
    nf = jnp.maximum(n, 1).astype(jnp.float32)
    large = max_exact + (jnp.log(nf / max_exact) / math.log(MAX_DISTANCE / max_exact)
                         * (half - max_exact)).astype(jnp.int32)
    large = jnp.minimum(large, half - 1)
    return ret + jnp.where(n < max_exact, n, large)

def to_blocks(a, nb):
    return jnp.swapaxes(a.reshape(a.shape[0], nb, Q_BLOCK, *a.shape[2:]), 0, 1)

def from_blocks(o):
    o = jnp.swapaxes(o, 0, 1)
    return o.reshape(o.shape[0], o.shape[1] * o.shape[2], -1)

def block_limit(t0):
    tq = t0 + jnp.arange(Q_BLOCK, dtype=jnp.int32)
    return (tq // CHUNK + 1) * CHUNK

def dsa_attention(q_a, k_a, v_a, q_idx, k_idx, w_idx, positions, rel_bias, topk):
    B, S = q_a.shape[0], q_a.shape[1]
    nb = S // Q_BLOCK
    key_ids = jnp.arange(S, dtype=jnp.int32)
    gather = jax.vmap(lambda a, i: a[i])
    idx_scale = IDX_DIM ** -0.5
    head_w_scale = IDX_HEADS ** -0.5
    attn_scale = A_HEAD_DIM ** -0.5
    k_idx_f = k_idx.astype(jnp.float32)

    def body(args):
        q_b, qi_b, wi_b, qpos_b, t0 = args
        limit = block_limit(t0)
        dots = jnp.einsum('bqhd,bsd->bqhs', qi_b.astype(jnp.float32), k_idx_f) * idx_scale
        score = jnp.einsum('bqh,bqhs->bqs', wi_b.astype(jnp.float32) * head_w_scale,
                           jax.nn.relu(dots))
        admissible = key_ids[None, :] < limit[:, None]
        score = jnp.where(admissible[None], score, -jnp.inf)
        _, sel = lax.top_k(score, topk)
        valid = sel < limit[None, :, None]
        k_sel = gather(k_a, sel)
        v_sel = gather(v_a, sel)
        pos_sel = gather(positions, sel)
        bias = rel_bias[t5_bucket(pos_sel - qpos_b[..., None])]
        s = jnp.einsum('bqhd,bqkd->bqhk', q_b, k_sel).astype(jnp.float32) * attn_scale
        s = s + jnp.moveaxis(bias, -1, 2).astype(jnp.float32)
        s = jnp.where(valid[:, :, None, :], s, -jnp.inf)
        p = jax.nn.softmax(s, axis=-1).astype(v_sel.dtype)
        return jnp.einsum('bqhk,bqkd->bqhd', p, v_sel)

    t0s = jnp.arange(nb, dtype=jnp.int32) * Q_BLOCK
    o = lax.map(body, (to_blocks(q_a, nb), to_blocks(q_idx, nb), to_blocks(w_idx, nb),
                       to_blocks(positions, nb), t0s))
    return from_blocks(o)

def mla_attention(q_nope, q_pe, k_nope, k_pe, v):
    S = q_nope.shape[1]
    nb = S // Q_BLOCK
    key_ids = jnp.arange(S, dtype=jnp.int32)
    scale = (QK_NOPE + QK_ROPE) ** -0.5

    def body(args):
        qn, qp, t0 = args
        limit = block_limit(t0)
        s = (jnp.einsum('bqhd,bshd->bhqs', qn, k_nope)
             + jnp.einsum('bqhr,bsr->bhqs', qp, k_pe)).astype(jnp.float32) * scale
        mask = key_ids[None, :] < limit[:, None]
        s = jnp.where(mask[None, None], s, -jnp.inf)
        p = jax.nn.softmax(s, axis=-1).astype(v.dtype)
        return jnp.einsum('bhqs,bshd->bqhd', p, v)

    t0s = jnp.arange(nb, dtype=jnp.int32) * Q_BLOCK
    o = lax.map(body, (to_blocks(q_nope, nb), to_blocks(q_pe, nb), t0s))
    return from_blocks(o)

def second_inputs(seed: int = 0) -> dict:
    key = jax.random.key(seed)
    ks = jax.random.split(key, 32)
    f32 = jnp.float32

    def nrm(k, shape, fan_in, mult=1.0):
        return jax.random.normal(k, shape, f32) * (mult * fan_in ** -0.5)

    def gain(k, shape):
        return 1.0 + 0.05 * jax.random.normal(k, shape, f32)

    x = jax.random.normal(ks[0], (BATCH, SEQ, D_MODEL), f32)
    c = jax.random.normal(ks[1], (BATCH, D_MODEL), f32)
    start = jax.random.randint(ks[2], (BATCH, 1), 0, 4096, dtype=jnp.int32)
    positions = start + jnp.arange(SEQ, dtype=jnp.int32)[None, :]
    L = DEPTH
    return {
        "x": x,
        "c": c,
        "positions": positions,
        "w_ada": nrm(ks[3], (L, D_MODEL, N_ADA * D_MODEL), D_MODEL, 0.5),
        "b_ada": 0.02 * jax.random.normal(ks[4], (L, N_ADA * D_MODEL), f32),
        "g_ffn1": gain(ks[5], (L, D_MODEL)),
        "w_ffn1_in": nrm(ks[6], (L, D_MODEL, 2 * D_FF), D_MODEL),
        "w_ffn1_down": nrm(ks[7], (L, D_FF, D_MODEL), D_FF),
        "g_mix": gain(ks[8], (L, D_MODEL)),
        "w_in": nrm(ks[9], (L, D_MODEL, IN_COLS), D_MODEL),
        "g_cq": gain(ks[10], (L, Q_LORA)),
        "w_uq": nrm(ks[11], (L, Q_LORA, B_HEADS * (QK_NOPE + QK_ROPE)), Q_LORA),
        "g_ckv": gain(ks[12], (L, KV_LORA)),
        "w_uk": nrm(ks[13], (L, KV_LORA, B_HEADS * QK_NOPE), KV_LORA),
        "w_uv": nrm(ks[14], (L, KV_LORA, B_HEADS * V_DIM), KV_LORA),
        "rel_bias": 0.5 * jax.random.normal(ks[15], (NUM_BUCKETS, A_HEADS), f32),
        "w_o_a": nrm(ks[16], (L, A_Q_W, D_MODEL), A_Q_W),
        "w_o_b": nrm(ks[17], (L, B_V_W, D_MODEL), B_V_W),
        "w_out": nrm(ks[18], (L, D_MODEL, D_MODEL), D_MODEL),
        "g_ffn2": gain(ks[19], (L, D_MODEL)),
        "w_ffn2_in": nrm(ks[20], (L, D_MODEL, 2 * D_FF), D_MODEL),
        "w_ffn2_down": nrm(ks[21], (L, D_FF, D_MODEL), D_FF),
        "g_final": gain(ks[22], (D_MODEL,)),
    }

def second_block(x, c, positions, w_ada, b_ada, g_ffn1, w_ffn1_in, w_ffn1_down, g_mix, w_in,
              g_cq, w_uq, g_ckv, w_uk, w_uv, rel_bias, w_o_a, w_o_b, w_out,
              g_ffn2, w_ffn2_in, w_ffn2_down, g_final):
    B, S, _ = x.shape
    topk = min(TOPK_MAX, S // 4)
    offsets = []
    acc = 0
    for n in IN_SIZES_2[:-1]:
        acc += n
        offsets.append(acc)
    cos, sin = rope_angles(positions)

    for l in range(DEPTH):
        mod = jax.nn.silu(c) @ w_ada[l] + b_ada[l]
        sh1, sc1, gt1, sh2, sc2, gt2, sh3, sc3, gt3 = jnp.split(mod, N_ADA, axis=-1)

        h = modulate_2(rmsnorm_2(x, g_ffn1[l]), sh1, sc1)
        x = x + 0.5 * gt1[:, None, :] * swiglu_2(h, w_ffn1_in[l], w_ffn1_down[l])

        h = modulate_2(rmsnorm_2(x, g_mix[l]), sh2, sc2)
        proj = h @ w_in[l]
        (q_a, k_a, v_a, q_idx, k_idx, w_idx, c_q, c_kv, k_rope,
         gate_logits) = jnp.split(proj, offsets, axis=-1)

        o_a = dsa_attention(q_a.reshape(B, S, A_HEADS, A_HEAD_DIM), k_a, v_a,
                            q_idx.reshape(B, S, IDX_HEADS, IDX_DIM), k_idx, w_idx,
                            positions, rel_bias, topk)

        q_b = (rmsnorm_2(c_q, g_cq[l]) @ w_uq[l]).reshape(B, S, B_HEADS, QK_NOPE + QK_ROPE)
        q_nope, q_pe = jnp.split(q_b, [QK_NOPE], axis=-1)
        c_kv_n = rmsnorm_2(c_kv, g_ckv[l])
        k_nope = (c_kv_n @ w_uk[l]).reshape(B, S, B_HEADS, QK_NOPE)
        v_b = (c_kv_n @ w_uv[l]).reshape(B, S, B_HEADS, V_DIM)
        q_pe = apply_rope(q_pe, cos[:, :, None, :], sin[:, :, None, :])
        k_pe = apply_rope(k_rope, cos, sin)
        o_b = mla_attention(q_nope, q_pe, k_nope, k_pe, v_b)

        g_a, g_b = jnp.split(jax.nn.sigmoid(gate_logits), 2, axis=-1)
        y = g_a * (o_a @ w_o_a[l]) + g_b * (o_b @ w_o_b[l])
        x = x + gt2[:, None, :] * (y @ w_out[l])

        h = modulate_2(rmsnorm_2(x, g_ffn2[l]), sh3, sc3)
        x = x + 0.5 * gt3[:, None, :] * swiglu_2(h, w_ffn2_in[l], w_ffn2_down[l])

    return rmsnorm_2(x, g_final)


def setup_inputs(seed=0):
    out = dict(first_inputs(seed))
    for name, value in second_inputs(seed + 1).items():
        if name != "x":
            out[name + "_2"] = value
    return out


def reference(
    x, c, ctx, c_ctx, w_mod, b_mod, norm1_g, w_in, gla_gate_up, gla_gate_bias, gla_norm_g,
    diff_q_norm_g, diff_k_norm_g, diff_lambda_q, diff_lambda_k, diff_norm_g, w_out, norm2_g,
    w_ffn_in, w_ffn_out, c_2, positions_2, w_ada_2, b_ada_2, g_ffn1_2, w_ffn1_in_2,
    w_ffn1_down_2, g_mix_2, w_in_2, g_cq_2, w_uq_2, g_ckv_2, w_uk_2, w_uv_2, rel_bias_2,
    w_o_a_2, w_o_b_2, w_out_2, g_ffn2_2, w_ffn2_in_2, w_ffn2_down_2, g_final_2,
):
    x = first_block(
        x, c, ctx, c_ctx, w_mod, b_mod, norm1_g, w_in, gla_gate_up, gla_gate_bias, gla_norm_g,
        diff_q_norm_g, diff_k_norm_g, diff_lambda_q, diff_lambda_k, diff_norm_g, w_out, norm2_g,
        w_ffn_in, w_ffn_out,
    )
    return second_block(
        x, c_2, positions_2, w_ada_2, b_ada_2, g_ffn1_2, w_ffn1_in_2, w_ffn1_down_2, g_mix_2,
        w_in_2, g_cq_2, w_uq_2, g_ckv_2, w_uk_2, w_uv_2, rel_bias_2, w_o_a_2, w_o_b_2, w_out_2,
        g_ffn2_2, w_ffn2_in_2, w_ffn2_down_2, g_final_2,
    )


_drawn_inputs = setup_inputs


def setup_inputs(seed=0):
    import zlib

    import numpy as np

    out = dict(_drawn_inputs(seed))
    spreads = {}
    factors = {'b_mod': 3.929,
     'norm1_g': 8.0,
     'gla_gate_bias': 8.0,
     'gla_norm_g': 8.0,
     'diff_q_norm_g': 8.0,
     'diff_k_norm_g': 8.0,
     'diff_lambda_q': 8.0,
     'diff_lambda_k': 8.0,
     'diff_norm_g': 36.022,
     'norm2_g': 8.0,
     'b_ada_2': 4.072,
     'g_ffn1_2': 8.0,
     'g_mix_2': 7.828,
     'g_cq_2': 8.0,
     'w_uq_2': 3.414,
     'g_ckv_2': 8.0,
     'w_uk_2': 3.861,
     'rel_bias_2': 20.722,
     'g_ffn2_2': 7.447}
    for name, (base, spread) in spreads.items():
        noise = np.random.default_rng([zlib.crc32(name.encode()), seed]).standard_normal(out[name].shape)
        drawn = base * np.exp(spread * noise) if base else spread * noise
        out[name] = __import__('jax').numpy.asarray(drawn.astype(out[name].dtype))
    for name, factor in factors.items():
        out[name] = (out[name] * factor).astype(out[name].dtype)
    return out
```

```python
import math
from contextlib import ExitStack

import numpy as np

import concourse.bass as bass
from concourse import mybir

F32 = mybir.dt.float32
F32R = mybir.dt.float32r
BF16 = mybir.dt.bfloat16
I32 = mybir.dt.int32
U32 = mybir.dt.uint32
ALU = mybir.AluOpType
ACT = mybir.ActivationFunctionType
AX = mybir.AxisListType.X

P = 128
D = 1024
KD = D // P
N = 512
NCTX = 256
NALL = NCTX + N
NT, NTC, NTA = N // P, NCTX // P, NALL // P
FFN = 2816
KF = FFN // P
EPS = 1e-6
HEADS = 4
GLA_DK, DV, DIFF_DH = 64, 128, 64
LEVELS = [64, 32, 16, 8, 4, 2, 1]
GRID_W = 64
LAM_INIT = 0.8 - 0.6 * math.exp(-0.3 * 0)
H2 = 8
DH2, ROPE2 = 64, 32
QK2 = DH2 + ROPE2
Q_LORA, KV_LORA = 384, 256
TOPK = 128
ROUNDS = TOPK // 8
QG = 16
NEG = -3.0e38
TAKEN = -3.3e38
HIDE = -2.0 ** 100
BUCKET_START = [1, 2, 3, 4, 5, 6, 7, 8, 12, 16, 23, 32, 46, 64, 91]
BUCKETS = list(range(15, -1, -1)) + list(range(17, 32))
BUCKET_FROM = [-1e30] + [1 - s for s in reversed(BUCKET_START)] + [s for s in BUCKET_START] + [1e30]

RING = 4
SPLIT = 2
SLOT = KD * P
N_SLOTS = 404

VEC = {}
for _name, _w in (("norm1_g", 8), ("norm2_g", 8), ("g_ffn1", 8), ("g_mix", 8), ("g_ffn2", 8), ("g_final", 8),
                  ("b_mod", 48), ("b_ada", 72), ("gla_g", 1), ("dq_g", 1), ("dk_g", 1), ("dn_g", 1),
                  ("g_cq", 3), ("g_ckv", 2), ("cond", 16), ("cond2", 8), ("gate_b", 4),
                  ("lam_q", 128), ("lam_k", 128), ("gate_up", 512), ("bias_at", 8), ("bias_before", 8)):
    VEC[_name] = (sum(w for _, w in VEC.values()), _w)
NVEC = sum(w for _, w in VEC.values())
CST = {}
for _name, _w in (("ident", 128), ("one", 1), ("comp", 2), ("eps", 1), ("rot2", 32), ("freq", 1), ("bucket_from", 1),
                  ("own_query", 64)):
    CST[_name] = (sum(w for _, w in CST.values()), _w)
NCST = sum(w for _, w in CST.values())
CSTA = {}
for _name, _w in (("rot", 128), ("cos", 512), ("sin", 512), ("carry", 512), ("levels", 128 * (1 + len(LEVELS)))):
    CSTA[_name] = (sum(w for _, w in CSTA.values()), _w)
NCSTA = sum(w for _, w in CSTA.values())


def full_columns(name, c, width=P):
    return (name, [(k * P, P, ((c, c + width, 0),)) for k in range(KD)])


def weight_rows(name, k):
    return (name, [(k * P, P, ((m * P, m * P + P, 0),)) for m in range(KD)])


def build(nc, A):
    ctx = ExitStack()
    sems = {}

    def S(name):
        if name not in sems:
            sems[name] = ctx.enter_context(nc.semaphore(name))
        return sems[name]

    top = [(nc.sbuf_base + 31) // 32 * 32]
    bytes_of = {F32: 4, F32R: 4, I32: 4, BF16: 2, U32: 4}

    def sb(name, shape, dt=F32):
        size = int(np.prod(shape[1:])) * bytes_of[dt]
        t = nc.alloc_sbuf_tensor_at(name, shape, dt, offset=top[0])
        top[0] += (size + 31) // 32 * 32
        assert top[0] <= nc.sbuf_usable_end, (name, top[0], nc.sbuf_usable_end)
        return t

    raw = [sb(f"raw{i}", [P, SLOT]) for i in range(RING)]
    w_hi = [sb(f"w_hi{i}", [P, SLOT], F32R) for i in range(SPLIT)]
    w_lo = [sb(f"w_lo{i}", [P, SLOT], F32R) for i in range(SPLIT)]
    xT = sb("xT", [P, KD, N])
    hh = sb("hh", [P, KD, N], F32R)
    hl = sb("hl", [P, KD, N], F32R)
    sq = [sb(f"sq{i}", [P, NALL]) for i in range(2)]
    t1 = [sb(f"t1{i}", [P, NALL]) for i in range(2)]
    vec = sb("vec", [P, NVEC])
    cst = sb("cst", [P, NCST])
    mod = sb("mod", [P, 48, 2])
    ada = sb("ada", [P, 72])
    cond = sb("cond", [P, KD, 2])
    cond2 = sb("cond2", [P, KD, 1])
    gain = {n: sb(f"gain_{n}", [P, KD]) for n in ("x1", "c1", "x2", "f1", "mx", "f2")}
    half_gate = {n: sb(f"half_gate_{n}", [P, KD]) for n in ("f1", "f2")}
    std = {}
    rs = {}
    for n, w in (("nx", NT), ("nc", NTC), ("nq", 32), ("nk", 48), ("no", 16), ("ng", 16), ("n2", NT), ("nf1", NT),
                 ("nm", NT), ("ncq", NT), ("nckv", NT), ("nf2", NT), ("nfin", NT)):
        std[n], rs[n] = sb(f"std_{n}", [P, w]), sb(f"rs_{n}", [P, w])
    lam = sb("lam", [P, 8])
    gain_dn = sb("gain_dn", [P, 1])
    gain_dq = sb("gain_dq", [P, 1])
    region = top[0]

    gkx = sb("gkx", [P, 2, N])
    gkc = sb("gkc", [P, 2, NCTX])
    gqx = sb("gqx", [P, 2, N])
    rT = sb("rT", [P, HEADS, N])
    vt = sb("vt", [P, NTA, HEADS * DV])
    dn = sb("dn", [32, NALL])
    csta = sb("csta", [P, NCSTA])
    region_diff = top[0]
    dq = sb("dq", [P, HEADS, N])
    dk = sb("dk", [P, HEADS, NALL])
    dvt = sb("dvt", [P, NTA, HEADS * DV])
    rot_q = sb("rot_q", [P, P])
    rot_k = sb("rot_k", [P, P])
    region_tmp = top[0]
    cT = sb("cT", [P, KD, NCTX])
    ch = sb("ch", [P, KD, NCTX], F32R)
    cl = sb("cl", [P, KD, NCTX], F32R)
    top[0] = region_tmp
    prob = [sb(f"prob{i}", [P, 2, NALL]) for i in range(2)]
    probT = [sb(f"probT{i}", [P, NTA, P]) for i in range(2)]
    od = sb("od", [P, HEADS, N])
    neg_max = [sb(f"neg_max{i}", [P, 2]) for i in range(2)]
    total = [sb(f"total{i}", [P, 2]) for i in range(2)]
    inv = [sb(f"inv{i}", [P, 4]) for i in range(2)]
    top[0] = region_diff
    yb = [sb(f"yb{i}", [P, NALL]) for i in range(2)]
    cumx = sb("cumx", [P, 2, 2 * N])
    cumc = sb("cumc", [P, 2, 2 * NCTX])
    kdT = sb("kdT", [P, 2, NTA, 2 * P])
    decay = sb("decay", [P, 2, 2, NTA])
    states = sb("states", [P, 2, 2, NT + 1, DV])
    qe = sb("qe", [P, 2, 2 * N])
    attnT = sb("attnT", [P, NT, HEADS, P])
    region_levels = top[0]
    lq = sb("lq", [P, 2 * N])
    lk = sb("lk", [P, 2 * N])
    top[0] = region_levels
    og = sb("og", [P, HEADS, N])

    top[0] = region
    act_hi = sb("act_hi", [P, KF * N], F32R)
    act_lo = sb("act_lo", [P, KF * N], F32R)
    silu = [sb(f"silu{i}", [P, N]) for i in range(2)]
    prod = [sb(f"prod{i}", [P, N]) for i in range(2)]

    top[0] = region
    qa = sb("qa", [DH2, N // QG, H2, QG])
    kva = sb("kva", [P, N])
    vat = sb("vat", [P, NT, P])
    region_qi = top[0]
    qi = sb("qi", [P, HEADS, N])
    ki = sb("ki", [P, N])
    wkr = sb("wkr", [P, N])
    posf = sb("posf", [P, N])
    posi = sb("posi", [P, N], I32)
    qfrom = sb("qfrom", [P, P])
    qposi = sb("qposi", [P, P], I32)
    cosr = sb("cosr", [P, N])
    sinr = sb("sinr", [P, N])
    wt = sb("wt", [P, NT, H2])
    best = sb("best", [P, 3, 8])
    sm = {n: [sb(f"{n}{i}", [P, 1]) for i in range(2)] for n in ("mla_max", "mla_sum", "mla_inv", "dsa_max", "dsa_sum", "dsa_inv")}
    region_lora = top[0]
    cq = sb("cq", [P, 3, N])
    cqh = sb("cqh", [P, 3, N], F32R)
    cql = sb("cql", [P, 3, N], F32R)
    region_ckv = top[0]
    ckv = sb("ckv", [P, 2, N])
    ckvh = sb("ckvh", [P, 2, N], F32R)
    ckvl = sb("ckvl", [P, 2, N], F32R)
    top[0] = region_lora
    kb = sb("kb", [QK2, H2, N])
    top[0] = region_lora
    oah = sb("oah", [P, HEADS, N], F32R)
    oal = sb("oal", [P, HEADS, N], F32R)
    top[0] = region_ckv
    obh = sb("obh", [P, HEADS, N], F32R)
    obl = sb("obl", [P, HEADS, N], F32R)
    score = [sb(f"score{i}", [P, (i + 2) * P]) for i in range(3)]
    hide = [sb(f"hide{i}", [P, (i + 1) * P], BF16) for i in range(4)]
    region_mla = top[0]
    qb = sb("qb", [QK2, H2, N])
    vbt = sb("vbt", [P, NT, H2 * DH2])
    top[0] = region_qi
    mp = [sb(f"mp{i}", [P, N]) for i in range(2)]
    mpT = [sb(f"mpT{i}", [P, NT, P]) for i in range(2)]
    top[0] = region_mla
    NSTEP = 8
    step = [sb(f"step{i}", [P, N], F32R) for i in range(NSTEP)]
    table = sb("table", [P, 4, P])
    table_hi = sb("table_hi", [P, 4, P], F32R)
    table_lo = sb("table_lo", [P, 4, P], F32R)
    delta = sb("delta", [P, H2])
    identb = sb("identb", [P, P // QG, H2, QG], BF16)
    pp, ppT = mp, mpT
    top[0] = region
    yh = sb("yh", [P, KD, N], F32R)
    yl = sb("yl", [P, KD, N], F32R)
    top[0] = region_mla
    sig_a = [sb(f"sig_a{i}", [P, N]) for i in range(2)]
    sig_b = [sb(f"sig_b{i}", [P, N]) for i in range(2)]

    top[0] = region
    fin = sb("fin", [P, KD, N])

    ps = ctx.enter_context(nc.psum_tensor("ps", [P, 8, 512], F32))

    def v(name, a=0, b=None):
        o, w = VEC[name]
        return vec[:, o + a:o + (w if b is None else b)]

    def c(name, a=0, b=None):
        o, w = CST[name]
        return cst[:, o + a:o + (w if b is None else b)]

    def ca(name, a=0, b=None):
        o, w = CSTA[name]
        return csta[:, o + a:o + (w if b is None else b)]

    ident = c("ident")

    stream = []
    slot_of = []
    after = []
    bank_uses = [0] * 8
    bank_empties = [0] * 8
    bank_freed = [None] * 8
    held = {}
    marks = {}

    def landed(n):
        return S(f"landed{n % RING}"), 16 * (n // RING + 1)

    def spent(n):
        return S(f"spent{n % RING}"), n // RING + 1

    def bank_full(b):
        return S(f"bank_full{b}")

    def bank_empty(b):
        return S(f"bank_empty{b}")

    def mark(name, ins):
        marks[name] = marks.get(name, 0) + 1
        ins.then_inc(S(name), 1)
        return marks[name]

    def settle(eng, name):
        eng.wait_ge(S(name), marks[name])

    def claim(pe, b, key, freed=None):
        if bank_freed[b] is not None:
            pe.wait_ge(*bank_freed[b])
        bank_uses[b] += 1
        if freed is None:
            bank_empties[b] += 1
            freed = (bank_empty(b), bank_empties[b])
        bank_freed[b] = freed
        held[key] = (b, bank_uses[b], freed)

    def also(b, key):
        bank_uses[b] += 1
        held[key] = (b, bank_uses[b], bank_freed[b])

    def full(eng, key):
        b, n, _ = held[key]
        eng.wait_ge(bank_full(b), n)
        return b

    def read(eng, key):
        b, _, freed = held[key]
        eng.wait_ge(*freed)
        return b

    def take_slot(pe, spec):
        n = len(stream)
        stream.append(spec)
        slot_of.append(n)
        after.append(None)
        pe.wait_ge(*spent(n))
        return len(slot_of) - 1

    def three_passes(pe, out, g, tile, width, rh, rl, first, last):
        wh = w_hi[g % SPLIT][:, tile * P:tile * P + width]
        wl = w_lo[g % SPLIT][:, tile * P:tile * P + width]
        pairs = ((wh, rh), (wh, rl), (wl, rh))
        for i, (w, r) in enumerate(pairs):
            mm = pe.matmul(out, w, r, start=first and i == 0, stop=last and i == 2)
        return mm

    next_split = [0]

    def split_slots(act, upto):
        while next_split[0] <= upto and next_split[0] < len(slot_of):
            g = next_split[0]
            act.wait_ge(*landed(slot_of[g]))
            if g >= SPLIT:
                act.wait_ge(*after[g - SPLIT])
            act.activation(w_hi[g % SPLIT][:, :], raw[slot_of[g] % RING][:, :], ACT.Copy).then_inc(S("w_hi_ready"), 1)
            next_split[0] += 1

    def ada_slot(pe, name, chunk, col, width, rhs):
        n = len(stream)
        stream.append(full_columns(name, chunk * P))
        pe.wait_ge(*landed(n))
        for k in range(KD):
            mm = pe.matmul(ps[:, 7, col:col + width], raw[n % RING][:, k * P:(k + 1) * P], rhs[:, k, :],
                           start=(k == 0), stop=(k == KD - 1))
        mm.then_inc(spent(n)[0], 1)
        return n

    ada_todo = [("w_mod", j) for j in range(48)] + [("w_ada", j) for j in range(72)]
    ada_batches = [[]]
    mod_copies = [0]

    def ada_slots(pe, count):
        for _ in range(min(count, len(ada_todo))):
            name, j = ada_todo.pop(0)
            if not ada_batches[-1]:
                pe.wait_ge(S("cond_ready"), 2)
                if bank_freed[7] is not None:
                    pe.wait_ge(*bank_freed[7])
            if name == "w_mod":
                n = ada_slot(pe, name, j, 2 * j, 2, cond)
            else:
                n = ada_slot(pe, name, j, 96 + j, 1, cond2)
            ada_batches[-1].append((name, j, n))

    def ada_batch_end():
        mod_copies[0] += len({name for name, _, _ in ada_batches[-1]})
        bank_freed[7] = (S("mod_ready"), mod_copies[0])
        ada_batches.append([])

    def ada_copy(dve, batch):
        done = ada_batches[batch]
        dve.wait_ge(*spent(done[-1][2]))
        m = [j for name, j, _ in done if name == "w_mod"]
        a = [j for name, j, _ in done if name == "w_ada"]
        if m:
            mark("mod_ready", dve.tensor_tensor(
                mod[:, m[0]:m[-1] + 1, :], ps[:, 7, 2 * m[0]:2 * m[-1] + 2].rearrange("p (j t) -> p j t", t=2),
                v("b_mod", m[0], m[-1] + 1).unsqueeze(2).broadcast_to([P, len(m), 2]), ALU.add))
        if a:
            mark("mod_ready", dve.tensor_tensor(
                ada[:, a[0]:a[-1] + 1], ps[:, 7, 96 + a[0]:97 + a[-1]], v("b_ada", a[0], a[-1] + 1), ALU.add))
        settle(dve, "mod_ready")

    norm_base = {}
    norm_next = dict(sq=0, sq_used=0, rs=0, t1=0, hi=0, ready=0, gated=0)

    def norm_starts(key, chunks, gated=0):
        norm_base[key] = dict(norm_next)
        for what, count in (("sq", chunks), ("sq_used", chunks - 1), ("rs", 1), ("t1", chunks), ("hi", chunks), ("ready", chunks),
                            ("gated", gated)):
            norm_next[what] += count

    def norm(key, what, count):
        return S("norm_" + what), norm_base[key][what] + count

    def norm_tensor(pe, key, chunks, tokens, ba, bb):
        tiles = tokens // P
        norm_starts(key, chunks)
        claim(pe, ba, key + "_ss")
        for k in range(chunks):
            pe.wait_ge(*norm(key, "sq", k + 1))
            for t in range(tiles):
                mm = pe.matmul(ps[:, ba, t:t + 1], sq[k % 2][:, t * P:(t + 1) * P], c("one"),
                               start=(k == 0 and t == 0), stop=(k == chunks - 1), skip_group_check=True)
            mm.then_inc(S("norm_sq_used") if k < chunks - 1 else bank_full(ba), 1)
        claim(pe, bb, key + "_rs", norm(key, "t1", chunks))
        pe.wait_ge(*norm(key, "rs", 1))
        for t in range(tiles):
            mm = pe.matmul(ps[:, bb, t * P:(t + 1) * P], rs[key][:, t:t + 1].broadcast_to([P, P]), ident,
                           start=True, stop=True)
        mm.then_inc(bank_full(bb), 1)

    def norm_scalar(act, key, src, chunks, tokens, width, hi, shift, ready):
        for k in range(chunks):
            ready(act, k)
            if k >= 2:
                act.wait_ge(*norm(key, "sq_used", k - 1))
            act.activation(sq[k % 2][:, 0:tokens], src[:, k, :], ACT.Square).then_inc(S("norm_sq"), 1)
        b = full(act, key + "_ss")
        act.activation(std[key][:, :], ps[:, b, 0:tokens // P], ACT.Sqrt, bias=c("eps"), scale=1.0 / width)\
           .then_inc(bank_empty(b), 1)
        if hi is None:
            return
        for k in range(chunks):
            act.wait_ge(*norm(key, "t1", k + 1))
            if shift is None:
                act.activation(hi[:, k, :], t1[k % 2][:, 0:tokens], ACT.Copy).then_inc(S("norm_hi"), 1)
            else:
                act.activation(hi[:, k, :], t1[k % 2][:, 0:tokens], ACT.Identity, bias=shift(k)).then_inc(S("norm_hi"), 1)

    def norm_vector(dve, key, src, chunks, tokens, gains, hi, lo, shift, out=None):
        read(dve, key + "_ss")
        dve.reciprocal(rs[key][:, :], std[key][:, :]).then_inc(S("norm_rs"), 1)
        b = full(dve, key + "_rs")

        def low(k):
            dve.wait_ge(*norm(key, "hi", k + 1))
            if shift is None:
                dve.tensor_tensor(lo[:, k, :], t1[k % 2][:, 0:tokens], hi[:, k, :].bitcast(F32), ALU.subtract)\
                   .then_inc(S("norm_ready"), 1)
            else:
                dve.scalar_tensor_tensor(out=lo[:, k, :], in0=t1[k % 2][:, 0:tokens], scalar=shift(k),
                                         in1=hi[:, k, :].bitcast(F32), op0=ALU.add, op1=ALU.subtract)\
                   .then_inc(S("norm_ready"), 1)

        for k in range(chunks):
            if k >= 2 and out is None:
                dve.wait_ge(*norm(key, "ready", k - 1))
            to = out[:, k, :] if out is not None else t1[k % 2][:, 0:tokens]
            dve.scalar_tensor_tensor(out=to, in0=src[:, k, :], scalar=gains(k), in1=ps[:, b, 0:tokens],
                                     op0=ALU.mult, op1=ALU.mult).then_inc(S("norm_t1"), 1)
            if k >= 1 and out is None:
                low(k - 1)
        if out is None:
            low(chunks - 1)


    def head_norm_tensor(pe, key, ba, bbs, gated=0):
        norm_starts(key, HEADS, gated)
        claim(pe, ba, key + "_ss")
        for h in range(HEADS):
            pe.wait_ge(*norm(key, "sq", h + 1))
            for t in range(NT):
                mm = pe.matmul(ps[:, ba, h * NT + t:h * NT + t + 1], sq[h % 2][:, t * P:(t + 1) * P], c("one"),
                               start=True, stop=True)
            mm.then_inc(S("norm_sq_used") if h < HEADS - 1 else bank_full(ba), 1)
        pe.wait_ge(*norm(key, "rs", 1))
        for h in range(HEADS):
            b = bbs[h % 2]
            claim(pe, b, (key, h), norm(key, "t1", h + 1))
            for t in range(NT):
                mm = pe.matmul(ps[:, b, t * P:(t + 1) * P], rs[key][:, h * NT + t:h * NT + t + 1].broadcast_to([P, P]),
                               ident, start=True, stop=True)
            mm.then_inc(bank_full(b), 1)

    def head_norm_scalar(act, key, src, chunk0, ready, final):
        for h in range(HEADS):
            ready(act, h)
            if h >= 2:
                act.wait_ge(*norm(key, "sq_used", h - 1))
            act.activation(sq[h % 2][:, 0:N], src[:, h, :], ACT.Square).then_inc(S("norm_sq"), 1)
        b = full(act, key + "_ss")
        act.activation(std[key][:, :], ps[:, b, 0:HEADS * NT], ACT.Sqrt, bias=c("eps"), scale=1.0 / DV)\
           .then_inc(bank_empty(b), 1)
        for h in range(HEADS):
            act.wait_ge(*norm(key, final, h + 1))
            act.activation(hh[:, chunk0 + h, :], t1[h % 2][:, 0:N], ACT.Copy).then_inc(S("norm_hi"), 1)

    def head_norm_vector(dve, key, src, chunk0, gains, times):
        read(dve, key + "_ss")
        dve.reciprocal(rs[key][:, :], std[key][:, :]).then_inc(S("norm_rs"), 1)
        for h in range(HEADS):
            b = full(dve, (key, h))
            if h >= 2:
                dve.wait_ge(*norm(key, "ready", h - 1))
            dve.scalar_tensor_tensor(out=t1[h % 2][:, 0:N], in0=src[:, h, :], scalar=gains, in1=ps[:, b, :],
                                     op0=ALU.mult, op1=ALU.mult).then_inc(S("norm_t1"), 1)
            if times is not None:
                dve.wait_ge(*norm(key, "t1", h + 1))
                dve.tensor_tensor(t1[h % 2][:, 0:N], t1[h % 2][:, 0:N], times[:, h, :], ALU.mult)\
                   .then_inc(S("norm_gated"), 1)
            dve.wait_ge(*norm(key, "hi", h + 1))
            dve.tensor_tensor(hl[:, chunk0 + h, :], t1[h % 2][:, 0:N], hh[:, chunk0 + h, :].bitcast(F32), ALU.subtract)\
               .then_inc(S("norm_ready"), 1)

    GQ, GK, GV, GR, GD, DQ, DK, DVC = 0, 256, 512, 1024, 1536, 1568, 2080, 2592
    chunks_a = ([("dk", h, DK + h * P, P, True) for h in range(HEADS)] + [("dv", h, DVC + h * P, P, True) for h in range(HEADS)]
                + [("dq", h, DQ + h * P, P, False) for h in range(HEADS)] + [("gd", 0, GD, 32, True)]
                + [("gk", i, GK + i * P, P, True) for i in range(2)] + [("gv", h, GV + h * P, P, True) for h in range(HEADS)]
                + [("gq", i, GQ + i * P, P, False) for i in range(2)] + [("gr", h, GR + h * P, P, False) for h in range(HEADS)])
    v_chunks = [(name, h) for name, h, *_ in chunks_a if name in ("dv", "gv")]
    chunk_of = {(name, h): i for i, (name, h, *_) in enumerate(chunks_a)}

    def projections_tensor(pe):
        def to_tokens(name, h):
            i = v_chunks.index((name, h))
            read(pe, ("c", chunk_of[(name, h)]))
            claim(pe, 4, ("vA", i))
            for t in range(4):
                mm = pe.transpose(ps[:, 4, t * P:(t + 1) * P], sq[i % 2][:, t * P:(t + 1) * P], ident)
            mm.then_inc(bank_full(4), 1)
            claim(pe, 5, ("vB", i))
            for t in range(4, NTA):
                mm = pe.transpose(ps[:, 5, (t - 4) * P:(t - 3) * P], sq[i % 2][:, t * P:(t + 1) * P], ident)
            mm.then_inc(bank_full(5), 1)

        last = None
        for i, (name, h, col, width, both) in enumerate(chunks_a):
            g = take_slot(pe, full_columns("w_in", col, width))
            for key, b, rh, rl, tokens, key_norm in ((("x", i), i % 2, hh, hl, N, "nx"), (("c", i), 2 + i % 2, ch, cl, NCTX, "nc"))[:1 + both]:
                claim(pe, b, key)
                for k in range(KD):
                    if i == 0:
                        pe.wait_ge(*norm(key_norm, "ready", k + 1))
                    mm = three_passes(pe, ps[0:width, b, 0:tokens], g, k, width, rh[:, k, :], rl[:, k, :], k == 0, k == KD - 1)
                mm.then_inc(bank_full(b), 1)
                after[g] = (bank_full(b), bank_uses[b])
            if last:
                to_tokens(*last)
            last = (name, h) if name in ("dv", "gv") else None
            ada_slots(pe, 2)
        ada_batch_end()

    def projections_scalar(act):
        split_slots(act, 1)
        for i, (name, h, col, width, both) in enumerate(chunks_a):
            ctx_to, x_to, func, scale = {
                "dk": lambda: (dk[:, h, 0:NCTX], dk[:, h, NCTX:], ACT.Copy, 1.0),
                "dv": lambda: (sq[v_chunks.index((name, h)) % 2][:, 0:NCTX], sq[v_chunks.index((name, h)) % 2][:, NCTX:], ACT.Copy, 1.0),
                "gv": lambda: (sq[v_chunks.index((name, h)) % 2][:, 0:NCTX], sq[v_chunks.index((name, h)) % 2][:, NCTX:], ACT.Copy, 1.0),
                "dq": lambda: (None, dq[:, h, :], ACT.Copy, 1.0),
                "gd": lambda: (dn[:, 0:NCTX], dn[:, NCTX:], ACT.Copy, 1.0),
                "gk": lambda: (gkc[:, h, :], gkx[:, h, :], ACT.Copy, 1.0),
                "gq": lambda: (None, gqx[:, h, :], ACT.Copy, GLA_DK ** -0.5),
                "gr": lambda: (None, rT[:, h, :], ACT.Silu, 1.0)}[name]()
            if name in ("dv", "gv") and v_chunks.index((name, h)) >= 2:
                full(act, ("vB", v_chunks.index((name, h)) - 2))
            b = full(act, ("x", i))
            ins = act.activation(x_to, ps[0:width, b, 0:N], func, scale=scale).then_inc(bank_empty(b), 1)
            if both:
                b = full(act, ("c", i))
                act.activation(ctx_to, ps[0:width, b, 0:NCTX], func, scale=scale).then_inc(bank_empty(b), 1)
            split_slots(act, i + 2)

    def projections_vector(dve):
        for i, (name, h) in enumerate(v_chunks):
            to = dvt if name == "dv" else vt
            b = full(dve, ("vA", i))
            dve.tensor_copy(to[:, 0:4, h * DV:(h + 1) * DV], ps[:, b, :].rearrange("p (t d) -> p t d", t=4)).then_inc(bank_empty(b), 1)
            b = full(dve, ("vB", i))
            dve.tensor_copy(to[:, 4:NTA, h * DV:(h + 1) * DV], ps[:, b, 0:2 * P].rearrange("p (t d) -> p t d", t=2))\
               .then_inc(bank_empty(b), 1)

    pairs = [(h, qt) for h in range(HEADS) for qt in range(NT)]
    flat = ps[:, :, :].rearrange("p b n -> p (b n)")

    def diff_tensor(pe):
        claim(pe, 4, "nq_ss")
        claim(pe, 5, "nk_ss")
        for i in range(2 * HEADS):
            h, tiles, b = i % HEADS, (NT, NTA)[i // HEADS], 4 + i // HEADS
            pe.wait_ge(S("diff_sq"), i + 1)
            for t in range(tiles):
                at = 2 * (h * tiles + t)
                mm = pe.matmul(ps[:, b, at:at + 2], sq[i % 2][:, t * P:(t + 1) * P], c("comp"), start=True, stop=True)
            mm.then_inc(bank_full(b) if h == HEADS - 1 else S("diff_sq_used"), 1)

        def spread(b, key, at, t):
            for comp in range(2):
                mm = pe.matmul(ps[64 * comp:64 * comp + 64, b, t * P:(t + 1) * P],
                               rs[key][:, at + comp:at + comp + 1].broadcast_to([P, DIFF_DH]), ident, start=True, stop=True)
            return mm

        pe.wait_ge(S("rot_ready"), 2)
        for h in range(HEADS):
            claim(pe, 0, ("rot_q", h))
            pe.matmul(ps[:, 0, :], rot_q[:, :], dq[:, h, :], start=True, stop=True).then_inc(bank_full(0), 1)
            claim(pe, 1, ("rs_q", h), (S("dq_ready"), h + 1))
            if h == 0:
                pe.wait_ge(S("diff_rs"), 1)
            for t in range(NT):
                mm = spread(1, "nq", 2 * (h * NT + t), t)
            mm.then_inc(bank_full(1), 1)
            claim(pe, 2, ("rot_k", h))
            pe.matmul(ps[:, 2, :], rot_k[:, :], dk[:, h, NCTX:], start=True, stop=True).then_inc(bank_full(2), 1)
            claim(pe, 6, ("rs_kc", h))
            if h == 0:
                pe.wait_ge(S("diff_rs"), 2)
            for t in range(NTC):
                mm = spread(6, "nk", 2 * (h * NTA + t), t)
            mm.then_inc(bank_full(6), 1)
            claim(pe, 3, ("rs_k", h), (S("dk_ready"), h + 1))
            for t in range(NT):
                mm = spread(3, "nk", 2 * (h * NTA + NTC + t), t)
            mm.then_inc(bank_full(3), 1)

        def scores(u):
            h, qt = pairs[u]
            pe.wait_ge(S("dq_ready"), h + 1)
            pe.wait_ge(S("dk_ready"), h + 1)
            for comp in range(2):
                rows, b = slice(64 * comp, 64 * comp + 64), 2 * comp
                if u == 0:
                    pe.wait_ge(*bank_freed[b + 1])
                claim(pe, b, (f"s{comp}", u))
                for a, z in ((0, 512), (512, NALL)):
                    mm = pe.matmul(flat[:, b * 512 + a:b * 512 + z], dq[rows, h, qt * P:(qt + 1) * P], dk[rows, h, a:z], start=True, stop=True)
                mm.then_inc(bank_full(b), 1)

        def mix_values(u):
            h, qt = pairs[u]
            pe.wait_ge(S("prob_ready"), u + 1)
            claim(pe, 4 + u % 2, ("tA", u), (S("probT_a"), u + 1))
            for t in range(4):
                mm = pe.transpose(ps[:, 4 + u % 2, t * P:(t + 1) * P], prob[u % 2][:, 0, t * P:(t + 1) * P], ident)
            mm.then_inc(bank_full(4 + u % 2), 1)
            claim(pe, 6 + u % 2, ("tB", u), (S("od_ready"), u + 1))
            for t in range(4, NTA):
                mm = pe.transpose(ps[:, 6 + u % 2, (t - 4) * P:(t - 3) * P], prob[u % 2][:, 0, t * P:(t + 1) * P], ident)
            mm.then_inc(bank_full(6 + u % 2), 1)
            also(6 + u % 2, ("pv", u))
            pe.wait_ge(S("probT_a"), u + 1)
            pe.wait_ge(S("probT_b"), u + 1)
            for t in range(NTA):
                mm = pe.matmul(ps[:, 6 + u % 2, 256:256 + P], dvt[:, t, h * DV:(h + 1) * DV], probT[u % 2][:, t, :],
                               start=(t == 0), stop=(t == NTA - 1))
            mm.then_inc(bank_full(6 + u % 2), 1)

        scores(0)
        for u in range(len(pairs)):
            if u + 1 < len(pairs):
                scores(u + 1)
            mix_values(u)
        bank_freed[1], bank_freed[3] = bank_freed[0], bank_freed[2]
        head_norm_tensor(pe, "no", 0, (1, 2))

    def diff_scalar(act):
        act.wait_ge(S("lam"), 2)
        act.activation(lam[:, 2:4], lam[:, 0:2], ACT.Exp).then_inc(S("lam_exp"), 1)
        for i in range(2 * HEADS):
            h, src = i % HEADS, (dq, dk)[i // HEADS]
            if i >= 2:
                j = i - 2
                if j == HEADS - 1:
                    full(act, "nq_ss")
                else:
                    act.wait_ge(S("diff_sq_used"), j + 1 - (j >= HEADS))
            act.activation(sq[i % 2][:, 0:src.shape[2]], src[:, h, :], ACT.Square).then_inc(S("diff_sq"), 1)
        for key in ("nq", "nk"):
            b = full(act, key + "_ss")
            act.activation(std[key][:, :], ps[:, b, 0:std[key].shape[1]], ACT.Sqrt, bias=c("eps"), scale=1.0 / DIFF_DH)\
               .then_inc(bank_empty(b), 1)

        def exps(u):
            if u >= 2:
                full(act, ("tB", u - 2))
            for comp in range(2):
                b = held[(f"s{comp}", u)][0]
                act.wait_ge(S("neg_max"), 2 * u + comp + 1)
                o = 1024 * comp
                act.activation(prob[u % 2][:, comp, :], flat[:, o:o + NALL], ACT.Exp, bias=neg_max[u % 2][:, comp:comp + 1],
                               accum_out=total[u % 2][:, comp:comp + 1]).then_inc(bank_empty(b), 1)

        exps(0)
        for u in range(len(pairs)):
            if u + 1 < len(pairs):
                exps(u + 1)
            b = full(act, ("tA", u))
            if u >= 2:
                full(act, ("pv", u - 2))
            act.activation(probT[u % 2][:, 0:4, :], ps[:, b, :].rearrange("p (t q) -> p t q", t=4), ACT.Copy).then_inc(S("probT_a"), 1)
        head_norm_scalar(act, "no", od, 4, lambda e, h: e.wait_ge(S("od_ready"), NT * (h + 1)), "t1")

    def diff_vector(dve):
        mark("lam", dve.tensor_tensor(t1[0][:, 0:P], v("lam_q"), v("lam_k"), ALU.mult))
        settle(dve, "lam")
        mark("lam", dve.tensor_reduce(lam[:, 0:2], t1[0][:, 0:P].rearrange("p (z d) -> p z d", z=2), AX, ALU.add))
        dve.wait_ge(S("lam_exp"), 1)
        mark("lam", dve.scalar_tensor_tensor(out=lam[:, 4:5], in0=lam[:, 3:4], scalar=-LAM_INIT, in1=lam[:, 2:3],
                                             op0=ALU.add, op1=ALU.subtract))
        mark("lam", dve.tensor_scalar(gain_dq[:, :], v("dq_g"), DIFF_DH ** -0.5, None, ALU.mult))
        mark("lam", dve.tensor_scalar(gain_dn[:, :], v("dn_g"), 1.0 - LAM_INIT, None, ALU.mult))
        settle(dve, "lam")
        mark("rot_ready", dve.tensor_scalar(rot_q[:, :], ca("rot"), gain_dq[:, :], None, ALU.mult))
        mark("rot_ready", dve.tensor_scalar(rot_k[:, :], ca("rot"), v("dk_g"), None, ALU.mult))
        for key in ("nq", "nk"):
            read(dve, key + "_ss")
            mark("diff_rs", dve.reciprocal(rs[key][:, :], std[key][:, :]))

        last_rotated = []

        def rotate(dst, gains, key_rot, key_rs, done):
            b = full(dve, key_rot)
            if last_rotated:
                read(dve, last_rotated.pop())
            last_rotated.append(key_rs)
            mark("rope_step", dve.tensor_tensor(t1[0][:, 0:N], ps[:, b, :], ca("sin"), ALU.mult))
            mark("rope_step", dve.scalar_tensor_tensor(out=t1[1][:, 0:N], in0=dst, scalar=gains, in1=ca("cos"),
                                                       op0=ALU.mult, op1=ALU.mult))
            settle(dve, "rope_step")
            dve.tensor_tensor(t1[1][:, 0:N], t1[1][:, 0:N], t1[0][:, 0:N], ALU.add).then_inc(bank_empty(b), 1)
            dve.wait_ge(*held[key_rot][2])
            b = full(dve, key_rs)
            dve.tensor_tensor(dst, t1[1][:, 0:N], ps[:, b, :], ALU.mult).then_inc(S(done), 1)

        for h in range(HEADS):
            rotate(dq[:, h, :], gain_dq[:, :], ("rot_q", h), ("rs_q", h), "dq_ready")
            b = full(dve, ("rs_kc", h))
            dve.scalar_tensor_tensor(out=dk[:, h, 0:NCTX], in0=dk[:, h, 0:NCTX], scalar=v("dk_g"), in1=ps[:, b, 0:NCTX],
                                     op0=ALU.mult, op1=ALU.mult).then_inc(bank_empty(b), 1)
            rotate(dk[:, h, NCTX:], v("dk_g"), ("rot_k", h), ("rs_k", h), "dk_ready")

        def maxima(u):
            for comp in range(2):
                full(dve, (f"s{comp}", u))
                o = 1024 * comp
                dve.tensor_reduce(neg_max[u % 2][:, comp:comp + 1], flat[:, o:o + NALL], AX, ALU.max, negate=True)\
                   .then_inc(S("neg_max"), 1)

        def difference(u):
            read(dve, ("s0", u))
            read(dve, ("s1", u))
            i, p = inv[u % 2], prob[u % 2]
            mark("diff_step", dve.reciprocal(i[:, 0:2], total[u % 2][:, :]))
            settle(dve, "diff_step")
            mark("diff_step", dve.tensor_tensor(i[:, 2:3], i[:, 1:2], lam[:, 4:5], ALU.mult))
            settle(dve, "diff_step")
            mark("diff_step", dve.tensor_scalar(p[:, 1, :], p[:, 1, :], i[:, 2:3], None, ALU.mult))
            settle(dve, "diff_step")
            dve.scalar_tensor_tensor(out=p[:, 0, :], in0=p[:, 0, :], scalar=i[:, 0:1], in1=p[:, 1, :], op0=ALU.mult, op1=ALU.add)\
               .then_inc(S("prob_ready"), 1)

        def outputs(u):
            h, qt = pairs[u]
            b = full(dve, ("pv", u))
            dve.tensor_copy(od[:, h, qt * P:(qt + 1) * P], ps[:, b, 256:256 + P]).then_inc(S("od_ready"), 1)

        maxima(0)
        for u in range(len(pairs)):
            difference(u)
            if u >= 1:
                outputs(u - 1)
            if u + 1 < len(pairs):
                maxima(u + 1)
            b = full(dve, ("tB", u))
            dve.tensor_copy(probT[u % 2][:, 4:NTA, :], ps[:, b, 0:2 * P].rearrange("p (t q) -> p t q", t=2)).then_inc(S("probT_b"), 1)
        outputs(len(pairs) - 1)
        head_norm_vector(dve, "no", od, 4, gain_dn[:, :], None)

    directions = [(d, pc) for d in range(2) for pc in range(2)]
    u_tiles = ([0, 1, 2, 3, 4], [1, 0, 5, 4, 3])
    GATE_SCALE = 1.0 / 16.0

    def halves(t, s):
        return t.rearrange("p (n two s) -> p n two s", two=2, s=s)

    def gla_tensor(pe):
        for i, (z, pc) in enumerate(directions):
            up = v("gate_up", z * 256 + pc * P, z * 256 + pc * P + P)[0:32, :]
            claim(pe, 2 * (i % 2), ("gx", i))
            pe.matmul(ps[:, 2 * (i % 2), :], up, dn[:, NCTX:], start=True, stop=True).then_inc(bank_full(2 * (i % 2)), 1)
            claim(pe, 2 * (i % 2) + 1, ("gc", i))
            pe.matmul(ps[:, 2 * (i % 2) + 1, 0:NCTX], up, dn[:, 0:NCTX], start=True, stop=True).then_inc(bank_full(2 * (i % 2) + 1), 1)
        for i, (d, pc) in enumerate(directions):
            pe.wait_ge(S("kd_ready"), 2 * (i + 1))
            claim(pe, 4, ("kA", i))
            for t in range(4):
                mm = pe.transpose(ps[:, 4, t * P:(t + 1) * P], t1[i % 2][:, t * P:(t + 1) * P], ident)
            mm.then_inc(bank_full(4), 1)
            claim(pe, 5, ("kB", i))
            for t in range(4, NTA):
                mm = pe.transpose(ps[:, 5, (t - 4) * P:(t - 3) * P], t1[i % 2][:, t * P:(t + 1) * P], ident)
            mm.then_inc(bank_full(5), 1)
            read(pe, ("kA", i))
            read(pe, ("kB", i))
            for j in range(0, 5, 2):
                b = (6, 7, 0)[j // 2]
                claim(pe, b, ("u", i, j))
                for o, t in enumerate(u_tiles[d][j:j + 2]):
                    mm = pe.matmul(ps[:, b, o * 256:(o + 1) * 256], kdT[:, d, t, pc * P:(pc + 1) * P],
                                   vt[:, t, pc * 256:(pc + 1) * 256], start=True, stop=True)
                mm.then_inc(bank_full(b), 1)
        for li in range(len(LEVELS) + 1):
            if li:
                pe.wait_ge(S("lq_ready"), li)
                pe.wait_ge(S("lk_ready"), li)
            q, k = (lq[:, :], lk[:, :]) if li else (gqx[:, :, :].rearrange("p c n -> p (c n)"), gkx[:, :, :].rearrange("p c n -> p (c n)"))
            for b in range(4):
                claim(pe, b, ("level", li, b))
                rows = slice(64 * (b % 2), 64 * (b % 2) + 64)
                for j in range(4):
                    at = (j % 2) * N + (2 * (b // 2) + j // 2) * P
                    mm = pe.matmul(ps[:, b, j * P:(j + 1) * P], k[rows, at:at + P], q[rows, at:at + P], start=True, stop=True)
                mm.then_inc(bank_full(b), 1)
        pe.wait_ge(S("qe_ready"), 2)
        read(pe, ("u", len(directions) - 1, 4))
        for b in range(4):
            read(pe, ("level", len(LEVELS), b))
        for h in range(HEADS):
            claim(pe, 4 + h, ("og", h))
            rows, pc = slice(64 * (h % 2), 64 * (h % 2) + 64), h // 2
            for t in range(NT):
                out = ps[:, 4 + h, t * P:(t + 1) * P]
                pe.matmul(out, vt[:, NTC + t, h * DV:(h + 1) * DV], attnT[:, t, h, :], start=True, stop=False)
                for d, at in ((0, t), (1, NT - 1 - t)):
                    mm = pe.matmul(out, states[rows, d, pc, at, :], qe[rows, d, pc * N + t * P:pc * N + (t + 1) * P],
                                   start=False, stop=(d == 1))
            mm.then_inc(bank_full(4 + h), 1)
        head_norm_tensor(pe, "ng", 0, (1, 2), HEADS)

    def gla_scalar(act):
        for i in range(len(directions)):
            if i:
                act.wait_ge(S("cum_ready"), i)
            b = full(act, ("gx", i))
            act.activation(yb[0][:, NCTX:], ps[:, b, :], ACT.Identity, bias=v("gate_b", i, i + 1)).then_inc(bank_empty(b), 1)
            b = full(act, ("gc", i))
            act.activation(yb[0][:, 0:NCTX], ps[:, b, 0:NCTX], ACT.Identity, bias=v("gate_b", i, i + 1)).then_inc(bank_empty(b), 1)
            read(act, ("gx", i))
            read(act, ("gc", i))
            mark("gate_step", act.activation(yb[1][:, :], yb[0][:, :], ACT.Abs))
            settle(act, "gate_step")
            mark("gate_step", act.activation(yb[1][:, :], yb[1][:, :], ACT.Exp, scale=-1.0))
            settle(act, "gate_step")
            act.activation(yb[1][:, :], yb[1][:, :], ACT.Ln, bias=1.0).then_inc(S("softplus_ready"), 1)
        for i, (d, pc) in enumerate(directions):
            act.wait_ge(S("to_edge"), 2 * (i + 1))
            act.activation(t1[i % 2][:, :], t1[i % 2][:, :], ACT.Exp, scale=GATE_SCALE).then_inc(S("edge_decay"), 1)
            edge = slice(P - 1, None, P) if d == 0 else slice(0, None, P)
            act.activation(decay[:, d, pc, 0:NTC], cumc[:, d, pc * NCTX:(pc + 1) * NCTX][:, edge], ACT.Exp, scale=GATE_SCALE)\
               .then_inc(S("decay_ready"), 1)
            act.activation(decay[:, d, pc, NTC:], cumx[:, d, pc * N:(pc + 1) * N][:, edge], ACT.Exp, scale=GATE_SCALE)\
               .then_inc(S("decay_ready"), 1)
            b = full(act, ("kA", i))
            act.activation(kdT[:, d, 0:4, pc * P:(pc + 1) * P], ps[:, b, :].rearrange("p (t k) -> p t k", t=4), ACT.Copy)\
               .then_inc(bank_empty(b), 1)
        for d in range(2):
            act.activation(qe[:, d, :], cumx[:, d, :], ACT.Exp, scale=GATE_SCALE).then_inc(S("q_decay"), 1)
        for li in range(1, len(LEVELS) + 1):
            act.wait_ge(S("level_sums"), 4 * li)
            act.activation(lq[:, :], lq[:, :], ACT.Exp, scale=GATE_SCALE).then_inc(S("lq_decay"), 1)
            act.activation(lk[:, :], lk[:, :], ACT.Exp, scale=GATE_SCALE).then_inc(S("lk_decay"), 1)
        for h in range(HEADS):
            b = full(act, ("og", h))
            act.activation(og[:, h, :], ps[:, b, :], ACT.Copy).then_inc(bank_empty(b), 1)
        head_norm_scalar(act, "ng", og, 0, lambda e, h: read(e, ("og", h)), "gated")

    def gla_vector(dve):
        carry = ca("carry")
        for i, (d, pc) in enumerate(directions):
            dve.wait_ge(S("softplus_ready"), i + 1)
            mark("gate", dve.scalar_tensor_tensor(out=yb[0][:, :], in0=yb[0][:, :], scalar=0.0, in1=yb[1][:, :],
                                                  op0=ALU.min, op1=ALU.subtract))
            settle(dve, "gate")
            gx, gc = yb[0][:, NCTX:], yb[0][:, 0:NCTX]
            ox, oc = cumx[:, d, pc * N:(pc + 1) * N], cumc[:, d, pc * NCTX:(pc + 1) * NCTX]
            if d:
                gx, gc, ox, oc = gx[:, ::-1], gc[:, ::-1], ox[:, ::-1], oc[:, ::-1]
            mark("gate", dve.tensor_tensor_scan(oc, carry[:, 0:NCTX], gc, 0.0, ALU.mult, ALU.add))
            mark("cum_ready", dve.tensor_tensor_scan(ox, carry, gx, 0.0, ALU.mult, ALU.add))
        settle(dve, "gate")
        settle(dve, "cum_ready")

        def keys_to_edge(i):
            d, pc = directions[i]
            if i >= 2:
                full(dve, ("kB", i - 2))
            for src, o, tiles in ((cumc, 0, NTC), (cumx, NCTX, NT)):
                w = tiles * P
                cum = src[:, d, pc * w:(pc + 1) * w].rearrange("p (t n) -> p t n", n=P)
                edge = cum[:, :, P - 1:P] if d == 0 else cum[:, :, 0:1]
                dve.tensor_tensor(t1[i % 2][:, o:o + w].rearrange("p (t n) -> p t n", n=P), edge.broadcast_to([P, tiles, P]), cum,
                                  ALU.subtract).then_inc(S("to_edge"), 1)
            dve.wait_ge(S("edge_decay"), i + 1)
            dve.tensor_tensor(t1[i % 2][:, 0:NCTX], t1[i % 2][:, 0:NCTX], gkc[:, pc, :], ALU.mult).then_inc(S("kd_ready"), 1)
            dve.tensor_tensor(t1[i % 2][:, NCTX:], t1[i % 2][:, NCTX:], gkx[:, pc, :], ALU.mult).then_inc(S("kd_ready"), 1)
            b = full(dve, ("kB", i))
            dve.tensor_copy(kdT[:, d, 4:NTA, pc * P:(pc + 1) * P], ps[:, b, 0:2 * P].rearrange("p (t k) -> p t k", t=2))\
               .then_inc(bank_empty(b), 1)

        def states_of(i):
            d, pc = directions[i]
            dve.wait_ge(S("decay_ready"), 2 * (i + 1))
            for j in range(5):
                b = full(dve, ("u", i, j - j % 2))
                for half in range(2):
                    rows = slice(64 * half, 64 * half + 64)
                    o = (j % 2) * 256 + half * DV
                    to = states[rows, d, pc, NT if j == 0 else j - 1, :]
                    if j == 0:
                        ins = dve.tensor_copy(to, ps[rows, b, o:o + DV])
                    else:
                        ins = dve.scalar_tensor_tensor(out=to, in0=states[rows, d, pc, NT if j == 1 else j - 2, :],
                                                       scalar=decay[rows, d, pc, u_tiles[d][j]:u_tiles[d][j] + 1],
                                                       in1=ps[rows, b, o:o + DV], op0=ALU.mult, op1=ALU.add)
                    if half and (j % 2 or j == 4):
                        ins.then_inc(bank_empty(b), 1)
                        dve.wait_ge(*held[("u", i, j - j % 2)][2])
                    else:
                        mark("state_step", ins)
                settle(dve, "state_step")

        for i in range(len(directions)):
            keys_to_edge(i)
            if i:
                states_of(i - 1)
        states_of(len(directions) - 1)
        q = gqx[:, :, :].rearrange("p c n -> p (c n)")
        for d in range(2):
            dve.wait_ge(S("q_decay"), d + 1)
            dve.tensor_tensor(qe[:, d, :], qe[:, d, :], q, ALU.mult).then_inc(S("qe_ready"), 1)

        def attention(li):
            mask = ca("levels", li * P, (li + 1) * P).unsqueeze(1).unsqueeze(1).broadcast_to([P, 2, 2, P])
            for b in range(4):
                full(dve, ("level", li, b))
                got = ps[:, b, :].rearrange("p (t h i) -> p t h i", t=2, h=2)
                to = attnT[:, 2 * (b // 2):2 * (b // 2) + 2, b % 2::2, :]
                if li == 0:
                    ins = dve.tensor_tensor(to, got, mask, ALU.mult)
                else:
                    ins = dve.copy_predicated(to, mask.bitcast(U32), got)
                ins.then_inc(bank_empty(b), 1)

        for li, s in enumerate(LEVELS, 1):
            if li >= 2:
                full(dve, ("level", li - 1, 3))
            fw, bw = halves(cumx[:, 0, :], s), halves(cumx[:, 1, :], s)
            to_q, to_k = halves(lq[:, :], s), halves(lk[:, :], s)
            shape = [P, 2 * N // (2 * s), s]
            mid_f = fw[:, :, 0, s - 1:s].broadcast_to(shape)
            mid_b = bw[:, :, 1, 0:1].broadcast_to(shape)
            mark("level_sums", dve.tensor_tensor(to_q[:, :, 0, :], bw[:, :, 0, :], mid_b, ALU.subtract))
            mark("level_sums", dve.tensor_tensor(to_q[:, :, 1, :], fw[:, :, 1, :], mid_f, ALU.subtract))
            mark("level_sums", dve.tensor_tensor(to_k[:, :, 0, :], mid_f, fw[:, :, 0, :], ALU.subtract))
            mark("level_sums", dve.tensor_tensor(to_k[:, :, 1, :], mid_b, bw[:, :, 1, :], ALU.subtract))
            attention(li - 1)
            dve.wait_ge(S("lq_decay"), li)
            dve.tensor_tensor(lq[:, :], lq[:, :], q, ALU.mult).then_inc(S("lq_ready"), 1)
        attention(len(LEVELS))
        head_norm_vector(dve, "ng", og, 0, v("gla_g"), rT)

    def gla_gpsimd(pool):
        k = gkx[:, :, :].rearrange("p c n -> p (c n)")
        for li in range(1, len(LEVELS) + 1):
            pool.wait_ge(S("lk_decay"), li)
            pool.tensor_tensor(lk[:, :], lk[:, :], k, ALU.mult).then_inc(S("lk_ready"), 1)

    RESIDUALS = ("mix1", "ffn1", "ffn2", "mix2", "ffn3")

    def residual(key, chunks):
        return S("residual_ready"), RESIDUALS.index(key) * KD + chunks

    def mixed_tensor(pe, key, name, rh, rl, parts, n_ada):
        for m in range(KD):
            g = take_slot(pe, full_columns(name, m * P))
            b = m % 4
            claim(pe, b, (key, m), residual(key, m + 1))
            for k in range(KD):
                if m == 0:
                    pe.wait_ge(*parts[k])
                mm = three_passes(pe, ps[:, b, :], g, k, P, rh[:, k, :], rl[:, k, :], k == 0, k == KD - 1)
            mm.then_inc(bank_full(b), 1)
            after[g] = (bank_full(b), bank_uses[b])
            ada_slots(pe, n_ada(m))
        if ada_batches[-1]:
            ada_batch_end()

    def mixed_vector(dve, key, gate):
        for m in range(KD):
            b = full(dve, (key, m))
            dve.scalar_tensor_tensor(out=xT[:, m, :], in0=ps[:, b, :], scalar=gate(m), in1=xT[:, m, :], op0=ALU.mult, op1=ALU.add)\
               .then_inc(S("residual_ready"), 1)

    def mixed_scalar(act, key, g0):
        for m in range(KD):
            full(act, (key, m))
            split_slots(act, g0 + m + 2)

    ffns = {}
    HALF = KF // 2

    def ffn_tensor(pe, key, key_norm, name_in, name_out, n_ada):
        per = 2 + n_ada
        f = ffns[key] = dict(i=len(ffns), n0=len(stream), g0=len(slot_of), per=per, batch=len(ada_batches) - 1)
        for b in range(4):
            pe.wait_ge(*bank_freed[b])
        f["full0"], f["empty0"] = bank_uses[:4], bank_empties[:4]
        for k in range(KD):
            pe.wait_ge(*norm(key_norm, "ready", k + 1))
        if n_ada:
            pe.wait_ge(*bank_freed[7])
            f["ada0"] = ada_todo[0][1]
        n0, g0 = f["n0"], f["g0"]
        with pe.Fori(0, HALF) as it:
            for j in range(2):
                for u in range(2):
                    n, g, b = n0 + per * j + u, g0 + 2 * j + u, 2 * j + u
                    pe.wait_ge(spent(n)[0], spent(n)[1] + it * (2 * per // RING))
                    pe.wait_ge(bank_empty(b), it + f["empty0"][b])
                    for k in range(KD):
                        mm = three_passes(pe, ps[:, b, :], g, k, P, hh[:, k, :], hl[:, k, :], k == 0, k == KD - 1)
                    mm.then_inc(bank_full(b), 1)
                for a in range(n_ada):
                    n = n0 + per * j + 2 + a
                    pe.wait_ge(landed(n)[0], landed(n)[1] + it * (16 * 2 * per // RING))
                    for k in range(KD):
                        mm = pe.matmul(ps[:, 7, bass.ds(it * (2 * n_ada) + (96 + f["ada0"] + j * n_ada + a), 1)],
                                       raw[n % RING][:, k * P:(k + 1) * P], cond2[:, k, :], start=(k == 0), stop=(k == KD - 1))
                    mm.then_inc(spent(n)[0], 1)
        for i in range(KF):
            stream.append(full_columns(name_in, i * P))
            stream.append(full_columns(name_in, FFN + i * P))
            slot_of.extend((n0 + per * i, n0 + per * i + 1))
            after.extend((None, None))
            for a in range(n_ada):
                name, c_ = ada_todo.pop(0)
                ada_batches[-1].append((name, c_, len(stream)))
                stream.append(full_columns(name, c_ * P))
        for b in range(4):
            bank_uses[b] += HALF
            bank_empties[b] += HALF
            bank_freed[b] = (bank_empty(b), bank_empties[b])
        if n_ada:
            ada_batch_end()
        f["after_in"] = [(bank_full(b), bank_uses[b]) for b in (2, 3)]
        after[-2], after[-1] = f["after_in"]

        f["n1"], f["g1"], f["slab0"] = len(stream), len(slot_of), marks.get("slab_done", 0)
        n1, g1 = f["n1"], f["g1"]
        act0 = KF * f["i"]

        def slab(k, it, act_at, first, last):
            n, g = n1 + k, g1 + k
            pe.wait_ge(spent(n)[0], spent(n)[1] + it)
            pe.wait_ge(S("act_ready"), it * RING + (act0 + k + 1))
            for m in range(KD):
                if first:
                    claim(pe, m, (key, m), residual(key, m + 1))
                mm = three_passes(pe, ps[:, m, :], g, m, P, act_hi[:, act_at], act_lo[:, act_at], first, last)
                if last:
                    mm.then_inc(bank_full(m), 1)
            if not last:
                mm.then_inc(S("slab_done"), 1)

        slab(0, 0, slice(0, N), True, False)
        with pe.Fori(0, (KF - 2) // RING) as it:
            for j in range(RING):
                slab(1 + j, it, bass.ds(it * (RING * N) + (1 + j) * N, N), False, False)
        slab(KF - 1, 0, slice((KF - 1) * N, KF * N), False, True)
        for k in range(KF):
            stream.append(weight_rows(name_out, k))
            slot_of.append(n1 + k)
            after.append((S("slab_done"), f["slab0"] + k + 1))
        after[-1] = (bank_full(KD - 1), bank_uses[KD - 1])
        marks["slab_done"] = f["slab0"] + KF - 1

    def ffn_scalar(act, key):
        f = ffns[key]
        n0, g0, per = f["n0"], f["g0"], f["per"]
        split_slots(act, g0 + 1)
        with act.Fori(0, HALF) as it:
            for j in range(2):
                for u in range(2):
                    n, g, b = n0 + per * (j + 1) + u, g0 + u, 2 * j + u
                    act.wait_ge(bank_full(b), it + (f["full0"][b] + 1))
                    act.wait_ge(landed(n)[0], landed(n)[1] + it * (16 * 2 * per // RING))
                    act.activation(w_hi[g % SPLIT][:, :], raw[n % RING][:, :], ACT.Copy).then_inc(S("w_hi_ready"), 1)
                    if u == 0:
                        act.activation(silu[j][:, :], ps[:, b, :], ACT.Silu).then_inc(bank_empty(b), 1)
                b = 2 * j + 1
                act.wait_ge(bank_empty(b), it + (f["empty0"][b] + 1))
                act.activation(act_hi[:, bass.ds(it * (2 * N) + j * N, N)], prod[j][:, :], ACT.Copy).then_inc(S("act_hi_ready"), 1)
        n1, g1 = f["n1"], f["g1"]
        with act.Fori(0, (KF - 2) // RING) as it:
            for j in range(RING):
                n, g = n1 + 2 + j, g1 + j
                act.wait_ge(S("slab_done"), it * RING + (f["slab0"] + j + 1))
                act.wait_ge(landed(n)[0], landed(n)[1] + it * 16)
                act.activation(w_hi[g % SPLIT][:, :], raw[n % RING][:, :], ACT.Copy).then_inc(S("w_hi_ready"), 1)
        next_split[0] = g1 + KF
        split_slots(act, g1 + KF)

    def split_low(pool, n, g, it=0):
        pool.wait_ge(S("w_hi_ready"), it * 4 + (g + 1))
        pool.tensor_tensor(w_lo[g % SPLIT][:, :], raw[n % RING][:, :], w_hi[g % SPLIT][:, :].bitcast(F32), ALU.subtract)\
            .then_inc(spent(n)[0], 1)

    def split_lows(pool, g0, g1):
        for g in range(g0, g1):
            split_low(pool, slot_of[g], g)

    def ffn_gpsimd(pool, key):
        f = ffns[key]
        with pool.Fori(0, HALF) as it:
            for j in range(2):
                for u in range(2):
                    split_low(pool, f["n0"] + f["per"] * j + u, f["g0"] + 2 * j + u, it)
        with pool.Fori(0, (KF - 2) // RING) as it:
            for j in range(RING):
                split_low(pool, f["n1"] + j, f["g1"] + j, it)
        split_lows(pool, f["g1"] + KF - 2, f["g1"] + KF)

    def ffn_vector(dve, key, gate):
        f = ffns[key]
        with dve.Fori(0, HALF) as it:
            for j in range(2):
                b = 2 * j
                dve.wait_ge(bank_empty(b), it + (f["empty0"][b] + 1))
                dve.wait_ge(bank_full(b + 1), it + (f["full0"][b + 1] + 1))
                dve.tensor_tensor(prod[j][:, :], silu[j][:, :], ps[:, b + 1, :], ALU.mult).then_inc(bank_empty(b + 1), 1)
                dve.wait_ge(S("act_hi_ready"), it * 2 + (KF * f["i"] + j + 1))
                at = bass.ds(it * (2 * N) + j * N, N)
                dve.tensor_tensor(act_lo[:, at], prod[j][:, :], act_hi[:, at].bitcast(F32), ALU.subtract).then_inc(S("act_ready"), 1)
        if f["per"] > 2:
            ada_copy(dve, f["batch"])
        mixed_vector(dve, key, gate)

    IN2 = dict(qa=0, ka=512, va=576, qi=640, ki=1152, wi=1216, cq=1224, ckv=1608, kr=1864, ga=1896, gb=2920)
    IDX_SCALE, HEAD_SCALE, A_SCALE, B_SCALE = DH2 ** -0.5, H2 ** -0.5, DH2 ** -0.5, QK2 ** -0.5

    def in2(*cuts):
        return ("w_in_2", [(k * P, P, cuts) for k in range(KD)])

    chunks_2 = ([("ki", 0, in2((IN2["ki"], IN2["ki"] + 64, 0), (IN2["ki"], IN2["ki"] + 64, 64))),
                 ("wkr", 0, in2((IN2["wi"], IN2["wi"] + H2, 0), (IN2["kr"], IN2["kr"] + ROPE2, 64)))]
                + [("qi", i, in2((IN2["qi"] + i * P, IN2["qi"] + (i + 1) * P, 0))) for i in range(4)]
                + [("cq", i, in2((IN2["cq"] + i * P, IN2["cq"] + (i + 1) * P, 0))) for i in range(3)]
                + [("ckv", i, in2((IN2["ckv"] + i * P, IN2["ckv"] + (i + 1) * P, 0))) for i in range(2)]
                + [("kva", 0, in2((IN2["ka"], IN2["ka"] + P, 0)))]
                + [("qa", i, in2((IN2["qa"] + i * P, IN2["qa"] + (i + 1) * P, 0))) for i in range(4)])
    second = {}

    def proj2_tensor(pe):
        second["g_proj"] = len(slot_of)
        for i, (name, h, spec) in enumerate(chunks_2):
            g = take_slot(pe, spec)
            b = i % 2
            claim(pe, b, (name, h))
            for k in range(KD):
                if i == 0:
                    pe.wait_ge(*norm("nm", "ready", k + 1))
                mm = three_passes(pe, ps[:, b, :], g, k, P, hh[:, k, :], hl[:, k, :], k == 0, k == KD - 1)
            mm.then_inc(bank_full(b), 1)
            after[g] = (bank_full(b), bank_uses[b])
        claim(pe, 2, "wt")
        read(pe, ("wkr", 0))
        for t in range(NT):
            mm = pe.transpose(ps[:, 2, t * H2:(t + 1) * H2], wkr[0:H2, t * P:(t + 1) * P], ident[0:H2, 0:H2])
        mm.then_inc(bank_full(2), 1)
        claim(pe, 3, "vat")
        read(pe, ("kva", 0))
        for t in range(NT):
            mm = pe.transpose(ps[:, 3, t * P:(t + 1) * P], kva[:, t * P:(t + 1) * P], ident)
        mm.then_inc(bank_full(3), 1)

    def proj2_scalar(act):
        for i, (name, h, _) in enumerate(chunks_2):
            b = full(act, (name, h))
            split_slots(act, second["g_proj"] + i + 2)
            if name == "qa":
                act.activation(qa[:, :, 2 * h, :], ps[0:64, b, :].rearrange("p (u q) -> p u q", q=QG), ACT.Copy, scale=A_SCALE)
                act.activation(qa[:, :, 2 * h + 1, :], ps[64:128, b, :].rearrange("p (u q) -> p u q", q=QG), ACT.Copy, scale=A_SCALE)\
                   .then_inc(bank_empty(b), 1)
                continue
            to = {"ki": ki[:, :], "wkr": wkr[:, :], "qi": qi[:, h, :], "cq": cq[:, h % 3, :], "ckv": ckv[:, h % 2, :], "kva": kva[:, :]}[name]
            act.activation(to, ps[:, b, :], ACT.Copy).then_inc(bank_empty(b), 1)

    PI_A = 6.28125
    PI_B = math.floor((2 * math.pi - PI_A) * 2.0 ** 21) / 2.0 ** 21
    TWO_PI = (PI_A, PI_B, 2 * math.pi - PI_A - PI_B)
    ROUND = 1.5 * 2.0 ** 23
    rot_rows = slice(64, 96)

    def rope2_vector(dve):
        mark("rope2", dve.tensor_copy(posf[:, :], posi[:, :]))
        mark("rope2", dve.tensor_copy(qfrom[:, :], qposi[:, :]))
        settle(dve, "rope2")
        mark("rope2", dve.tensor_scalar(qfrom[:, :], qfrom[:, :], c("bucket_from"), None, ALU.add))
        ang, turns = sinr[rot_rows, :], t1[1][rot_rows, 0:N]
        for shift, to in ((0.25, cosr[rot_rows, :]), (0.0, sinr[rot_rows, :])):
            if shift:
                mark("rope2", dve.tensor_scalar(ang, posf[rot_rows, :], c("freq")[rot_rows, :], None, ALU.mult))
                settle(dve, "rope2")
            mark("rope2", dve.tensor_scalar(turns, ang, 1 / (2 * math.pi), shift, ALU.mult, ALU.add))
            settle(dve, "rope2")
            mark("rope2", dve.tensor_scalar(turns, turns, ROUND, None, ALU.add))
            settle(dve, "rope2")
            mark("rope2", dve.tensor_scalar(turns, turns, ROUND, None, ALU.subtract))
            settle(dve, "rope2")
            for i, part in enumerate(TWO_PI):
                mark("rope2", dve.scalar_tensor_tensor(out=to, in0=turns, scalar=-part, in1=ang if i == 0 else to,
                                                       op0=ALU.mult, op1=ALU.add))
                settle(dve, "rope2")
            if shift:
                mark("rope2", dve.tensor_scalar(to, to, math.pi / 2, None, ALU.add))
                settle(dve, "rope2")
            mark("rope2_angle", dve.tensor_scalar(to, to, 3.1415925, -3.1415925, ALU.min, ALU.max))

    def rope2_scalar(act):
        for i, to in enumerate((cosr, sinr)):
            act.wait_ge(S("rope2_angle"), i + 1)
            act.activation(to[rot_rows, :], to[rot_rows, :], ACT.Sin).then_inc(S("rope2_table"), 1)

    index_units = [(qt, h) for qt in range(1, NT) for h in range(H2)]

    def index_tensor(pe):
        for i, (qt, h) in enumerate(index_units):
            b, rows, keys = 6 + i % 2, slice(64 * (h % 2), 64 * (h % 2) + 64), (qt + 1) * P
            claim(pe, b, ("dots", i))
            if i == 0:
                read(pe, ("qi", 3))
            pe.matmul(ps[:, b, 0:keys], qi[rows, h // 2, qt * P:(qt + 1) * P], ki[rows, 0:keys], start=True, stop=True)\
              .then_inc(bank_full(b), 1)

    def index_scalar(act):
        for i, (qt, h) in enumerate(index_units):
            keys = (qt + 1) * P
            if i >= 2:
                act.wait_ge(S("index_sum"), i - 1)
            b = full(act, ("dots", i))
            act.activation(sq[i % 2][:, 0:keys], ps[:, b, 0:keys], ACT.Relu, scale=IDX_SCALE).then_inc(bank_empty(b), 1)

    def index_vector(dve):
        b = full(dve, "wt")
        dve.tensor_scalar(wt[:, :, :], ps[:, b, 0:NT * H2].rearrange("p (t h) -> p t h", t=NT), HEAD_SCALE, None, ALU.mult)\
           .then_inc(bank_empty(b), 1)
        read(dve, "wt")
        for i, (qt, h) in enumerate(index_units):
            keys, to = (qt + 1) * P, score[qt - 1]
            read(dve, ("dots", i))
            if h == 0:
                ins = dve.tensor_scalar(to[:, :], sq[i % 2][:, 0:keys], wt[:, qt, h:h + 1], None, ALU.mult)
            else:
                dve.wait_ge(S("index_sum"), i)
                ins = dve.scalar_tensor_tensor(out=to[:, :], in0=sq[i % 2][:, 0:keys], scalar=wt[:, qt, h:h + 1], in1=to[:, :],
                                               op0=ALU.mult, op1=ALU.add)
            ins.then_inc(S("index_sum"), 1)
        dve.wait_ge(S("index_sum"), len(index_units))
        for qt in range(1, NT):
            mark("topk", dve.memset(score[qt - 1][0:64, qt * P + 64:(qt + 1) * P], NEG))
        settle(dve, "topk")

    def topk_round(dve, r):
        for qt in range(1, NT):
            mark("topk", dve.max(best[:, qt - 1, :], score[qt - 1][:, :]))
        settle(dve, "topk")
        for qt in range(1, NT):
            mark("topk", dve.match_replace(score[qt - 1][:, :], best[:, qt - 1, :], score[qt - 1][:, :], TAKEN))
        settle(dve, "topk")

    def topk_end(dve):
        mark("hide_ready", dve.memset(hide[0][:, :], 0.0))
        settle(dve, "hide_ready")
        mark("hide_ready", dve.memset(hide[0][0:64, 64:P], HIDE))
        for qt in range(1, NT):
            mark("hide_ready", dve.tensor_scalar(hide[qt][:, :], score[qt - 1][:, :], TAKEN, HIDE, ALU.is_gt, ALU.mult))

    def uq_tiles():
        tiles = [(k * P, P, ((h * QK2, (h + 1) * QK2, 0),)) for h in range(H2) for k in range(3)]
        return [("w_uq_2", tiles[i:i + 8]) for i in range(0, 24, 8)]

    def pair_tiles(name):
        return (name, [(k * P, P, ((i * P, (i + 1) * P, 0),)) for i in range(4) for k in range(2)])

    def lora_tensor(pe):
        norm_tensor(pe, "ncq", 3, N, 4, 4)
        norm_tensor(pe, "nckv", 2, N, 5, 5)
        second["g_uq"] = len(slot_of)
        turn = c("rot2")[rot_rows, :]

        def rotate_q(h):
            read(pe, ("uq", h))
            claim(pe, 2 + h % 2, ("rot2", h))
            pe.matmul(ps[rot_rows, 2 + h % 2, :], turn, qb[rot_rows, h, :], start=True, stop=True).then_inc(bank_full(2 + h % 2), 1)

        specs = uq_tiles()
        for h in range(H2):
            claim(pe, h % 2, ("uq", h))
            for k in range(3):
                if h == 0:
                    pe.wait_ge(*norm("ncq", "ready", k + 1))
                i = 3 * h + k
                if i % 8 == 0:
                    g = take_slot(pe, specs[i // 8])
                mm = three_passes(pe, ps[0:QK2, h % 2, :], g, i % 8, QK2, cqh[:, k, :], cql[:, k, :], k == 0, k == 2)
                if i % 8 == 7 and k < 2:
                    mark("slab_done", mm)
                    after[g] = (S("slab_done"), marks["slab_done"])
            mm.then_inc(bank_full(h % 2), 1)
            if 3 * h + 2 == 23:
                after[g] = (bank_full(h % 2), bank_uses[h % 2])
            if h:
                rotate_q(h - 1)
        rotate_q(H2 - 1)
        for name, key in (("w_uk_2", "uk"), ("w_uv_2", "uv")):
            g = take_slot(pe, pair_tiles(name))
            for i in range(4):
                claim(pe, i % 2, (key, i))
                for k in range(2):
                    if key == "uk" and i == 0:
                        pe.wait_ge(*norm("nckv", "ready", k + 1))
                    mm = three_passes(pe, ps[:, i % 2, :], g, 2 * i + k, P, ckvh[:, k, :], ckvl[:, k, :], k == 0, k == 1)
                mm.then_inc(bank_full(i % 2), 1)
                after[g] = (bank_full(i % 2), bank_uses[i % 2])
                if key == "uk" and i == 0:
                    claim(pe, 2, "rot2_k")
                    pe.matmul(ps[rot_rows, 2, :], turn, wkr[rot_rows, :], start=True, stop=True).then_inc(bank_full(2), 1)
                if key == "uv" and i:
                    to_tokens2(pe, i - 1)
        to_tokens2(pe, 3)

    def to_tokens2(pe, i):
        read(pe, ("uv", i))
        claim(pe, 4 + i % 2, ("vb", i))
        for t in range(NT):
            mm = pe.transpose(ps[:, 4 + i % 2, t * P:(t + 1) * P], sq[i % 2][:, t * P:(t + 1) * P], ident)
        mm.then_inc(bank_full(4 + i % 2), 1)

    def lora_scalar(act):
        act.wait_ge(S("index_sum"), len(index_units))
        norm_scalar(act, "ncq", cq, 3, N, Q_LORA, cqh, None, lambda e, k: read(e, ("cq", k)))
        norm_scalar(act, "nckv", ckv, 2, N, KV_LORA, ckvh, None, lambda e, k: read(e, ("ckv", k)))
        g0 = second["g_uq"]
        for h in range(H2):
            b = full(act, ("uq", h))
            act.activation(qb[:, h, :], ps[0:QK2, b, :], ACT.Copy, scale=B_SCALE).then_inc(bank_empty(b), 1)
            if 3 * h + 2 >= 7:
                split_slots(act, g0 + 2 + (3 * h + 2 - 7) // 8)
        for i in range(4):
            b = full(act, ("uk", i))
            act.activation(kb[0:64, 2 * i, :], ps[0:64, b, :], ACT.Copy)
            act.activation(kb[0:64, 2 * i + 1, :], ps[64:128, b, :], ACT.Copy).then_inc(bank_empty(b), 1)
        for i in range(4):
            if i >= 2:
                full(act, ("vb", i - 2))
            b = full(act, ("uv", i))
            act.activation(sq[i % 2][:, 0:N], ps[:, b, :], ACT.Copy).then_inc(bank_empty(b), 1)
        split_slots(act, second["g_gated"] + 1)

    def lora_vector(dve):
        b = full(dve, "vat")
        dve.tensor_copy(vat[:, :, :], ps[:, b, :].rearrange("p (t d) -> p t d", t=NT)).then_inc(bank_empty(b), 1)
        norm_vector(dve, "ncq", cq, 3, N, lambda k: v("g_cq", k, k + 1), cqh, cql, None)
        norm_vector(dve, "nckv", ckv, 2, N, lambda k: v("g_ckv", k, k + 1), ckvh, ckvl, None)
        dve.wait_ge(S("rope2_table"), 2)
        dve.wait_ge(*norm("nckv", "ready", 2))

        last_rotated = []

        def rotate(src, dst, key):
            b = full(dve, key)
            if last_rotated:
                read(dve, last_rotated.pop())
            last_rotated.append(key)
            mark("rope2_step", dve.tensor_tensor(t1[0][rot_rows, 0:N], ps[rot_rows, b, :], sinr[rot_rows, :], ALU.mult))
            mark("rope2_step", dve.tensor_tensor(t1[1][rot_rows, 0:N], src, cosr[rot_rows, :], ALU.mult))
            settle(dve, "rope2_step")
            dve.tensor_tensor(dst, t1[0][rot_rows, 0:N], t1[1][rot_rows, 0:N], ALU.add).then_inc(bank_empty(b), 1)

        for h in range(H2):
            rotate(qb[rot_rows, h, :], qb[rot_rows, h, :], ("rot2", h))
        rotate(wkr[rot_rows, :], kb[rot_rows, 0, :], "rot2_k")
        read(dve, "rot2_k")
        for h in range(1, H2):
            mark("kb_ready", dve.tensor_copy(kb[rot_rows, h, :], kb[rot_rows, 0, :]))
        for i in range(4):
            b = full(dve, ("vb", i))
            dve.tensor_copy(vbt[:, :, i * P:(i + 1) * P], ps[:, b, :].rearrange("p (t d) -> p t d", t=NT)).then_inc(bank_empty(b), 1)

    mla_units = [(h, qt) for h in range(H2) for qt in range(NT)]

    def mla_tensor(pe):
        read(pe, ("uk", 3))
        pe.wait_ge(S("kb_ready"), H2 - 1)
        read(pe, ("rot2", H2 - 1))
        read(pe, ("vb", 3))

        def scores(u):
            h, qt = mla_units[u]
            claim(pe, u % 2, ("ms", u))
            pe.matmul(ps[:, u % 2, 0:(qt + 1) * P], qb[:, h, qt * P:(qt + 1) * P], kb[:, h, 0:(qt + 1) * P], start=True, stop=True)\
              .then_inc(bank_full(u % 2), 1)

        scores(0)
        for u, (h, qt) in enumerate(mla_units):
            if u + 1 < len(mla_units):
                scores(u + 1)
            pe.wait_ge(S("mp_ready"), u + 1)
            b = 2 + u % 2
            claim(pe, b, ("mt", u))
            for t in range(qt + 1):
                mm = pe.transpose(ps[:, b, t * P:(t + 1) * P], mp[u % 2][:, t * P:(t + 1) * P], ident)
            mm.then_inc(bank_full(b), 1)
            read(pe, ("mt", u))
            ob = 4 + h // 2 % 2
            if h % 2 == 0 and qt == 0:
                claim(pe, ob, ("ob", h // 2), (S("ob_ready"), h // 2 + 1))
            rows = slice(64 * (h % 2), 64 * (h % 2) + 64)
            for t in range(qt + 1):
                mm = pe.matmul(ps[rows, ob, qt * P:(qt + 1) * P], vbt[:, t, h * DH2:(h + 1) * DH2], mpT[u % 2][:, t, :],
                               start=(t == 0), stop=(t == qt))
            if h % 2 and qt == NT - 1:
                mm.then_inc(bank_full(ob), 1)
            else:
                mm.then_inc(S("mla_pv"), 1)

    def pv_done(u):
        return sum(not (h % 2 and qt == NT - 1) for h, qt in mla_units[:u + 1])

    def mla_scalar(act):
        def exps(u):
            h, qt = mla_units[u]
            keys = (qt + 1) * P
            if u >= 2:
                full(act, ("mt", u - 2))
            act.wait_ge(S("mla_max"), u + 1)
            b = held[("ms", u)][0]
            act.activation(mp[u % 2][:, 0:keys], ps[:, b, 0:keys], ACT.Exp, bias=sm["mla_max"][u % 2][:, :],
                           accum_out=sm["mla_sum"][u % 2][:, :]).then_inc(bank_empty(b), 1)

        exps(0)
        for u, (h, qt) in enumerate(mla_units):
            if u + 1 < len(mla_units):
                exps(u + 1)
            if u >= 2:
                ph, pqt = mla_units[u - 2]
                if ph % 2 and pqt == NT - 1:
                    full(act, ("ob", ph // 2))
                else:
                    act.wait_ge(S("mla_pv"), pv_done(u - 2))
            b = full(act, ("mt", u))
            act.activation(mpT[u % 2][:, 0:qt + 1, :], ps[:, b, 0:(qt + 1) * P].rearrange("p (t q) -> p t q", q=P), ACT.Copy)\
               .then_inc(bank_empty(b), 1)
            if h % 2 and qt == NT - 1:
                b = full(act, ("ob", h // 2))
                act.activation(obh[:, h // 2, :], ps[:, b, :], ACT.Copy).then_inc(S("ob_hi"), 1)

    def mla_vector(dve):
        def maxima(u):
            h, qt = mla_units[u]
            keys = (qt + 1) * P
            b = full(dve, ("ms", u))
            mark("mla_step", dve.memset(ps[0:64, b, keys - 64:keys], NEG))
            settle(dve, "mla_step")
            dve.tensor_reduce(sm["mla_max"][u % 2][:, :], ps[:, b, 0:keys], AX, ALU.max, negate=True).then_inc(S("mla_max"), 1)

        maxima(0)
        for u, (h, qt) in enumerate(mla_units):
            keys = (qt + 1) * P
            if u + 1 < len(mla_units):
                maxima(u + 1)
            read(dve, ("ms", u))
            mark("mla_step", dve.reciprocal(sm["mla_inv"][u % 2][:, :], sm["mla_sum"][u % 2][:, :]))
            settle(dve, "mla_step")
            dve.tensor_scalar(mp[u % 2][:, 0:keys], mp[u % 2][:, 0:keys], sm["mla_inv"][u % 2][:, :], None, ALU.mult)\
               .then_inc(S("mp_ready"), 1)
            if u % 2 == 0:
                topk_round(dve, u // 2)
            if h % 2 and qt == NT - 1:
                b = full(dve, ("ob", h // 2))
                dve.wait_ge(S("ob_hi"), h // 2 + 1)
                dve.tensor_tensor(obl[:, h // 2, :], ps[:, b, :], obh[:, h // 2, :].bitcast(F32), ALU.subtract).then_inc(S("ob_ready"), 1)
        topk_end(dve)

    dsa_units = list(range(N // QG))

    def dsa_tensor(pe):
        pe.wait_ge(S("table_ready"), 4)
        pe.wait_ge(S("identb_ready"), 1)
        read(pe, ("qa", 3))
        read(pe, "vat")
        pe.wait_ge(S("hide_ready"), 2 + NT - 1)

        def scores(u):
            qt, b = u // 8, u % 2
            keys = (qt + 1) * P
            claim(pe, b, ("ds", u))
            out = ps[:, b, 0:keys]
            pe.matmul(out, qa[:, u, :, :].rearrange("p h q -> p (h q)"), kva[0:64, 0:keys], start=True, stop=False)
            pe.matmul(out, identb[:, u % 8, :, :].rearrange("p h q -> p (h q)"), hide[qt][:, :], start=False, stop=False)
            for j in range(4):
                i = 4 * u + j
                pe.wait_ge(S("step_ready"), i + 1)
                pe.matmul(out, table_hi[:, j, :], step[i % NSTEP][:, 0:keys], start=False, stop=False)
                mm = pe.matmul(out, table_lo[:, j, :], step[i % NSTEP][:, 0:keys], start=False, stop=(j == 3))
            mm.then_inc(bank_full(b), 1)

        scores(0)
        for u in dsa_units:
            qt = u // 8
            if u + 1 < len(dsa_units):
                scores(u + 1)
            pe.wait_ge(S("pp_ready"), u + 1)
            b = 2 + u % 2
            claim(pe, b, ("dt", u))
            for t in range(qt + 1):
                mm = pe.transpose(ps[:, b, t * P:(t + 1) * P], pp[u % 2][:, t * P:(t + 1) * P], ident)
            mm.then_inc(bank_full(b), 1)
            read(pe, ("dt", u))
            ob = 4 + u // 4 % 2
            if u % 4 == 0:
                claim(pe, ob, ("oa", u // 4), (S("oa_ready"), 2 * (u // 4 + 1)))
            for t in range(qt + 1):
                mm = pe.matmul(ps[0:64, ob, (u % 4) * P:(u % 4 + 1) * P], vat[:, t, 64:128], ppT[u % 2][:, t, :],
                               start=(t == 0), stop=(t == qt))
            mm.then_inc(bank_full(ob) if u % 4 == 3 else S("dsa_pv"), 1)

    def oa_views(i, half):
        src = ps[0:64, held[("oa", i)][0], :].rearrange("p (u c z q) -> p c z u q", u=4, c=4, z=2)[:, :, half, :, :]
        rows, cols = slice(64 * half, 64 * half + 64), slice(i * 4 * QG, (i + 1) * 4 * QG)
        return src, oah[rows, :, cols].rearrange("p c (u q) -> p c u q", u=4), oal[rows, :, cols].rearrange("p c (u q) -> p c u q", u=4)

    def dsa_scalar(act):
        act.activation(identb[:, :, :, :], ident.rearrange("p (u q) -> p u q", q=QG).unsqueeze(2).broadcast_to([P, P // QG, H2, QG]), ACT.Copy)\
           .then_inc(S("identb_ready"), 1)
        for j in range(4):
            act.wait_ge(S("table_full"), j + 1)
            act.activation(table_hi[:, j, :], table[:, j, :], ACT.Copy).then_inc(S("table_hi"), 1)

        def exps(u):
            keys = (u // 8 + 1) * P
            if u >= 2:
                full(act, ("dt", u - 2))
            act.wait_ge(S("dsa_max"), u + 1)
            b = held[("ds", u)][0]
            act.activation(pp[u % 2][:, 0:keys], ps[:, b, 0:keys], ACT.Exp, bias=sm["dsa_max"][u % 2][:, :],
                           accum_out=sm["dsa_sum"][u % 2][:, :]).then_inc(bank_empty(b), 1)

        exps(0)
        for u in dsa_units:
            qt = u // 8
            if u + 1 < len(dsa_units):
                exps(u + 1)
            if u >= 2:
                if (u - 2) % 4 == 3:
                    full(act, ("oa", (u - 2) // 4))
                else:
                    act.wait_ge(S("dsa_pv"), 3 * ((u - 2) // 4) + (u - 2) % 4 + 1)
            b = full(act, ("dt", u))
            act.activation(ppT[u % 2][:, 0:qt + 1, :], ps[:, b, 0:(qt + 1) * P].rearrange("p (t q) -> p t q", q=P), ACT.Copy)\
               .then_inc(bank_empty(b), 1)
            if u % 4 == 3:
                full(act, ("oa", u // 4))
                for half in range(2):
                    src, hi, _ = oa_views(u // 4, half)
                    act.activation(hi, src, ACT.Copy).then_inc(S("oa_hi"), 1)

    def dsa_vector(dve):
        mark("table_step", dve.tensor_tensor(delta[:, :], v("bias_at"), v("bias_before"), ALU.subtract))
        settle(dve, "table_step")
        for j in range(4):
            dve.tensor_tensor(table[:, j, :].rearrange("p (h q) -> p h q", h=H2), delta[:, :].unsqueeze(2).broadcast_to([P, H2, QG]),
                              c("own_query", j * QG, (j + 1) * QG).unsqueeze(1).broadcast_to([P, H2, QG]), ALU.mult)\
               .then_inc(S("table_full"), 1)
        for j in range(4):
            dve.wait_ge(S("table_hi"), j + 1)
            dve.tensor_tensor(table_lo[:, j, :], table[:, j, :], table_hi[:, j, :].bitcast(F32), ALU.subtract).then_inc(S("table_ready"), 1)

        def steps(u):
            keys = (u // 8 + 1) * P
            if u >= 2:
                full(dve, ("ds", u - 2))
            for i in range(4 * u, 4 * u + 4):
                dve.tensor_scalar(step[i % NSTEP][:, 0:keys], posf[:, 0:keys], qfrom[:, i:i + 1], None, ALU.is_ge).then_inc(S("step_ready"), 1)

        def maxima(u):
            b = full(dve, ("ds", u))
            dve.tensor_reduce(sm["dsa_max"][u % 2][:, :], ps[:, b, 0:(u // 8 + 1) * P], AX, ALU.max, negate=True).then_inc(S("dsa_max"), 1)

        steps(0)
        steps(1)
        maxima(0)
        for u in dsa_units:
            keys = (u // 8 + 1) * P
            if u + 1 < len(dsa_units):
                maxima(u + 1)
            if u + 2 < len(dsa_units):
                steps(u + 2)
            read(dve, ("ds", u))
            mark("dsa_step", dve.reciprocal(sm["dsa_inv"][u % 2][:, :], sm["dsa_sum"][u % 2][:, :]))
            settle(dve, "dsa_step")
            dve.tensor_scalar(pp[u % 2][:, 0:keys], pp[u % 2][:, 0:keys], sm["dsa_inv"][u % 2][:, :], None, ALU.mult)\
               .then_inc(S("pp_ready"), 1)
            if u % 4 == 3:
                full(dve, ("oa", u // 4))
                for half in range(2):
                    src, hi, lo = oa_views(u // 4, half)
                    dve.wait_ge(S("oa_hi"), 2 * (u // 4) + 2)
                    dve.tensor_tensor(lo, src, hi.bitcast(F32), ALU.subtract).then_inc(S("oa_ready"), 1)

    def gated_specs(m):
        both = [("w_o_a_2", k * P, m * P) for k in range(4)] + [("w_o_b_2", k * P, m * P) for k in range(4)]
        return (in2((IN2["ga"] + m * P, IN2["ga"] + (m + 1) * P, 0)), in2((IN2["gb"] + m * P, IN2["gb"] + (m + 1) * P, 0)),
                ("", [(n, r, P, ((col, col + P, 0),)) for n, r, col in both]))

    def gated_tensor(pe):
        second["g_gated"] = len(slot_of)
        for m in range(KD):
            gate_a, gate_b, out_ab = gated_specs(m)
            for key, b, spec in (("ga", 0, gate_a), ("gb", 1, gate_b)):
                b += 4 * (m % 2)
                g = take_slot(pe, spec)
                claim(pe, b, (key, m))
                for k in range(KD):
                    mm = three_passes(pe, ps[:, b, :], g, k, P, hh[:, k, :], hl[:, k, :], k == 0, k == KD - 1)
                mm.then_inc(bank_full(b), 1)
                after[g] = (bank_full(b), bank_uses[b])
            g = take_slot(pe, out_ab)
            for key, b, hi, lo, first in (("pa", 2, oah, oal, 0), ("pb", 3, obh, obl, 4)):
                b += 4 * (m % 2)
                claim(pe, b, (key, m))
                if m == 0:
                    pe.wait_ge(S("oa_ready"), 2 * N // (4 * QG))
                    pe.wait_ge(S("ob_ready"), HEADS)
                for k in range(4):
                    mm = three_passes(pe, ps[:, b, :], g, first + k, P, hi[:, k, :], lo[:, k, :], k == 0, k == 3)
                mm.then_inc(bank_full(b), 1)
                after[g] = (bank_full(b), bank_uses[b])

    def gated_scalar(act):
        g0 = second["g_gated"]
        for m in range(KD):
            for i, (key, to) in enumerate((("ga", sig_a), ("gb", sig_b))):
                b = full(act, (key, m))
                split_slots(act, g0 + 3 * m + i + 2)
                if m >= 2:
                    act.wait_ge(S("y_ready"), m - 1)
                act.activation(to[m % 2][:, :], ps[:, b, :], ACT.Sigmoid).then_inc(bank_empty(b), 1)
            full(act, ("pb", m))
            split_slots(act, g0 + 3 * m + 4)
            act.wait_ge(S("y_sum"), m + 1)
            act.activation(yh[:, m, :], sig_a[m % 2][:, :], ACT.Copy).then_inc(S("y_hi"), 1)

    def gated_vector(dve):
        for m in range(KD):
            for key, gate, to in (("a", "ga", sig_a), ("b", "gb", sig_b)):
                read(dve, (gate, m))
                b = full(dve, ("p" + key, m))
                dve.tensor_tensor(to[m % 2][:, :], to[m % 2][:, :], ps[:, b, :], ALU.mult).then_inc(bank_empty(b), 1)
                read(dve, ("p" + key, m))
            dve.tensor_tensor(sig_a[m % 2][:, :], sig_a[m % 2][:, :], sig_b[m % 2][:, :], ALU.add).then_inc(S("y_sum"), 1)
            dve.wait_ge(S("y_hi"), m + 1)
            dve.tensor_tensor(yl[:, m, :], sig_a[m % 2][:, :], yh[:, m, :].bitcast(F32), ALU.subtract).then_inc(S("y_ready"), 1)

    def scaled(dve, to, scale, gains):
        mark("gain_ready", dve.scalar_tensor_tensor(out=to[:, :], in0=scale, scalar=1.0, in1=gains, op0=ALU.add, op1=ALU.mult))

    def gains_1(dve):
        scaled(dve, gain["x1"], mod[:, 8:16, 0], v("norm1_g"))
        scaled(dve, gain["c1"], mod[:, 8:16, 1], v("norm1_g"))
        settle(dve, "gain_ready")

    def gains_2(dve):
        scaled(dve, gain["x2"], mod[:, 32:40, 0], v("norm2_g"))
        settle(dve, "gain_ready")

    def gains_3(dve):
        scaled(dve, gain["f1"], ada[:, 8:16], v("g_ffn1"))
        scaled(dve, gain["mx"], ada[:, 32:40], v("g_mix"))
        scaled(dve, gain["f2"], ada[:, 56:64], v("g_ffn2"))
        for n, at in (("f1", 16), ("f2", 64)):
            mark("gain_ready", dve.tensor_scalar(half_gate[n][:, :], ada[:, at:at + KD], 0.5, None, ALU.mult))
        settle(dve, "gain_ready")

    def of(t):
        return lambda k: t[:, k:k + 1]

    def x_shift(at, which=0):
        return lambda k: mod[:, at + k, which:which + 1]

    def after_chunk(key):
        return lambda e, k: e.wait_ge(*residual(key, k + 1))

    def x_loaded(e, k):
        e.wait_ge(S(f"x_loaded{k // 4}"), 16)

    def c_loaded(e, k):
        e.wait_ge(S("c_loaded"), 16)

    block = ctx.enter_context(nc.Block())
    firsts = {}

    @block.tensor
    def _(pe):
        pe.wait_ge(S("cst_loaded"), 16)
        pe.wait_ge(S("vec_loaded"), 16)
        ada_slots(pe, 16)
        ada_batch_end()
        norm_tensor(pe, "nx", KD, N, 4, 4)
        norm_tensor(pe, "nc", KD, NCTX, 5, 5)
        projections_tensor(pe)
        diff_tensor(pe)
        gla_tensor(pe)
        firsts["mix1"] = len(slot_of)
        mixed_tensor(pe, "mix1", "w_out", hh, hl, [norm("ng", "ready", k + 1) for k in range(4)] + [norm("no", "ready", k + 1) for k in range(4)],
                     lambda m: 2 if m < 2 else 1)
        norm_tensor(pe, "n2", KD, N, 4, 5)
        ffn_tensor(pe, "ffn1", "n2", "w_ffn_in", "w_ffn_out", 2)
        norm_tensor(pe, "nf1", KD, N, 4, 5)
        ffn_tensor(pe, "ffn2", "nf1", "w_ffn1_in_2", "w_ffn1_down_2", 0)
        norm_tensor(pe, "nm", KD, N, 4, 5)
        proj2_tensor(pe)
        index_tensor(pe)
        lora_tensor(pe)
        mla_tensor(pe)
        dsa_tensor(pe)
        gated_tensor(pe)
        firsts["mix2"] = len(slot_of)
        mixed_tensor(pe, "mix2", "w_out_2", yh, yl, [(S("y_ready"), k + 1) for k in range(KD)], lambda m: 0)
        norm_tensor(pe, "nf2", KD, N, 4, 5)
        ffn_tensor(pe, "ffn3", "nf2", "w_ffn2_in_2", "w_ffn2_down_2", 0)
        norm_tensor(pe, "nfin", KD, N, 4, 5)

    @block.scalar
    def _(act):
        act.wait_ge(S("vec_loaded"), 16)
        act.wait_ge(S("cst_loaded"), 16)
        act.activation(cond[:, :, :], v("cond").rearrange("p (k t) -> p k t", t=2), ACT.Silu).then_inc(S("cond_ready"), 1)
        act.activation(cond2[:, :, 0], v("cond2"), ACT.Silu).then_inc(S("cond_ready"), 1)
        norm_scalar(act, "nx", xT, KD, N, D, hh, x_shift(0), x_loaded)
        norm_scalar(act, "nc", cT, KD, NCTX, D, ch, x_shift(0, 1), c_loaded)
        projections_scalar(act)
        diff_scalar(act)
        gla_scalar(act)
        mixed_scalar(act, "mix1", firsts["mix1"])
        norm_scalar(act, "n2", xT, KD, N, D, hh, x_shift(24), after_chunk("mix1"))
        ffn_scalar(act, "ffn1")
        norm_scalar(act, "nf1", xT, KD, N, D, hh, of(ada), after_chunk("ffn1"))
        ffn_scalar(act, "ffn2")
        norm_scalar(act, "nm", xT, KD, N, D, hh, lambda k: ada[:, 24 + k:25 + k], after_chunk("ffn2"))
        act.dma_start(posi[:, :], A["posi"]).then_inc(S("posi_loaded"), 16)
        act.dma_start(qposi[:, :], A["qposi"]).then_inc(S("qposi_loaded"), 16)
        split_slots(act, second["g_proj"] + 1)
        proj2_scalar(act)
        rope2_scalar(act)
        index_scalar(act)
        lora_scalar(act)
        mla_scalar(act)
        dsa_scalar(act)
        gated_scalar(act)
        mixed_scalar(act, "mix2", firsts["mix2"])
        norm_scalar(act, "nf2", xT, KD, N, D, hh, lambda k: ada[:, 48 + k:49 + k], after_chunk("mix2"))
        ffn_scalar(act, "ffn3")
        norm_scalar(act, "nfin", xT, KD, N, D, None, None, after_chunk("ffn3"))

    @block.vector
    def _(dve):
        dve.wait_ge(S("vec_loaded"), 16)
        dve.wait_ge(S("cst_loaded"), 16)
        ada_copy(dve, 0)
        gains_1(dve)
        x_loaded(dve, 0)
        x_loaded(dve, KD - 1)
        norm_vector(dve, "nx", xT, KD, N, of(gain["x1"]), hh, hl, x_shift(0))
        c_loaded(dve, 0)
        norm_vector(dve, "nc", cT, KD, NCTX, of(gain["c1"]), ch, cl, x_shift(0, 1))
        projections_vector(dve)
        ada_copy(dve, 1)
        gains_2(dve)
        dve.wait_ge(S("csta_loaded"), 16)
        diff_vector(dve)
        gla_vector(dve)
        mixed_vector(dve, "mix1", lambda m: mod[:, 16 + m, 0:1])
        ada_copy(dve, 2)
        norm_vector(dve, "n2", xT, KD, N, of(gain["x2"]), hh, hl, x_shift(24))
        ffn_vector(dve, "ffn1", lambda m: mod[:, 40 + m, 0:1])
        gains_3(dve)
        norm_vector(dve, "nf1", xT, KD, N, of(gain["f1"]), hh, hl, of(ada))
        ffn_vector(dve, "ffn2", of(half_gate["f1"]))
        norm_vector(dve, "nm", xT, KD, N, of(gain["mx"]), hh, hl, lambda k: ada[:, 24 + k:25 + k])
        dve.wait_ge(S("posi_loaded"), 16)
        dve.wait_ge(S("qposi_loaded"), 16)
        rope2_vector(dve)
        index_vector(dve)
        lora_vector(dve)
        mla_vector(dve)
        dsa_vector(dve)
        gated_vector(dve)
        mixed_vector(dve, "mix2", lambda m: ada[:, 40 + m:41 + m])
        norm_vector(dve, "nf2", xT, KD, N, of(gain["f2"]), hh, hl, lambda k: ada[:, 48 + k:49 + k])
        ffn_vector(dve, "ffn3", of(half_gate["f2"]))
        norm_vector(dve, "nfin", xT, KD, N, lambda k: v("g_final", k, k + 1), None, None, None, out=fin)

    @block.gpsimd
    def _(pool):
        split_lows(pool, 0, len(chunks_a))
        gla_gpsimd(pool)
        split_lows(pool, len(chunks_a), ffns["ffn1"]["g0"])
        ffn_gpsimd(pool, "ffn1")
        ffn_gpsimd(pool, "ffn2")
        split_lows(pool, ffns["ffn2"]["g1"] + KF, ffns["ffn3"]["g0"])
        ffn_gpsimd(pool, "ffn3")

    @block.sync
    def _(sp):
        sp.dma_start(vec[:, :], A["vec"]).then_inc(S("vec_loaded"), 16)
        sp.dma_start(cst[:, :], A["cst"]).then_inc(S("cst_loaded"), 16)
        for s in range(RING):
            sp.dma_start(raw[s][:, :], A["stream"][s * P:(s + 1) * P, :]).then_inc(S(f"landed{s}"), 16)
        for i in range(2):
            sp.dma_start(xT[:, 4 * i:4 * i + 4, :], A["xT"][:, 4 * i:4 * i + 4, :]).then_inc(S(f"x_loaded{i}"), 16)
        sp.dma_start(cT[:, :, :], A["cT"]).then_inc(S("c_loaded"), 16)
        sp.dma_start(csta[:, :], A["csta"]).then_inc(S("csta_loaded"), 16)
        with sp.Fori(1, len(stream) // RING) as it:
            for s in range(RING):
                sp.wait_ge(S(f"spent{s}"), it)
                sp.dma_start(raw[s][:, :], A["stream"][bass.ds(it * (RING * P) + s * P, P), :]).then_inc(S(f"landed{s}"), 16)
        for k in range(KD):
            sp.wait_ge(*norm("nfin", "t1", k + 1))
            sp.dma_start(A["out"][:, k, :], fin[:, k, :]).then_inc(S("stored"), 16)
        sp.wait_ge(S("stored"), 16 * KD)

    assert len(stream) == N_SLOTS and len(stream) % RING == 0
    ctx.close()
    return stream


def constants():
    p = np.arange(P)
    stay = np.zeros((P, NCST), np.float32)
    first = np.zeros((P, NCSTA), np.float32)

    def put(to, table, name, value):
        o, w = table[name]
        to[:, o:o + w] = value

    put(stay, CST, "ident", np.eye(P))
    put(stay, CST, "one", 1.0)
    put(stay, CST, "comp", p[:, None] // DIFF_DH == np.arange(2))
    put(stay, CST, "eps", EPS)
    half = ROPE2 // 2
    turn = np.zeros((P, ROPE2))
    for i in range(half):
        turn[DH2 + half + i, i] = -1.0
        turn[DH2 + i, half + i] = 1.0
    put(stay, CST, "rot2", turn)
    freq = np.float32(10000.0) ** (np.float32(-2.0) * np.arange(half, dtype=np.float32) / np.float32(ROPE2))
    put(stay, CST, "freq", freq[p % half][:, None])
    put(stay, CST, "bucket_from", np.array(BUCKET_FROM)[p % 32][:, None])
    put(stay, CST, "own_query", np.concatenate([np.arange(QG) == 4 * j + p[:, None] // 32 for j in range(4)], axis=1))

    rot = np.zeros((P, P))
    for o in range(0, P, 32):
        for i in range(16):
            rot[o + 16 + i, o + i] = -1.0
            rot[o + i, o + 16 + i] = 1.0
    put(first, CSTA, "rot", rot)
    t = np.arange(N)
    inv_freq = np.float32(10000.0) ** (-np.arange(16, dtype=np.float32) / np.float32(16))
    axis = (p % DIFF_DH) // 32
    at = np.where(axis[:, None] == 0, t // GRID_W, t % GRID_W).astype(np.float32)
    angle = at * inv_freq[p % 16][:, None]
    put(first, CSTA, "cos", np.cos(angle))
    put(first, CSTA, "sin", np.sin(angle))
    put(first, CSTA, "carry", (t % P != 0)[None, :])
    levels = [2.0 * np.eye(P)] + [(p[:, None] // (2 * s) == p // (2 * s)) & (p[:, None] // s != p // s) for s in LEVELS]
    put(first, CSTA, "levels", np.concatenate(levels, axis=1))
    return stay, first


def small_vectors(a):
    out = np.zeros((P, NVEC), np.float32)

    def put(name, value):
        o, w = VEC[name]
        out[:value.shape[0], o:o + w] = value

    def columns(w):
        return w.reshape(-1, P).T

    for name, src in (("norm1_g", "norm1_g"), ("norm2_g", "norm2_g"), ("g_ffn1", "g_ffn1_2"), ("g_mix", "g_mix_2"), ("g_ffn2", "g_ffn2_2"),
                      ("g_final", "g_final_2"), ("b_mod", "b_mod"), ("b_ada", "b_ada_2"), ("gla_g", "gla_norm_g"),
                      ("dn_g", "diff_norm_g"), ("g_cq", "g_cq_2"), ("g_ckv", "g_ckv_2"), ("cond2", "c_2"), ("gate_b", "gla_gate_bias")):
        put(name, columns(a[src]))
    put("dq_g", columns(np.tile(a["diff_q_norm_g"].reshape(-1), 2)))
    put("dk_g", columns(np.tile(a["diff_k_norm_g"].reshape(-1), 2)))
    put("cond", np.stack([columns(a["c"]), columns(a["c_ctx"])], axis=2).reshape(P, 2 * KD))
    put("lam_q", np.tile(a["diff_lambda_q"].reshape(1, -1), (P, 1)))
    put("lam_k", np.tile(a["diff_lambda_k"].reshape(1, -1), (P, 1)))
    up = np.zeros((32, 512), np.float32)
    for z in range(2):
        up[16 * z:16 * z + 16, 256 * z:256 * z + 256] = a["gla_gate_up"][0, z]
    put("gate_up", up)
    bias_at, bias_before = np.zeros((P, H2), np.float32), np.zeros((P, H2), np.float32)
    for p in range(P):
        if p % 32 < 31:
            bias_at[p] = a["rel_bias_2"][BUCKETS[p % 32]]
        if 1 <= p % 32 < 31:
            bias_before[p] = a["rel_bias_2"][BUCKETS[p % 32 - 1]]
    put("bias_at", bias_at)
    put("bias_before", bias_before)
    return out


def stream_array(a, stream):
    out = np.zeros((len(stream), P, KD, P), np.float32)
    for n, (name, tiles) in enumerate(stream):
        for i, tile in enumerate(tiles):
            source, row, rows, cuts = tile if not name else (name,) + tile
            w = a["w_ada_2" if source == "w_ada" else source]
            w = w.reshape(w.shape[-2:])
            for c0, c1, to in cuts:
                out[n, :rows, i, to:to + c1 - c0] = w[row:row + rows, c0:c1]
    return out.reshape(len(stream) * P, KD * P)


def kernel(**inputs):
    import concourse.bacc as bacc
    from concourse.bass_utils import run_bass_kernel_spmd

    a = {name: np.asarray(value) for name, value in inputs.items()}
    positions = a["positions_2"].reshape(N)
    cst, csta = constants()
    arrays = {
        "vec": small_vectors(a), "cst": cst, "csta": csta,
        "xT": np.ascontiguousarray(a["x"].reshape(N, KD, P).transpose(2, 1, 0)),
        "cT": np.ascontiguousarray(a["ctx"].reshape(NCTX, KD, P).transpose(2, 1, 0)),
        "posi": np.ascontiguousarray(np.broadcast_to(positions, (P, N))),
        "qposi": np.ascontiguousarray(np.repeat(positions.reshape(P, 4).T, 32, axis=0)),
    }
    nc = bacc.Bacc("TRN2", target_bir_lowering=False, num_devices=1)
    A = {name: nc.dram_tensor(name, v.shape, mybir.dt.from_np(v.dtype), kind="ExternalInput").ap() for name, v in arrays.items()}
    A["stream"] = nc.dram_tensor("stream", (N_SLOTS * P, SLOT), F32, kind="ExternalInput").ap()
    A["out"] = nc.dram_tensor("out", (P, KD, N), F32, kind="ExternalOutput").ap()
    arrays["stream"] = stream_array(a, build(nc, A))
    r = run_bass_kernel_spmd(nc, [arrays], core_ids=[0])
    return r.results[0]["out"].transpose(2, 1, 0).reshape(1, N, D)
```

```python
import math
from contextlib import ExitStack

import numpy as np

import concourse.bass as bass
from concourse import mybir

F32 = mybir.dt.float32
F32R = mybir.dt.float32r
BF16 = mybir.dt.bfloat16
I32 = mybir.dt.int32
U32 = mybir.dt.uint32
ALU = mybir.AluOpType
ACT = mybir.ActivationFunctionType
AX = mybir.AxisListType.X

P = 128
D = 1024
KD = D // P
N = 512
NCTX = 256
NALL = NCTX + N
NT, NTC, NTA = N // P, NCTX // P, NALL // P
FFN = 2816
KF = FFN // P
EPS = 1e-6
HEADS = 4
GLA_DK, DV, DIFF_DH = 64, 128, 64
LEVELS = [64, 32, 16, 8, 4, 2, 1]
GRID_W = 64
LAM_INIT = 0.8 - 0.6 * math.exp(-0.3 * 0)
H2 = 8
DH2, ROPE2 = 64, 32
QK2 = DH2 + ROPE2
Q_LORA, KV_LORA = 384, 256
TOPK = 128
ROUNDS = TOPK // 8
QG = 16
NEG = -3.0e38
TAKEN = -3.3e38
HIDE = -2.0 ** 100
BUCKET_START = [1, 2, 3, 4, 5, 6, 7, 8, 12, 16, 23, 32, 46, 64, 91]
BUCKETS = list(range(15, -1, -1)) + list(range(17, 32))
BUCKET_FROM = [-1e30] + [1 - s for s in reversed(BUCKET_START)] + [s for s in BUCKET_START] + [1e30]

RING = 4
SPLIT = 2
SLOT = KD * P
N_SLOTS = 420

VEC = {}
for _name, _w in (("norm1_g", 8), ("norm2_g", 8), ("g_ffn1", 8), ("g_mix", 8), ("g_ffn2", 8), ("g_final", 8),
                  ("b_mod", 48), ("b_ada", 72), ("gla_g", 1), ("dq_g", 1), ("dk_g", 1), ("dn_g", 1),
                  ("g_cq", 3), ("g_ckv", 2), ("gate_b", 4),
                  ("lam_q", 128), ("lam_k", 128), ("gate_up", 512), ("bias_at", 8), ("bias_before", 8)):
    VEC[_name] = (sum(w for _, w in VEC.values()), _w)
NVEC = sum(w for _, w in VEC.values())
CST = {}
for _name, _w in (("ident", 128), ("one", 1), ("comp", 2), ("eps", 1), ("rot2", 32), ("freq", 1), ("bucket_from", 1),
                  ("own_query", 64)):
    CST[_name] = (sum(w for _, w in CST.values()), _w)
NCST = sum(w for _, w in CST.values())
CSTA = {}
for _name, _w in (("rot", 128), ("cos", 512), ("sin", 512), ("carry", 512), ("levels", 128 * (1 + len(LEVELS)))):
    CSTA[_name] = (sum(w for _, w in CSTA.values()), _w)
NCSTA = sum(w for _, w in CSTA.values())


def full_columns(name, c, width=P):
    return (name, [(k * P, P, ((c, c + width, 0),)) for k in range(KD)])


def weight_rows(name, k):
    return (name, [(k * P, P, ((m * P, m * P + P, 0),)) for m in range(KD)])


def build(nc, A):
    ctx = ExitStack()
    sems = {}

    def S(name):
        if name not in sems:
            sems[name] = ctx.enter_context(nc.semaphore(name))
        return sems[name]

    top = [(nc.sbuf_base + 31) // 32 * 32]
    bytes_of = {F32: 4, F32R: 4, I32: 4, BF16: 2, U32: 4}

    def sb(name, shape, dt=F32):
        size = int(np.prod(shape[1:])) * bytes_of[dt]
        t = nc.alloc_sbuf_tensor_at(name, shape, dt, offset=top[0])
        top[0] += (size + 31) // 32 * 32
        assert top[0] <= nc.sbuf_usable_end, (name, top[0], nc.sbuf_usable_end)
        return t

    raw = [sb(f"raw{i}", [P, SLOT]) for i in range(RING)]
    w_hi = [sb(f"w_hi{i}", [P, SLOT], F32R) for i in range(SPLIT)]
    w_lo = [sb(f"w_lo{i}", [P, SLOT], F32R) for i in range(SPLIT)]
    xT = sb("xT", [P, KD, N])
    lq_odd = sb("lq_odd", [P, 2 * N])
    top[0] -= 2 * N * 4
    od = sb("od", [P, HEADS, N])
    top[0] -= HEADS * N * 4
    hh = sb("hh", [P, KD, N], F32R)
    lk = [sb(f"lk{i}", [P, 2 * N]) for i in range(2)]
    top[0] -= 2 * 2 * N * 4
    og = sb("og", [P, HEADS, N])
    top[0] -= HEADS * N * 4
    prob = [sb(f"prob{i}", [P, 2, NALL]) for i in range(2)]
    top[0] -= 2 * 2 * NALL * 4
    hl = sb("hl", [P, KD, N], F32R)
    sq = [sb(f"sq{i}", [P, NALL]) for i in range(2)]
    t1 = [sb(f"t1{i}", [P, NALL]) for i in range(2)]
    vec = sb("vec", [P, NVEC])
    cst = sb("cst", [P, NCST])
    mod = sb("mod", [P, 48, 2])
    ada = sb("ada", [P, 72])
    gain = {n: sb(f"gain_{n}", [P, KD]) for n in ("x1", "c1", "x2", "f1", "mx", "f2")}
    half_gate = {n: sb(f"half_gate_{n}", [P, KD]) for n in ("f1", "f2")}
    std = {}
    rs = {}
    for n, w in (("nx", NT), ("nc", NTC), ("nq", 32), ("nk", 48), ("no", 16), ("ng", 16), ("n2", NT), ("nf1", NT),
                 ("nm", NT), ("ncq", NT), ("nckv", NT), ("nf2", NT), ("nfin", NT)):
        std[n], rs[n] = sb(f"std_{n}", [P, w]), sb(f"rs_{n}", [P, w])
    lam = sb("lam", [P, 8])
    gain_dn = sb("gain_dn", [P, 1])
    gain_dq = sb("gain_dq", [P, 1])
    cond_ada = sb("cond_ada", [P, D])
    region = top[0]

    gkx = sb("gkx", [P, 2, N])
    gkc = sb("gkc", [P, 2, NCTX])
    gqx = sb("gqx", [P, 2, N])
    rT = sb("rT", [P, HEADS, N])
    vt = sb("vt", [P, NTA, HEADS * DV])
    dn = sb("dn", [32, NALL])
    csta = sb("csta", [P, NCSTA])
    cond = sb("cond", [P, D])
    region_diff = top[0]
    dq = sb("dq", [P, HEADS, N])
    dk = sb("dk", [P, HEADS, NALL])
    dvt = sb("dvt", [P, NTA, HEADS * DV])
    end_dvt, top[0] = top[0], top[0] - NTA * HEADS * DV * 4
    cond_ctx = sb("cond_ctx", [P, D])
    top[0] = end_dvt
    rot_q = sb("rot_q", [P, P])
    rot_k = sb("rot_k", [P, P])
    region_tmp = top[0]
    cT = sb("cT", [P, KD, NCTX])
    ch = sb("ch", [P, KD, NCTX], F32R)
    cl = sb("cl", [P, KD, NCTX], F32R)
    top[0] = region_tmp
    dqc = sb("dqc", [P, HEADS, 2, N])
    probT = [sb(f"probT{i}", [P, NTA, P]) for i in range(2)]
    neg_max = [sb(f"neg_max{i}", [P, 2]) for i in range(2)]
    total = [sb(f"total{i}", [P, 2]) for i in range(2)]
    inv = [sb(f"inv{i}", [P, 4]) for i in range(2)]
    top[0] = region_diff
    cumx = sb("cumx", [P, 2, 2 * N])
    cumc = sb("cumc", [P, 2, 2 * NCTX])
    region_yb = top[0]
    kdT = sb("kdT", [P, 2, NTA, 2 * P])
    end_kdT, top[0] = top[0], region_yb
    gate = [sb(f"gate{i}", [P, NALL]) for i in range(4)]
    soft = [sb(f"soft{i}", [P, NALL]) for i in range(4)]
    top[0] = end_kdT
    decay = sb("decay", [P, 2, 2, NTA])
    states = sb("states", [P, 2, 2, NT + 1, DV])
    qe = sb("qe", [P, 2, 2 * N])
    attnT = sb("attnT", [P, NT, HEADS, P])
    lq = [sb("lq_even", [P, 2 * N]), lq_odd]

    top[0] = region
    act_hi = sb("act_hi", [P, KF * N], F32R)
    act_lo = sb("act_lo", [P, KF * N], F32R)
    silu = [sb(f"silu{i}", [P, N]) for i in range(2)]
    prod = [sb(f"prod{i}", [P, N]) for i in range(2)]

    region_second = region - D * 4
    top[0] = region_second
    posi = sb("posi", [P, N], I32)
    qposi = sb("qposi", [P, P], I32)
    top[0] = region_second
    qa = sb("qa", [P, N // QG, H2, QG], F32R)
    kva = t1[0][:, 0:N]
    vat = sb("vat", [P, NT, DH2])
    region_qi = top[0]
    qi = sb("qi", [P, H2, N], F32R)
    ki_hi = sb("ki_hi", [P, N], F32R)
    ki_lo = sb("ki_lo", [P, N], F32R)
    wkr = sb("wkr", [P, N])
    posf = sb("posf", [P, N])
    qfrom = sb("qfrom", [P, P])
    cosr = sb("cosr", [P, N])
    sinr = sb("sinr", [P, N])
    ka_hi = sb("ka_hi", [P, N], F32R)
    ka_lo = sb("ka_lo", [P, N], F32R)
    wt = sb("wt", [P, NT, H2])
    best = sb("best", [P, 3, 8])
    sm = {n: [sb(f"{n}{i}", [P, 1]) for i in range(2)] for n in ("mla_max", "mla_sum", "mla_inv", "dsa_max", "dsa_sum", "dsa_inv")}
    region_lora = top[0]
    cq = sb("cq", [P, 3, N])
    cqh = sb("cqh", [P, 3, N], F32R)
    cql = sb("cql", [P, 3, N], F32R)
    region_ckv = top[0]
    ckv = sb("ckv", [P, 2, N])
    ckvh = sb("ckvh", [P, 2, N], F32R)
    ckvl = sb("ckvl", [P, 2, N], F32R)
    top[0] = region_lora
    kb = sb("kb", [QK2, H2, N])
    top[0] = region_lora
    y_b = sb("y_b", [P, KD, N])
    top[0] = region_ckv
    obh = sb("obh", [P, HEADS, N], F32R)
    obl = sb("obl", [P, HEADS, N], F32R)
    top[0] = region_ckv
    oah = sb("oah", [P, HEADS, N], F32R)
    oal = sb("oal", [P, HEADS, N], F32R)
    score = [sb(f"score{i}", [P, (i + 2) * P]) for i in range(3)]
    hide = [sb(f"hide{i}", [P, (i + 1) * P], BF16) for i in range(4)]
    region_mla = top[0]
    qb = sb("qb", [QK2, H2, N])
    top[0] = region_qi
    mp = [sb(f"mp{i}", [P, N]) for i in range(2)]
    mpT = [sb(f"mpT{i}", [P, NT, P]) for i in range(2)]
    region_vbt = top[0]
    vbt = sb("vbt", [P, NT, H2 * DH2])
    top[0] = region_vbt
    table = sb("table", [P, 4, P])
    table_hi = sb("table_hi", [P, 4, P], F32R)
    table_lo = sb("table_lo", [P, 4, P], F32R)
    identb = sb("identb", [P, P // QG, H2, QG], BF16)
    top[0] = region_mla
    NSTEP = 8
    step = [sb(f"step{i}", [P, N], F32R) for i in range(NSTEP)]
    delta = sb("delta", [P, H2])
    pp, ppT = mp, mpT
    top[0] = region_second
    yh = sb("yh", [P, KD, N], F32R)
    yl = sb("yl", [P, KD, N], F32R)
    top[0] = region_mla
    sig = [sb(f"sig{i}", [P, N]) for i in range(4)]

    top[0] = region
    fin = sb("fin", [P, KD, N])

    ps = ctx.enter_context(nc.psum_tensor("ps", [P, 8, 512], F32))

    def v(name, a=0, b=None):
        o, w = VEC[name]
        return vec[:, o + a:o + (w if b is None else b)]

    def c(name, a=0, b=None):
        o, w = CST[name]
        return cst[:, o + a:o + (w if b is None else b)]

    def ca(name, a=0, b=None):
        o, w = CSTA[name]
        return csta[:, o + a:o + (w if b is None else b)]

    ident = c("ident")

    stream = []
    slot_of = []
    after = []
    bank_uses = [0] * 8
    bank_empties = [0] * 8
    bank_freed = [None] * 8
    held = {}
    marks = {}
    firsts = {}

    def landed(n):
        return S(f"landed{n % RING}"), 16 * (n // RING + 1)

    def spent(n):
        return S(f"spent{n % RING}"), n // RING + 1

    def bank_full(b):
        return S(f"bank_full{b}")

    def bank_empty(b):
        return S(f"bank_empty{b}")

    def mark(name, ins):
        marks[name] = marks.get(name, 0) + 1
        ins.then_inc(S(name), 1)
        return marks[name]

    def settle(eng, name):
        eng.wait_ge(S(name), marks[name])

    def claim(pe, b, key, freed=None):
        if bank_freed[b] is not None:
            pe.wait_ge(*bank_freed[b])
        bank_uses[b] += 1
        if freed is None:
            bank_empties[b] += 1
            freed = (bank_empty(b), bank_empties[b])
        bank_freed[b] = freed
        held[key] = (b, bank_uses[b], freed)

    def also(b, key):
        bank_uses[b] += 1
        held[key] = (b, bank_uses[b], bank_freed[b])

    def full(eng, key):
        b, n, _ = held[key]
        eng.wait_ge(bank_full(b), n)
        return b

    def read(eng, key):
        b, _, freed = held[key]
        eng.wait_ge(*freed)
        return b

    def new_slot(spec):
        slot_of.append(len(stream))
        after.append(None)
        stream.append(spec)

    def take_slot(pe, spec):
        new_slot(spec)
        pe.wait_ge(*spent(slot_of[-1]))
        return len(slot_of) - 1

    def three_passes(pe, out, g, tile, width, rh, rl, first, last):
        wh = w_hi[g % SPLIT][:, tile * P:tile * P + width]
        wl = w_lo[g % SPLIT][:, tile * P:tile * P + width]
        pairs = ((wh, rh), (wh, rl), (wl, rh))
        for i, (w, r) in enumerate(pairs):
            mm = pe.matmul(out, w, r, start=first and i == 0, stop=last and i == 2)
        return mm

    next_split = [0]

    def split_slots(act, upto):
        while next_split[0] <= upto and next_split[0] < len(slot_of):
            g = next_split[0]
            act.wait_ge(*landed(slot_of[g]))
            if g >= SPLIT:
                act.wait_ge(*after[g - SPLIT])
            act.activation(w_hi[g % SPLIT][:, :], raw[slot_of[g] % RING][:, :], ACT.Copy).then_inc(S("w_hi_ready"), 1)
            next_split[0] += 1

    mod_todo = [("w_mod", j) for j in range(6 * KD)] + [("w_ada_2", j) for j in range(9 * KD)]
    mod_place = {}

    def modulation_slots(count, todo=mod_todo):
        now = todo[:count]
        del todo[:count]
        for name, j in now:
            mod_place[(name, j)] = len(stream)
            stream.append(("w_mod" if name == "w_ctx" else name, j))
        return now

    def modulations(dve, chunks):
        for name, j in chunks:
            n = mod_place[(name, j)]
            if j == 0:
                dve.wait_ge(S("cond_ready"), {"w_mod": 1, "w_ctx": 2, "w_ada_2": 3}[name])
            dve.wait_ge(*landed(n))
            slot = raw[n % RING][:, :]
            if name == "w_ada_2":
                to, condition = ada[:, j:j + 1], cond_ada[:, :]
            elif name == "w_ctx":
                to, condition = mod[:, j, 1:2], cond_ctx[:, :]
            else:
                to, condition = mod[:, j, 0:1], cond[:, :]
            dve.scalar_tensor_tensor(out=slot, in0=slot, scalar=1.0, in1=condition, op0=ALU.mult, op1=ALU.mult, accum_out=to)\
               .then_inc(spent(n)[0], 1)

    def norm_modulation(dve, name, of_context):
        dve.wait_ge(*spent(mod_place[(name, 2 * KD - 1)]))
        m = mod[:, 0:2 * KD, of_context]
        mark("mod_ready", dve.tensor_tensor(m, m, v("b_mod", 0, 2 * KD), ALU.add))
        settle(dve, "mod_ready")

    def modulation_biases(dve, name):
        if name == "w_mod":
            dve.wait_ge(*spent(mod_place[(name, 6 * KD - 1)]))
            mark("mod_ready", dve.tensor_tensor(mod[:, 2 * KD:, 0], mod[:, 2 * KD:, 0], v("b_mod", 2 * KD), ALU.add))
        else:
            cols = slice(0, 8 * KD) if name == "w_ada_2" else slice(8 * KD, 9 * KD)
            dve.wait_ge(*spent(mod_place[("w_ada_2", cols.stop - 1)]))
            mark("mod_ready", dve.tensor_tensor(ada[:, cols], ada[:, cols], v("b_ada", cols.start, cols.stop), ALU.add))
        settle(dve, "mod_ready")

    norm_base = {}
    norm_next = dict(sq=0, sq_used=0, rs=0, t1=0, hi=0, ready=0, gated=0)

    def norm_starts(key, chunks, gated=0):
        norm_base[key] = dict(norm_next)
        for what, count in (("sq", chunks), ("sq_used", chunks - 1), ("rs", 1), ("t1", chunks), ("hi", chunks), ("ready", chunks),
                            ("gated", gated)):
            norm_next[what] += count

    def norm(key, what, count):
        return S("norm_" + what), norm_base[key][what] + count

    def norm_sum(pe, key, k, chunks, tokens, ba):
        if k == 0:
            norm_starts(key, chunks)
            claim(pe, ba, key + "_ss")
        pe.wait_ge(*norm(key, "sq", k + 1))
        for t in range(tokens // P):
            mm = pe.matmul(ps[:, ba, t * P:(t + 1) * P], sq[k % 2][:, t * P:(t + 1) * P], c("one").broadcast_to([P, P]),
                           start=(k == 0 and t == 0), stop=(k == chunks - 1), skip_group_check=True)
        mm.then_inc(S("norm_sq_used") if k < chunks - 1 else bank_full(ba), 1)

    def norm_tensor(pe, key, chunks, tokens, ba, bb, first=0):
        tiles = tokens // P
        for k in range(first, chunks):
            norm_sum(pe, key, k, chunks, tokens, ba)
        claim(pe, bb, key + "_rs", norm(key, "t1", chunks))
        pe.wait_ge(*norm(key, "rs", 1))
        for t in range(tiles):
            mm = pe.matmul(ps[:, bb, t * P:(t + 1) * P], rs[key][:, t:t + 1].broadcast_to([P, P]), ident,
                           start=True, stop=True)
        mm.then_inc(bank_full(bb), 1)

    def norm_square(act, key, src, k, tokens, ready):
        ready(act, k)
        if k >= 2:
            act.wait_ge(*norm(key, "sq_used", k - 1))
        act.activation(sq[k % 2][:, 0:tokens], src[:, k, :], ACT.Square).then_inc(S("norm_sq"), 1)

    def norm_scalar(act, key, src, chunks, tokens, width, hi, shift, ready, meanwhile=None):
        if ready is not None:
            for k in range(chunks):
                norm_square(act, key, src, k, tokens, ready)
        b = full(act, key + "_ss")
        act.activation(std[key][:, :], ps[:, b, 0:tokens:P], ACT.Sqrt, bias=c("eps"), scale=1.0 / width).then_inc(bank_empty(b), 1)
        if hi is None:
            return
        if meanwhile is not None:
            meanwhile()
        for k in range(chunks):
            act.wait_ge(*norm(key, "t1", k + 1))
            if shift is None:
                act.activation(hi[:, k, :], t1[k % 2][:, 0:tokens], ACT.Copy).then_inc(S("norm_hi"), 1)
            else:
                act.activation(hi[:, k, :], t1[k % 2][:, 0:tokens], ACT.Identity, bias=shift(k)).then_inc(S("norm_hi"), 1)

    def norm_vector(dve, key, src, chunks, tokens, gains, hi, lo, shift, out=None):
        read(dve, key + "_ss")
        dve.reciprocal(rs[key][:, :], std[key][:, :]).then_inc(S("norm_rs"), 1)
        b = full(dve, key + "_rs")

        def low(k):
            dve.wait_ge(*norm(key, "hi", k + 1))
            if shift is None:
                dve.tensor_tensor(lo[:, k, :], t1[k % 2][:, 0:tokens], hi[:, k, :].bitcast(F32), ALU.subtract)\
                   .then_inc(S("norm_ready"), 1)
            else:
                dve.scalar_tensor_tensor(out=lo[:, k, :], in0=t1[k % 2][:, 0:tokens], scalar=shift(k),
                                         in1=hi[:, k, :].bitcast(F32), op0=ALU.add, op1=ALU.subtract)\
                   .then_inc(S("norm_ready"), 1)

        for k in range(chunks):
            if k >= 2 and out is None:
                dve.wait_ge(*norm(key, "ready", k - 1))
            to = out[:, k, :] if out is not None else t1[k % 2][:, 0:tokens]
            dve.scalar_tensor_tensor(out=to, in0=src[:, k, :], scalar=gains(k), in1=ps[:, b, 0:tokens],
                                     op0=ALU.mult, op1=ALU.mult).then_inc(S("norm_t1"), 1)
            if k >= 1 and out is None:
                low(k - 1)
        if out is None:
            low(chunks - 1)


    def head_norm_starts(key, gated=0):
        norm_starts(key, HEADS, gated)
        norm_next["sq_used"] = norm_base[key]["sq_used"]
        norm_next["rs"] = norm_base[key]["rs"] + HEADS

    def head_sum(pe, key, h, b):
        claim(pe, b, (key + "_ss", h))
        pe.wait_ge(*norm(key, "sq", h + 1))
        for t in range(NT):
            mm = pe.matmul(ps[:, b, t * P:(t + 1) * P], sq[h % 2][:, t * P:(t + 1) * P], c("one").broadcast_to([P, P]),
                           start=True, stop=True)
        mm.then_inc(bank_full(b), 1)

    def head_spread(pe, key, h, b):
        claim(pe, b, (key, h), norm(key, "t1", h + 1))
        pe.wait_ge(*norm(key, "rs", h + 1))
        for t in range(NT):
            mm = pe.matmul(ps[:, b, t * P:(t + 1) * P], rs[key][:, h * NT + t:h * NT + t + 1].broadcast_to([P, P]),
                           ident, start=True, stop=True)
        mm.then_inc(bank_full(b), 1)

    def head_norm_scalar(act, key, src, chunk0, ready, final, meanwhile=None):
        for turn in range(HEADS + 2):
            h = turn
            if h < HEADS:
                ready(act, h)
                act.activation(sq[h % 2][:, 0:N], src[:, h, :], ACT.Square).then_inc(S("norm_sq"), 1)
            h = turn - 1
            if 0 <= h < HEADS:
                b = full(act, (key + "_ss", h))
                act.activation(std[key][:, h * NT:(h + 1) * NT], ps[:, b, 0:N:P], ACT.Sqrt, bias=c("eps"), scale=1.0 / DV)\
                   .then_inc(bank_empty(b), 1)
            h = turn - 2
            if 0 <= h < HEADS:
                if h == HEADS - 1 and meanwhile is not None:
                    meanwhile()
                act.wait_ge(*norm(key, final, h + 1))
                act.activation(hh[:, chunk0 + h, :], t1[h % 2][:, 0:N], ACT.Copy).then_inc(S("norm_hi"), 1)

    def head_norm_vector(dve, key, src, chunk0, gains, times, meanwhile=None):
        def low(h):
            dve.wait_ge(*norm(key, "hi", h + 1))
            dve.tensor_tensor(hl[:, chunk0 + h, :], t1[h % 2][:, 0:N], hh[:, chunk0 + h, :].bitcast(F32), ALU.subtract)\
               .then_inc(S("norm_ready"), 1)

        for h in range(HEADS):
            read(dve, (key + "_ss", h))
            cols = slice(h * NT, (h + 1) * NT)
            dve.reciprocal(rs[key][:, cols], std[key][:, cols]).then_inc(S("norm_rs"), 1)
            b = full(dve, (key, h))
            if h >= 2:
                dve.wait_ge(*norm(key, "ready", h - 1))
            dve.scalar_tensor_tensor(out=t1[h % 2][:, 0:N], in0=src[:, h, :], scalar=gains, in1=ps[:, b, :],
                                     op0=ALU.mult, op1=ALU.mult).then_inc(S("norm_t1"), 1)
            if times is not None:
                dve.wait_ge(*norm(key, "t1", h + 1))
                dve.tensor_tensor(t1[h % 2][:, 0:N], t1[h % 2][:, 0:N], times[:, h, :], ALU.mult)\
                   .then_inc(S("norm_gated"), 1)
            if meanwhile is not None:
                meanwhile(h)
            if h:
                low(h - 1)
        low(HEADS - 1)

    GQ, GK, GV, GR, GD, DQ, DK, DVC = 0, 256, 512, 1024, 1536, 1568, 2080, 2592
    chunks_a = ([("gq", i, GQ + i * P, P, False) for i in range(2)] + [("dq", h, DQ + h * P, P, False) for h in range(HEADS)]
                + [("gr", h, GR + h * P, P, False) for h in range(HEADS)] + [("dk", h, DK + h * P, P, True) for h in range(HEADS)]
                + [("dv", h, DVC + h * P, P, True) for h in range(HEADS)] + [("gd", 0, GD, 32, True)]
                + [("gk", i, GK + i * P, P, True) for i in range(2)] + [("gv", h, GV + h * P, P, True) for h in range(HEADS)])
    AT_NC, AT_SUMS, AT_TURNS = 4, 8, 17
    v_chunks = [(name, h) for name, h, *_ in chunks_a if name in ("dv", "gv")]
    chunk_of = {(name, h): i for i, (name, h, *_) in enumerate(chunks_a)}

    mods_of_chunk = []

    def projections_tensor(pe):
        def to_tokens(name, h):
            i = v_chunks.index((name, h))
            read(pe, ("c", chunk_of[(name, h)]))
            claim(pe, 4, ("vA", i))
            for t in range(4):
                mm = pe.transpose(ps[:, 4, t * P:(t + 1) * P], sq[i % 2][:, t * P:(t + 1) * P], ident)
            mm.then_inc(bank_full(4), 1)
            claim(pe, 5, ("vB", i))
            for t in range(4, NTA):
                mm = pe.transpose(ps[:, 5, (t - 4) * P:(t - 3) * P], sq[i % 2][:, t * P:(t + 1) * P], ident)
            mm.then_inc(bank_full(5), 1)

        last = None
        ctx_todo = [("w_ctx", j) for j in range(2 * KD)]
        g0 = len(slot_of)
        specs = [full_columns("w_in", col, width) for _, _, col, width, _ in chunks_a]
        for spec in specs[:2]:
            new_slot(spec)
        for i, (name, h, col, width, both) in enumerate(chunks_a):
            if i + 2 < len(specs):
                new_slot(specs[i + 2])
            mods_of_chunk.append(modulation_slots(4, ctx_todo) or modulation_slots(4))
            g = g0 + i
            pe.wait_ge(*spent(slot_of[g]))
            for key, b, rh, rl, tokens, key_norm in ((("x", i), i % 2, hh, hl, N, "nx"), (("c", i), 2 + i % 2, ch, cl, NCTX, "nc"))[:1 + both]:
                claim(pe, b, key)
                for k in range(KD):
                    if i == 0 or key == ("c", AT_SUMS + 2):
                        pe.wait_ge(*norm(key_norm, "ready", k + 1))
                    mm = three_passes(pe, ps[0:width, b, 0:tokens], g, k, width, rh[:, k, :], rl[:, k, :], k == 0, k == KD - 1)
                mm.then_inc(bank_full(b), 1)
                after[g] = (bank_full(b), bank_uses[b])
            if last:
                to_tokens(*last)
            last = (name, h) if name in ("dv", "gv") else None
            if i == AT_NC + 1:
                norm_tensor(pe, "nc", KD, NCTX, 6, 7)
            if AT_SUMS <= i < AT_SUMS + 2 * HEADS:
                diff_sums(pe, i - AT_SUMS)
            if i >= AT_TURNS:
                diff_turn(pe, i - AT_TURNS)
        assert len(chunks_a) == AT_TURNS + 2 * HEADS and chunks_a[AT_SUMS + 2][0] == "dk"
        if last:
            to_tokens(*last)

    def projections_scalar(act):
        for i, (name, h, col, width, both) in enumerate(chunks_a):
            ctx_to, x_to, func, scale = {
                "dk": lambda: (dk[:, h, 0:NCTX], dk[:, h, NCTX:], ACT.Copy, 1.0),
                "dv": lambda: (sq[v_chunks.index((name, h)) % 2][:, 0:NCTX], sq[v_chunks.index((name, h)) % 2][:, NCTX:], ACT.Copy, 1.0),
                "gv": lambda: (sq[v_chunks.index((name, h)) % 2][:, 0:NCTX], sq[v_chunks.index((name, h)) % 2][:, NCTX:], ACT.Copy, 1.0),
                "dq": lambda: (None, dq[:, h, :], ACT.Copy, 1.0),
                "gd": lambda: (dn[:, 0:NCTX], dn[:, NCTX:], ACT.Copy, 1.0),
                "gk": lambda: (gkc[:, h, :], gkx[:, h, :], ACT.Copy, 1.0),
                "gq": lambda: (None, gqx[:, h, :], ACT.Copy, GLA_DK ** -0.5),
                "gr": lambda: (None, rT[:, h, :], ACT.Silu, 1.0)}[name]()
            if name in ("dv", "gv") and v_chunks.index((name, h)) >= 2:
                full(act, ("vB", v_chunks.index((name, h)) - 2))
            b = full(act, ("x", i))
            ins = act.activation(x_to, ps[0:width, b, 0:N], func, scale=scale).then_inc(bank_empty(b), 1)
            if both:
                b = full(act, ("c", i))
                act.activation(ctx_to, ps[0:width, b, 0:NCTX], func, scale=scale).then_inc(bank_empty(b), 1)
            split_slots(act, min(i + 2, len(chunks_a) - 1))
            if i == AT_NC:
                norm_scalar(act, "nc", cT, KD, NCTX, D, ch, x_shift(0, 1), c_loaded)
            if AT_SUMS - 1 <= i < AT_SUMS - 1 + 2 * HEADS:
                diff_square(act, i - AT_SUMS + 1)
            for key, at in (("nq", AT_SUMS + HEADS), ("nk", AT_SUMS + 2 * HEADS)):
                if i == at:
                    b = full(act, key + "_ss")
                    act.activation(std[key][:, :], ps[:, b, 0:std[key].shape[1]], ACT.Sqrt, bias=c("eps"), scale=1.0 / DIFF_DH)\
                       .then_inc(bank_empty(b), 1)

    def projections_vector(dve):
        for i, chunks in enumerate(mods_of_chunk):
            modulations(dve, chunks)
            if i and chunks_a[i - 1][0] in ("dv", "gv"):
                values_vector(dve, *chunks_a[i - 1][:2])
            if i == AT_NC:
                norm_modulation(dve, "w_ctx", 1)
                scaled(dve, gain["c1"], mod[:, 8:16, 1], v("norm1_g"))
                settle(dve, "gain_ready")
                c_loaded(dve, 0)
                norm_vector(dve, "nc", cT, KD, NCTX, of(gain["c1"]), ch, cl, x_shift(0, 1))
            if i == AT_NC + 1:
                diff_gains(dve)
            for key, at in (("nq", AT_SUMS + HEADS + 1), ("nk", AT_TURNS)):
                if i == at:
                    read(dve, key + "_ss")
                    mark("diff_rs", dve.reciprocal(rs[key][:, :], std[key][:, :]))
            if i >= AT_TURNS:
                diff_rotate(dve, i - AT_TURNS)
        if chunks_a[-1][0] in ("dv", "gv"):
            values_vector(dve, *chunks_a[-1][:2])

    def values_vector(dve, name, h):
        i, to = v_chunks.index((name, h)), dvt if name == "dv" else vt
        b = full(dve, ("vA", i))
        dve.tensor_copy(to[:, 0:4, h * DV:(h + 1) * DV], ps[:, b, :].rearrange("p (t d) -> p t d", t=4)).then_inc(bank_empty(b), 1)
        b = full(dve, ("vB", i))
        dve.tensor_copy(to[:, 4:NTA, h * DV:(h + 1) * DV], ps[:, b, 0:2 * P].rearrange("p (t d) -> p t d", t=2))\
           .then_inc(bank_empty(b), 1)

    pairs = [(h, qt) for h in range(HEADS) for qt in range(NT)]
    flat = ps[:, :, :].rearrange("p b n -> p (b n)")

    def diff_sums(pe, i):
        h, tiles, b, key = i % HEADS, (NT, NTA)[i // HEADS], 6 + i // HEADS, ("nq", "nk")[i // HEADS]
        if h == 0:
            claim(pe, b, key + "_ss")
        pe.wait_ge(S("diff_sq"), i + 1)
        for t in range(tiles):
            at = 2 * (h * tiles + t)
            mm = pe.matmul(ps[:, b, at:at + 2], t1[i % 2][:, t * P:(t + 1) * P], c("comp"), start=True, stop=True)
        mm.then_inc(bank_full(b) if h == HEADS - 1 else S("diff_sq_used"), 1)

    def diff_square(act, i):
        h, key = i % HEADS, ("dq", "dk")[i // HEADS]
        src, at = (dq, dk)[i // HEADS], chunk_of[(key, h)]
        read(act, ("x", at))
        if key == "dk":
            read(act, ("c", at))
        if i == 0:
            act.wait_ge(*norm("nc", "ready", KD))
        if i >= 2:
            j = i - 2
            if j == HEADS - 1:
                full(act, "nq_ss")
            else:
                act.wait_ge(S("diff_sq_used"), j + 1 - (j >= HEADS))
        act.activation(t1[i % 2][:, 0:src.shape[2]], src[:, h, :], ACT.Square).then_inc(S("diff_sq"), 1)

    def spread(pe, b, key, at, t):
        for comp in range(2):
            mm = pe.matmul(ps[64 * comp:64 * comp + 64, b, t * P:(t + 1) * P],
                           rs[key][:, at + comp:at + comp + 1].broadcast_to([P, DIFF_DH]), ident, start=True, stop=True)
        return mm

    def diff_turn(pe, i):
        h, key = i // 2, "qk"[i % 2]
        if i == 0:
            pe.wait_ge(S("rot_ready"), 2)
        claim(pe, 6, ("rot_" + key, h))
        w, src = (rot_k, dk[:, h, NCTX:]) if i % 2 else (rot_q, dq[:, h, :])
        pe.matmul(ps[:, 6, :], w[:, :], src, start=True, stop=True).then_inc(bank_full(6), 1)
        claim(pe, 7, ("rs_" + key, h), (S("diff_rotated"), i + 1))
        if i < 2:
            pe.wait_ge(S("diff_rs"), i + 1)
        for t in range(NT):
            mm = spread(pe, 7, "n" + key, 2 * (h * NTA + NTC + t if i % 2 else h * NT + t), t)
        mm.then_inc(bank_full(7), 1)

    def diff_gains(dve):
        dve.wait_ge(S("csta_loaded"), 16)
        mark("lam", dve.tensor_scalar(gain_dq[:, :], v("dq_g"), DIFF_DH ** -0.5, None, ALU.mult))
        mark("lam", dve.tensor_scalar(gain_dn[:, :], v("dn_g"), 1.0 - LAM_INIT, None, ALU.mult))
        settle(dve, "lam")
        mark("rot_ready", dve.tensor_scalar(rot_q[:, :], ca("rot"), gain_dq[:, :], None, ALU.mult))
        mark("rot_ready", dve.tensor_scalar(rot_k[:, :], ca("rot"), v("dk_g"), None, ALU.mult))

    def diff_rotate(dve, i):
        h, key = i // 2, "qk"[i % 2]
        x, gains = (dk[:, h, NCTX:], v("dk_g")) if i % 2 else (dq[:, h, :], gain_dq[:, :])
        b = full(dve, ("rot_" + key, h))
        if i:
            dve.wait_ge(S("diff_rotated"), i)
        mark("rope_step", dve.tensor_tensor(t1[0][:, 0:N], ps[:, b, :], ca("sin"), ALU.mult))
        mark("rope_step", dve.scalar_tensor_tensor(out=t1[1][:, 0:N], in0=x, scalar=gains, in1=ca("cos"), op0=ALU.mult, op1=ALU.mult))
        settle(dve, "rope_step")
        dve.tensor_tensor(t1[1][:, 0:N], t1[1][:, 0:N], t1[0][:, 0:N], ALU.add).then_inc(bank_empty(b), 1)
        read(dve, ("rot_" + key, h))
        b = full(dve, ("rs_" + key, h))
        dve.tensor_tensor(x, t1[1][:, 0:N], ps[:, b, :], ALU.mult).then_inc(S("diff_rotated"), 1)

    def diff_tensor(pe):
        for h in range(HEADS):
            claim(pe, 6 + h % 2, ("rs_kc", h))
            for t in range(NTC):
                mm = spread(pe, 6 + h % 2, "nk", 2 * (h * NTA + t), t)
            mm.then_inc(bank_full(6 + h % 2), 1)

        def scores(u):
            h, qt = pairs[u]
            pe.wait_ge(S("dqc_zero"), 2)
            pe.wait_ge(S("dq_ready"), 2 * (h + 1))
            read(pe, ("rs_kc", h))
            for comp in range(2):
                b = 2 * comp
                if u == 0:
                    pe.wait_ge(*bank_freed[b + 1])
                claim(pe, b, (f"s{comp}", u))
                for a, z in ((0, 512), (512, NALL)):
                    mm = pe.matmul(flat[:, b * 512 + a:b * 512 + z], dqc[:, h, comp, qt * P:(qt + 1) * P], dk[:, h, a:z], start=True, stop=True)
                mm.then_inc(bank_full(b), 1)

        def turn(u):
            pe.wait_ge(S("prob_ready"), u + 1)
            claim(pe, 4 + u % 2, ("tA", u), (S("probT_a"), u + 1))
            for t in range(4):
                mm = pe.transpose(ps[:, 4 + u % 2, t * P:(t + 1) * P], prob[u % 2][:, 0, t * P:(t + 1) * P], ident)
            mm.then_inc(bank_full(4 + u % 2), 1)
            claim(pe, 6 + u % 2, ("tB", u), (S("od_ready"), u + 1))
            for t in range(4, NTA):
                mm = pe.transpose(ps[:, 6 + u % 2, (t - 4) * P:(t - 3) * P], prob[u % 2][:, 0, t * P:(t + 1) * P], ident)
            mm.then_inc(bank_full(6 + u % 2), 1)

        def mix_values(u):
            h, qt = pairs[u]
            also(6 + u % 2, ("pv", u))
            pe.wait_ge(S("probT_a"), u + 1)
            pe.wait_ge(S("probT_b"), u + 1)
            for t in range(NTA):
                mm = pe.matmul(ps[:, 6 + u % 2, 256:256 + P], dvt[:, t, h * DV:(h + 1) * DV], probT[u % 2][:, t, :],
                               start=(t == 0), stop=(t == NTA - 1))
            mm.then_inc(bank_full(6 + u % 2), 1)

        scores(0)
        for u in range(len(pairs)):
            if u + 1 < len(pairs):
                scores(u + 1)
            turn(u)
            if u:
                mix_values(u - 1)
        mix_values(len(pairs) - 1)
        bank_freed[1], bank_freed[3] = bank_freed[0], bank_freed[2]
        head_norm_starts("no")
        for h in range(2):
            head_sum(pe, "no", h, 4 + h)

    def diff_scalar(act, meanwhile):
        act.wait_ge(S("lam"), 4)
        act.activation(lam[:, 2:4], lam[:, 0:2], ACT.Exp).then_inc(S("lam_exp"), 1)
        act.wait_ge(S("diff_rotated"), 2 * HEADS)
        full(act, ("c", len(chunks_a) - 1))
        for h in range(HEADS):
            for z in range(2):
                rows = slice(64 * z, 64 * z + 64)
                act.activation(dqc[rows, h, z, :], dq[rows, h, :], ACT.Copy).then_inc(S("dq_ready"), 1)

        def exps(u):
            if u >= 2:
                full(act, ("tB", u - 2))
            for comp in range(2):
                b = held[(f"s{comp}", u)][0]
                act.wait_ge(S("neg_max"), 2 * u + comp + 1)
                o = 1024 * comp
                act.activation(prob[u % 2][:, comp, :], flat[:, o:o + NALL], ACT.Exp, bias=neg_max[u % 2][:, comp:comp + 1],
                               accum_out=total[u % 2][:, comp:comp + 1]).then_inc(bank_empty(b), 1)

        exps(0)
        for u in range(len(pairs)):
            if u + 1 < len(pairs):
                exps(u + 1)
            b = full(act, ("tA", u))
            if u >= 2:
                full(act, ("pv", u - 2))
            act.activation(probT[u % 2][:, 0:4, :], ps[:, b, :].rearrange("p (t q) -> p t q", t=4), ACT.Copy).then_inc(S("probT_a"), 1)
        meanwhile()
        head_norm_scalar(act, "no", od, 4, lambda e, h: e.wait_ge(S("od_ready"), NT * (h + 1)), "t1")

    def diff_vector(dve):
        dve.wait_ge(S("diff_rotated"), 2 * HEADS)
        mark("lam", dve.tensor_tensor(t1[0][:, 0:P], v("lam_q"), v("lam_k"), ALU.mult))
        settle(dve, "lam")
        mark("lam", dve.tensor_reduce(lam[:, 0:2], t1[0][:, 0:P].rearrange("p (z d) -> p z d", z=2), AX, ALU.add))
        dve.wait_ge(S("lam_exp"), 1)
        mark("lam", dve.scalar_tensor_tensor(out=lam[:, 4:5], in0=lam[:, 3:4], scalar=-LAM_INIT, in1=lam[:, 2:3],
                                             op0=ALU.add, op1=ALU.subtract))
        settle(dve, "lam")
        for h in range(HEADS):
            b = full(dve, ("rs_kc", h))
            dve.scalar_tensor_tensor(out=dk[:, h, 0:NCTX], in0=dk[:, h, 0:NCTX], scalar=v("dk_g"), in1=ps[:, b, 0:NCTX],
                                     op0=ALU.mult, op1=ALU.mult).then_inc(bank_empty(b), 1)

        def maxima(u):
            for comp in range(2):
                full(dve, (f"s{comp}", u))
                o = 1024 * comp
                dve.tensor_reduce(neg_max[u % 2][:, comp:comp + 1], flat[:, o:o + NALL], AX, ALU.max, negate=True)\
                   .then_inc(S("neg_max"), 1)

        def difference(u):
            read(dve, ("s0", u))
            read(dve, ("s1", u))
            i, p = inv[u % 2], prob[u % 2]
            mark("diff_step", dve.reciprocal(i[:, 0:2], total[u % 2][:, :]))
            settle(dve, "diff_step")
            mark("diff_step", dve.tensor_tensor(i[:, 2:3], i[:, 1:2], lam[:, 4:5], ALU.mult))
            settle(dve, "diff_step")
            mark("diff_step", dve.tensor_scalar(p[:, 1, :], p[:, 1, :], i[:, 2:3], None, ALU.mult))
            settle(dve, "diff_step")
            dve.scalar_tensor_tensor(out=p[:, 0, :], in0=p[:, 0, :], scalar=i[:, 0:1], in1=p[:, 1, :], op0=ALU.mult, op1=ALU.add)\
               .then_inc(S("prob_ready"), 1)

        def outputs(u):
            h, qt = pairs[u]
            b = full(dve, ("pv", u))
            dve.tensor_copy(od[:, h, qt * P:(qt + 1) * P], ps[:, b, 256:256 + P]).then_inc(S("od_ready"), 1)

        maxima(0)
        for u in range(len(pairs)):
            difference(u)
            if u + 1 < len(pairs):
                maxima(u + 1)
            if u >= 2:
                full(dve, ("pv", u - 2))
            b = full(dve, ("tB", u))
            dve.tensor_copy(probT[u % 2][:, 4:NTA, :], ps[:, b, 0:2 * P].rearrange("p (t q) -> p t q", t=2)).then_inc(S("probT_b"), 1)
            if u:
                outputs(u - 1)
        outputs(len(pairs) - 1)
        head_norm_vector(dve, "no", od, 4, gain_dn[:, :], None)

    directions = [(d, pc) for d in range(2) for pc in range(2)]
    u_tiles = ([0, 1, 2, 3, 4], [1, 0, 5, 4, 3])
    GATE_SCALE = 1.0 / 16.0
    AT_QE = 3

    AT_MODS = (2, 4, 5, 6)

    def halves(t, s):
        return t.rearrange("p (n two s) -> p n two s", two=2, s=s)

    mods_of_gate = []

    def gla_tensor(pe):
        def level(li):
            q, k = (lq[li % 2], lk[li % 2]) if li else (gqx[:, :, :].rearrange("p c n -> p (c n)"), gkx[:, :, :].rearrange("p c n -> p (c n)"))
            for b in range(4):
                at_bank = b + 4 * (li % 2)
                claim(pe, at_bank, ("level", li, b))
                rows = slice(64 * (b % 2), 64 * (b % 2) + 64)
                for j in range(4):
                    at = (j % 2) * N + (2 * (b // 2) + j // 2) * P
                    mm = pe.matmul(ps[:, at_bank, j * P:(j + 1) * P], k[rows, at:at + P], q[rows, at:at + P], start=True, stop=True)
                mm.then_inc(bank_full(at_bank), 1)

        firsts["mix1_diff"] = len(slot_of)
        for pair in range(4):
            new_slot(half_slots(pair, 1))
            if pair % 2:
                mods_of_gate.append(modulation_slots(4))
        for i, (z, pc) in enumerate(directions):
            up = v("gate_up", z * 256 + pc * P, z * 256 + pc * P + P)[0:32, :]
            claim(pe, 2 * (i % 2), ("gx", i))
            pe.matmul(ps[:, 2 * (i % 2), :], up, dn[:, NCTX:], start=True, stop=True).then_inc(bank_full(2 * (i % 2)), 1)
            claim(pe, 2 * (i % 2) + 1, ("gc", i))
            pe.matmul(ps[:, 2 * (i % 2) + 1, 0:NCTX], up, dn[:, 0:NCTX], start=True, stop=True).then_inc(bank_full(2 * (i % 2) + 1), 1)
            if i < 2:
                head_spread(pe, "no", i, 6 + i)
                head_sum(pe, "no", i + 2, 4 + i)
            if i == 1:
                for h in range(2, HEADS):
                    head_spread(pe, "no", h, 6 + h % 2)
        half_mixed_tensor(pe, "mix1_diff", 1, firsts["mix1_diff"], 4, "no")
        level(0)
        for i, (d, pc) in enumerate(directions):
            pe.wait_ge(S("kd_ready"), 2 * (i + 1))
            claim(pe, 4, ("kA", i))
            for t in range(4):
                mm = pe.transpose(ps[:, 4, t * P:(t + 1) * P], t1[i % 2][:, t * P:(t + 1) * P], ident)
            mm.then_inc(bank_full(4), 1)
            claim(pe, 5, ("kB", i))
            for t in range(4, NTA):
                mm = pe.transpose(ps[:, 5, (t - 4) * P:(t - 3) * P], t1[i % 2][:, t * P:(t + 1) * P], ident)
            mm.then_inc(bank_full(5), 1)
            read(pe, ("kA", i))
            read(pe, ("kB", i))
            for j in range(0, 5, 2):
                b = (6, 7, 0)[j // 2]
                claim(pe, b, ("u", i, j))
                for o, t in enumerate(u_tiles[d][j:j + 2]):
                    mm = pe.matmul(ps[:, b, o * 256:(o + 1) * 256], kdT[:, d, t, pc * P:(pc + 1) * P],
                                   vt[:, t, pc * 256:(pc + 1) * 256], start=True, stop=True)
                mm.then_inc(bank_full(b), 1)
        for li in range(1, len(LEVELS) + 1):
            pe.wait_ge(S("lq_ready"), li)
            pe.wait_ge(S("lk_ready"), li)
            level(li)
        pe.wait_ge(S("qe_ready"), 2)
        read(pe, ("u", len(directions) - 1, 4))
        for b in range(4):
            read(pe, ("level", len(LEVELS), b))
        head_norm_starts("ng", HEADS)
        for h in range(HEADS):
            claim(pe, 4 + h, ("og", h))
            rows, pc = slice(64 * (h % 2), 64 * (h % 2) + 64), h // 2
            for t in range(NT):
                out = ps[:, 4 + h, t * P:(t + 1) * P]
                pe.matmul(out, vt[:, NTC + t, h * DV:(h + 1) * DV], attnT[:, t, h, :], start=True, stop=False)
                for d, at in ((0, t), (1, NT - 1 - t)):
                    mm = pe.matmul(out, states[rows, d, pc, at, :], qe[rows, d, pc * N + t * P:pc * N + (t + 1) * P],
                                   start=False, stop=(d == 1))
            mm.then_inc(bank_full(4 + h), 1)
            if h >= 2:
                head_spread(pe, "ng", h - 2, 2 + h % 2)
            if h:
                head_sum(pe, "ng", h - 1, (h - 1) % 2)
        head_sum(pe, "ng", HEADS - 1, (HEADS - 1) % 2)
        for h in (HEADS - 2, HEADS - 1):
            head_spread(pe, "ng", h, 2 + h % 2)
        mods_of_gate.append(modulation_slots(len(mod_todo) - KD))

    def gla_scalar(act):
        for i in range(len(directions)):
            for key, cols in (("gx", slice(NCTX, NALL)), ("gc", slice(0, NCTX))):
                b = full(act, (key, i))
                act.activation(gate[i][:, cols], ps[:, b, 0:cols.stop - cols.start], ACT.Identity, bias=v("gate_b", i, i + 1))\
                   .then_inc(bank_empty(b), 1)
        for i in range(len(directions)):
            read(act, ("gx", i))
            read(act, ("gc", i))
            mark("gate_step", act.activation(soft[i][:, :], gate[i][:, :], ACT.Abs))
        settle(act, "gate_step")
        for i in range(len(directions)):
            mark("gate_step", act.activation(soft[i][:, :], soft[i][:, :], ACT.Exp, scale=-1.0))
        settle(act, "gate_step")
        split_slots(act, firsts["mix1_diff"] + 2)
        for i in range(len(directions)):
            act.activation(soft[i][:, :], soft[i][:, :], ACT.Ln, bias=1.0).then_inc(S("softplus_ready"), 1)
        split_slots(act, firsts["mix1_diff"] + 3)

        def transposed(i):
            d, pc = directions[i]
            b = full(act, ("kA", i))
            act.activation(kdT[:, d, 0:4, pc * P:(pc + 1) * P], ps[:, b, :].rearrange("p (t k) -> p t k", t=4), ACT.Copy)\
               .then_inc(bank_empty(b), 1)

        def level_decay(li):
            act.wait_ge(S("level_sums"), 4 * li)
            for t, done in ((lk[li % 2], "lk_decay"), (lq[li % 2], "lq_decay")):
                act.activation(t[:, :], t[:, :], ACT.Exp, scale=GATE_SCALE).then_inc(S(done), 1)

        for i, (d, pc) in enumerate(directions):
            act.wait_ge(S("to_edge"), 2 * (i + 1))
            act.activation(t1[i % 2][:, :], t1[i % 2][:, :], ACT.Exp, scale=GATE_SCALE).then_inc(S("edge_decay"), 1)
            edge = slice(P - 1, None, P) if d == 0 else slice(0, None, P)
            act.activation(decay[:, d, pc, 0:NTC], cumc[:, d, pc * NCTX:(pc + 1) * NCTX][:, edge], ACT.Exp, scale=GATE_SCALE)\
               .then_inc(S("decay_ready"), 1)
            act.activation(decay[:, d, pc, NTC:], cumx[:, d, pc * N:(pc + 1) * N][:, edge], ACT.Exp, scale=GATE_SCALE)\
               .then_inc(S("decay_ready"), 1)
            if i:
                transposed(i - 1)
        level_decay(1)
        transposed(len(directions) - 1)
        for li in range(2, len(LEVELS) + 1):
            level_decay(li)
            if li == AT_QE:
                for d in range(2):
                    act.activation(qe[:, d, :], cumx[:, d, :], ACT.Exp, scale=GATE_SCALE).then_inc(S("q_decay"), 1)
        def output(e, h):
            b = full(e, ("og", h))
            e.activation(og[:, h, :], ps[:, b, :], ACT.Copy).then_inc(bank_empty(b), 1)
            read(e, ("og", h))

        head_norm_scalar(act, "ng", og, 0, output, "gated", lambda: split_slots(act, firsts["mix1"]))

    def mix_gate(m):
        return mod[:, 16 + m, 0:1]

    def gla_vector(dve):
        carry = ca("carry")
        modulation_biases(dve, "w_mod")
        modulations(dve, mods_of_gate[0])
        for m in range(2):
            mixed_chunk(dve, "mix1_diff", mix_gate, m)
        modulations(dve, mods_of_gate[1][:2])
        late_mods = mods_of_gate[1][2:] + mods_of_gate[2]
        for i, (d, pc) in enumerate(directions):
            dve.wait_ge(S("softplus_ready"), i + 1)
            mark("gate", dve.scalar_tensor_tensor(out=gate[i][:, :], in0=gate[i][:, :], scalar=0.0, in1=soft[i][:, :],
                                                  op0=ALU.min, op1=ALU.subtract))
            settle(dve, "gate")
            gx, gc = gate[i][:, NCTX:], gate[i][:, 0:NCTX]
            ox, oc = cumx[:, d, pc * N:(pc + 1) * N], cumc[:, d, pc * NCTX:(pc + 1) * NCTX]
            if d:
                gx, gc, ox, oc = gx[:, ::-1], gc[:, ::-1], ox[:, ::-1], oc[:, ::-1]
            mark("gate", dve.tensor_tensor_scan(oc, carry[:, 0:NCTX], gc, 0.0, ALU.mult, ALU.add))
            mark("cum_ready", dve.tensor_tensor_scan(ox, carry, gx, 0.0, ALU.mult, ALU.add))
            mixed_chunk(dve, "mix1_diff", mix_gate, 2 + i)
        settle(dve, "gate")
        settle(dve, "cum_ready")

        def sums_to_edge(i):
            d, pc = directions[i]
            if i >= 2:
                full(dve, ("kB", i - 2))
            for src, o, tiles in ((cumc, 0, NTC), (cumx, NCTX, NT)):
                w = tiles * P
                cum = src[:, d, pc * w:(pc + 1) * w].rearrange("p (t n) -> p t n", n=P)
                edge = cum[:, :, P - 1:P] if d == 0 else cum[:, :, 0:1]
                dve.tensor_tensor(t1[i % 2][:, o:o + w].rearrange("p (t n) -> p t n", n=P), edge.broadcast_to([P, tiles, P]), cum,
                                  ALU.subtract).then_inc(S("to_edge"), 1)

        def decayed_keys(i):
            d, pc = directions[i]
            dve.wait_ge(S("edge_decay"), i + 1)
            dve.tensor_tensor(t1[i % 2][:, 0:NCTX], t1[i % 2][:, 0:NCTX], gkc[:, pc, :], ALU.mult).then_inc(S("kd_ready"), 1)
            dve.tensor_tensor(t1[i % 2][:, NCTX:], t1[i % 2][:, NCTX:], gkx[:, pc, :], ALU.mult).then_inc(S("kd_ready"), 1)

        def transposed(i):
            d, pc = directions[i]
            b = full(dve, ("kB", i))
            dve.tensor_copy(kdT[:, d, 4:NTA, pc * P:(pc + 1) * P], ps[:, b, 0:2 * P].rearrange("p (t k) -> p t k", t=2))\
               .then_inc(bank_empty(b), 1)

        def states_of(i):
            d, pc = directions[i]
            dve.wait_ge(S("decay_ready"), 2 * (i + 1))
            for j in range(5):
                b = full(dve, ("u", i, j - j % 2))
                for half in range(2):
                    rows = slice(64 * half, 64 * half + 64)
                    o = (j % 2) * 256 + half * DV
                    to = states[rows, d, pc, NT if j == 0 else j - 1, :]
                    if j == 0:
                        ins = dve.tensor_copy(to, ps[rows, b, o:o + DV])
                    else:
                        ins = dve.scalar_tensor_tensor(out=to, in0=states[rows, d, pc, NT if j == 1 else j - 2, :],
                                                       scalar=decay[rows, d, pc, u_tiles[d][j]:u_tiles[d][j] + 1],
                                                       in1=ps[rows, b, o:o + DV], op0=ALU.mult, op1=ALU.add)
                    if half and (j % 2 or j == 4):
                        ins.then_inc(bank_empty(b), 1)
                        dve.wait_ge(*held[("u", i, j - j % 2)][2])
                    else:
                        mark("state_step", ins)
                settle(dve, "state_step")

        q = gqx[:, :, :].rearrange("p c n -> p (c n)")

        def attention(li):
            mask = ca("levels", li * P, (li + 1) * P).unsqueeze(1).unsqueeze(1).broadcast_to([P, 2, 2, P])
            for b in range(4):
                if li:
                    read(dve, ("level", li - 1, b))
                at_bank = full(dve, ("level", li, b))
                got = ps[:, at_bank, :].rearrange("p (t h i) -> p t h i", t=2, h=2)
                to = attnT[:, 2 * (b // 2):2 * (b // 2) + 2, b % 2::2, :]
                if li == 0:
                    ins = dve.tensor_tensor(to, got, mask, ALU.mult)
                else:
                    ins = dve.copy_predicated(to, mask.bitcast(U32), got)
                ins.then_inc(bank_empty(at_bank), 1)

        def sums(li):
            s = LEVELS[li - 1]
            if li >= 3:
                full(dve, ("level", li - 2, 3))
            fw, bw = halves(cumx[:, 0, :], s), halves(cumx[:, 1, :], s)
            to_q, to_k = halves(lq[li % 2][:, :], s), halves(lk[li % 2][:, :], s)
            shape = [P, 2 * N // (2 * s), s]
            mid_f = fw[:, :, 0, s - 1:s].broadcast_to(shape)
            mid_b = bw[:, :, 1, 0:1].broadcast_to(shape)
            mark("level_sums", dve.tensor_tensor(to_k[:, :, 0, :], mid_f, fw[:, :, 0, :], ALU.subtract))
            mark("level_sums", dve.tensor_tensor(to_k[:, :, 1, :], mid_b, bw[:, :, 1, :], ALU.subtract))
            mark("level_sums", dve.tensor_tensor(to_q[:, :, 0, :], bw[:, :, 0, :], mid_b, ALU.subtract))
            mark("level_sums", dve.tensor_tensor(to_q[:, :, 1, :], fw[:, :, 1, :], mid_f, ALU.subtract))

        for i in range(2):
            sums_to_edge(i)
            mixed_chunk(dve, "mix1_diff", mix_gate, 6 + i)
        decayed_keys(0)
        attention(0)
        for i in range(len(directions)):
            if i == len(directions) - 1:
                sums(1)
            if i:
                decayed_keys(i)
                states_of(i - 1)
            transposed(i)
            if i + 2 < len(directions):
                sums_to_edge(i + 2)
        sums(2)
        for li in range(1, len(LEVELS) + 1):
            dve.wait_ge(S("lq_decay"), li)
            dve.tensor_tensor(lq[li % 2][:, :], lq[li % 2][:, :], q, ALU.mult).then_inc(S("lq_ready"), 1)
            if li == 1:
                states_of(len(directions) - 1)
            elif li < len(LEVELS):
                sums(li + 1)
            if li > 1:
                attention(li - 1)
            if li in AT_MODS:
                modulations(dve, late_mods[AT_MODS.index(li):AT_MODS.index(li) + 1])
            if li == AT_QE:
                for d in range(2):
                    dve.wait_ge(S("q_decay"), d + 1)
                    dve.tensor_tensor(qe[:, d, :], qe[:, d, :], q, ALU.mult).then_inc(S("qe_ready"), 1)
        attention(len(LEVELS))
        head_norm_vector(dve, "ng", og, 0, v("gla_g"), rT, lambda h: modulations(dve, late_mods[len(AT_MODS) + h:len(AT_MODS) + h + 1]))

    def diff_gpsimd(pool):
        full(pool, ("c", len(chunks_a) - 1))
        for z in range(2):
            pool.memset(dqc[64 - 64 * z:128 - 64 * z, :, z, :], 0.0).then_inc(S("dqc_zero"), 1)

    def gla_gpsimd(pool):
        k = gkx[:, :, :].rearrange("p c n -> p (c n)")
        for li in range(1, len(LEVELS) + 1):
            pool.wait_ge(S("lk_decay"), li)
            pool.tensor_tensor(lk[li % 2][:, :], lk[li % 2][:, :], k, ALU.mult).then_inc(S("lk_ready"), 1)

    SUM_LAG = 2
    RESIDUALS = ("mix1_diff", "mix1", "ffn1", "ffn2", "mix2", "ffn3")

    def residual(key, chunks):
        return S("residual_ready"), RESIDUALS.index(key) * KD + chunks

    def half_slots(pair, half):
        return ("w_out", [((4 * half + k) * P, P, ((m * P, m * P + P, 0),)) for m in (2 * pair, 2 * pair + 1) for k in range(4)])

    def half_mixed_tensor(pe, key, half, g0, bank0, ready, sums_of=None):
        for m in range(KD):
            g, b = g0 + m // 2, bank0 + m % 4
            if m % 2 == 0:
                pe.wait_ge(*spent(slot_of[g]))
            claim(pe, b, (key, m), residual(key, m + 1))
            for k in range(4):
                if m == 0:
                    pe.wait_ge(*norm(ready, "ready", k + 1))
                mm = three_passes(pe, ps[:, b, :], g, 4 * (m % 2) + k, P, hh[:, 4 * half + k, :], hl[:, 4 * half + k, :], k == 0, k == 3)
            mm.then_inc(bank_full(b), 1)
            after[g] = (bank_full(b), bank_uses[b])
            if sums_of is not None and m >= SUM_LAG:
                norm_sum(pe, sums_of, m - SUM_LAG, KD, N, 4)

    def half_mixed_scalar(act, key, g0, squares_of):
        for pair in range(KD // 2):
            full(act, (key, 2 * pair + 1))
            split_slots(act, g0 + pair + 2)
            for m in (2 * pair, 2 * pair + 1):
                norm_square(act, squares_of, xT, m, N, after_chunk(key))

    def mixed_tensor(pe, key, name, rh, rl, parts, sums_of):
        for m in range(KD):
            g = take_slot(pe, full_columns(name, m * P))
            b = m % 4
            claim(pe, b, (key, m), residual(key, m + 1))
            for k in range(KD):
                if m == 0:
                    pe.wait_ge(*parts[k])
                mm = three_passes(pe, ps[:, b, :], g, k, P, rh[:, k, :], rl[:, k, :], k == 0, k == KD - 1)
            mm.then_inc(bank_full(b), 1)
            after[g] = (bank_full(b), bank_uses[b])
            if m >= SUM_LAG:
                norm_sum(pe, sums_of, m - SUM_LAG, KD, N, 4)

    def mixed_vector(dve, key, gate):
        for m in range(KD):
            mixed_chunk(dve, key, gate, m)

    def mixed_chunk(dve, key, gate, m):
        b = full(dve, (key, m))
        if key == "mix1":
            dve.wait_ge(*residual("mix1_diff", KD))
        dve.scalar_tensor_tensor(out=xT[:, m, :], in0=ps[:, b, :], scalar=gate(m), in1=xT[:, m, :], op0=ALU.mult, op1=ALU.add)\
           .then_inc(S("residual_ready"), 1)

    def mixed_scalar(act, key, g0, squares_of):
        for m in range(KD):
            full(act, (key, m))
            split_slots(act, g0 + m + 2)
            norm_square(act, squares_of, xT, m, N, after_chunk(key))

    ffns = {}
    HALF = KF // 2

    def ffn_tensor(pe, key, key_norm, name_in, name_out):
        f = ffns[key] = dict(i=len(ffns), n0=len(stream), g0=len(slot_of))
        for b in range(4):
            pe.wait_ge(*bank_freed[b])
        f["full0"], f["empty0"] = bank_uses[:4], bank_empties[:4]
        n0, g0 = f["n0"], f["g0"]

        def product(j, u, it):
            n, g, b = n0 + 2 * j + u, g0 + 2 * j + u, 2 * j + u
            pe.wait_ge(spent(n)[0], spent(n)[1] + it)
            pe.wait_ge(bank_empty(b), it + f["empty0"][b])
            for k in range(KD):
                mm = three_passes(pe, ps[:, b, :], g, k, P, hh[:, k, :], hl[:, k, :], k == 0, k == KD - 1)
            mm.then_inc(bank_full(b), 1)

        for u in range(2):
            pe.wait_ge(*spent(n0 + u))
            pe.wait_ge(bank_empty(u), f["empty0"][u])
        for k in range(KD):
            pe.wait_ge(*norm(key_norm, "ready", k + 1))
            for u in range(2):
                mm = three_passes(pe, ps[:, u, :], g0 + u, k, P, hh[:, k, :], hl[:, k, :], k == 0, k == KD - 1)
                if k == KD - 1:
                    mm.then_inc(bank_full(u), 1)
        for u in range(2):
            product(1, u, 0)
        with pe.Fori(1, HALF) as it:
            for j in range(2):
                for u in range(2):
                    product(j, u, it)
        for i in range(KF):
            stream.append(full_columns(name_in, i * P))
            stream.append(full_columns(name_in, FFN + i * P))
            slot_of.extend((n0 + 2 * i, n0 + 2 * i + 1))
            after.extend((None, None))
        for b in range(4):
            bank_uses[b] += HALF
            bank_empties[b] += HALF
            bank_freed[b] = (bank_empty(b), bank_empties[b])
        f["after_in"] = [(bank_full(b), bank_uses[b]) for b in (2, 3)]
        after[-2], after[-1] = f["after_in"]

        f["n1"], f["g1"], f["slab0"] = len(stream), len(slot_of), marks.get("slab_done", 0)
        n1, g1 = f["n1"], f["g1"]
        act0 = KF * f["i"]

        def slab(k, it, act_at, first, last):
            n, g = n1 + k, g1 + k
            pe.wait_ge(spent(n)[0], spent(n)[1] + it)
            pe.wait_ge(S("act_ready"), it * RING + (act0 + k + 1))
            for m in range(KD):
                if first:
                    claim(pe, m, (key, m), residual(key, m + 1))
                mm = three_passes(pe, ps[:, m, :], g, m, P, act_hi[:, act_at], act_lo[:, act_at], first, last)
                if last:
                    mm.then_inc(bank_full(m), 1)
            if not last:
                mm.then_inc(S("slab_done"), 1)

        slab(0, 0, slice(0, N), True, False)
        with pe.Fori(0, (KF - 2) // RING) as it:
            for j in range(RING):
                slab(1 + j, it, bass.ds(it * (RING * N) + (1 + j) * N, N), False, False)
        slab(KF - 1, 0, slice((KF - 1) * N, KF * N), False, True)
        for k in range(KF):
            stream.append(weight_rows(name_out, k))
            slot_of.append(n1 + k)
            after.append((S("slab_done"), f["slab0"] + k + 1))
        after[-1] = (bank_full(KD - 1), bank_uses[KD - 1])
        f["mods"] = modulation_slots(KD // 2)
        marks["slab_done"] = f["slab0"] + KF - 1

    def ffn_scalar(act, key):
        f = ffns[key]
        n0, g0 = f["n0"], f["g0"]
        split_slots(act, g0 + 1)
        with act.Fori(0, HALF) as it:
            for j in range(2):
                for u in range(2):
                    n, g, b = n0 + 2 * (j + 1) + u, g0 + u, 2 * j + u
                    act.wait_ge(bank_full(b), it + (f["full0"][b] + 1))
                    act.wait_ge(landed(n)[0], landed(n)[1] + it * 16)
                    act.activation(w_hi[g % SPLIT][:, :], raw[n % RING][:, :], ACT.Copy).then_inc(S("w_hi_ready"), 1)
                    if u == 0:
                        act.activation(silu[j][:, :], ps[:, b, :], ACT.Silu).then_inc(bank_empty(b), 1)
                b = 2 * j + 1
                act.wait_ge(bank_empty(b), it + (f["empty0"][b] + 1))
                act.activation(act_hi[:, bass.ds(it * (2 * N) + j * N, N)], prod[j][:, :], ACT.Copy).then_inc(S("act_hi_ready"), 1)
        n1, g1 = f["n1"], f["g1"]
        with act.Fori(0, (KF - 2) // RING) as it:
            for j in range(RING):
                n, g = n1 + 2 + j, g1 + j
                act.wait_ge(S("slab_done"), it * RING + (f["slab0"] + j + 1))
                act.wait_ge(landed(n)[0], landed(n)[1] + it * 16)
                act.activation(w_hi[g % SPLIT][:, :], raw[n % RING][:, :], ACT.Copy).then_inc(S("w_hi_ready"), 1)
        next_split[0] = g1 + KF
        split_slots(act, g1 + KF)

    def split_low(pool, n, g, it=0):
        pool.wait_ge(S("w_hi_ready"), it * 4 + (g + 1))
        pool.tensor_tensor(w_lo[g % SPLIT][:, :], raw[n % RING][:, :], w_hi[g % SPLIT][:, :].bitcast(F32), ALU.subtract)\
            .then_inc(spent(n)[0], 1)

    def split_lows(pool, g0, g1):
        for g in range(g0, g1):
            split_low(pool, slot_of[g], g)

    def ffn_gpsimd(pool, key):
        f = ffns[key]
        with pool.Fori(0, HALF) as it:
            for j in range(2):
                for u in range(2):
                    split_low(pool, f["n0"] + 2 * j + u, f["g0"] + 2 * j + u, it)
        with pool.Fori(0, (KF - 2) // RING) as it:
            for j in range(RING):
                split_low(pool, f["n1"] + j, f["g1"] + j, it)
        split_lows(pool, f["g1"] + KF - 2, f["g1"] + KF)

    def ffn_vector(dve, key, gate):
        f = ffns[key]
        with dve.Fori(0, HALF) as it:
            for j in range(2):
                b = 2 * j
                dve.wait_ge(bank_empty(b), it + (f["empty0"][b] + 1))
                dve.wait_ge(bank_full(b + 1), it + (f["full0"][b + 1] + 1))
                dve.tensor_tensor(prod[j][:, :], silu[j][:, :], ps[:, b + 1, :], ALU.mult).then_inc(bank_empty(b + 1), 1)
                dve.wait_ge(S("act_hi_ready"), it * 2 + (KF * f["i"] + j + 1))
                at = bass.ds(it * (2 * N) + j * N, N)
                dve.tensor_tensor(act_lo[:, at], prod[j][:, :], act_hi[:, at].bitcast(F32), ALU.subtract).then_inc(S("act_ready"), 1)
        modulations(dve, f["mods"])
        if key == "ffn2":
            modulation_biases(dve, "last")
            half_gain(dve, "f2", 64)
        mixed_vector(dve, key, gate)

    IN2 = dict(qa=0, ka=512, va=576, qi=640, ki=1152, wi=1216, cq=1224, ckv=1608, kr=1864, ga=1896, gb=2920)
    IDX_SCALE, HEAD_SCALE, A_SCALE, B_SCALE = DH2 ** -0.5, H2 ** -0.5, DH2 ** -0.5, QK2 ** -0.5

    def in2(*cuts):
        return ("w_in_2", [(k * P, P, cuts) for k in range(KD)])

    chunks_2 = ([("ki", 0, in2((IN2["ki"], IN2["ki"] + 64, 0), (IN2["ki"], IN2["ki"] + 64, 64))),
                 ("wkr", 0, in2((IN2["wi"], IN2["wi"] + H2, 0), (IN2["kr"], IN2["kr"] + ROPE2, 64)))]
                + [("qi", i, in2((IN2["qi"] + i * P, IN2["qi"] + (i + 1) * P, 0))) for i in range(4)]
                + [("cq", i, in2((IN2["cq"] + i * P, IN2["cq"] + (i + 1) * P, 0))) for i in range(3)]
                + [("ckv", i, in2((IN2["ckv"] + i * P, IN2["ckv"] + (i + 1) * P, 0))) for i in range(2)]
                + [("kva", 0, in2((IN2["ka"], IN2["ka"] + P, 0)))]
                + [("qa", i, in2((IN2["qa"] + i * P, IN2["qa"] + (i + 1) * P, 0))) for i in range(4)])
    second = {}
    index_units = [(qt, h) for qt in range(1, NT) for h in range(H2)]
    AT_INDEX = 7
    AT_KVA = [name for name, _, _ in chunks_2].index("kva")

    def proj2_tensor(pe):
        second["g_proj"] = len(slot_of)
        for i, (name, h, spec) in enumerate(chunks_2):
            g = take_slot(pe, spec)
            b = i % 2
            claim(pe, b, (name, h), {"qa": (S("qa_ready"), 2 * h + 2), "kva": (S("ka_ready"), 2), "qi": (S("qi_ready"), 2 * h + 2),
                                       "ki": (S("ki_ready"), 1)}.get(name))
            for k in range(KD):
                if i == 0:
                    pe.wait_ge(*norm("nm", "ready", k + 1))
                mm = three_passes(pe, ps[:, b, :], g, k, P, hh[:, k, :], hl[:, k, :], k == 0, k == KD - 1)
            mm.then_inc(bank_full(b), 1)
            after[g] = (bank_full(b), bank_uses[b])
            if i == AT_INDEX - 1:
                claim(pe, 4, "wt")
                read(pe, ("wkr", 0))
                for t in range(NT):
                    mm = pe.transpose(ps[:, 4, t * H2:(t + 1) * H2], wkr[0:H2, t * P:(t + 1) * P], ident[0:H2, 0:H2])
                mm.then_inc(bank_full(4), 1)
            if 0 <= i - AT_INDEX < len(index_units) // 4:
                for j in range(4 * (i - AT_INDEX), 4 * (i - AT_INDEX) + 4):
                    index_tensor(pe, j)
        claim(pe, 3, "vat")
        pe.wait_ge(S("va_ready"), 1)
        for t in range(NT):
            mm = pe.transpose(ps[:, 3, t * DH2:(t + 1) * DH2], kva[64:128, t * P:(t + 1) * P], ident[64:128, 64:128])
        mm.then_inc(bank_full(3), 1)

    def qa_views(b, h, z):
        here, other = slice(64 * z, 64 * z + 64), slice(64 - 64 * z, 128 - 64 * z)
        return ps[here, b, :].rearrange("p (u q) -> p u q", q=QG), qa[here, :, 2 * h + z, :], qa[other, :, 2 * h + z, :]

    def qi_views(b, h, z):
        here, other = slice(64 * z, 64 * z + 64), slice(64 - 64 * z, 128 - 64 * z)
        return ps[here, b, :], qi[here, 2 * h + z, :], qi[other, 2 * h + z, :]

    def lower_parts(dve, name, h, views, scale):
        b = full(dve, (name, h))
        dve.wait_ge(S(name + "_hi"), 2 * h + 2)
        for z in range(2):
            src, hi, lo = views(b, h, z)
            dve.scalar_tensor_tensor(out=lo, in0=src, scalar=scale, in1=hi.bitcast(F32), op0=ALU.mult, op1=ALU.subtract)\
               .then_inc(S(name + "_ready"), 1)

    def proj2_vector(dve):
        b = full(dve, ("ki", 0))
        dve.wait_ge(S("ki_hi"), 1)
        dve.tensor_tensor(ki_lo[:, :], ps[:, b, :], ki_hi[:, :].bitcast(F32), ALU.subtract).then_inc(S("ki_ready"), 1)
        for h in range(4):
            lower_parts(dve, "qi", h, qi_views, 1.0)
        rope2_vector(dve)
        b = full(dve, "wt")
        dve.tensor_scalar(wt[:, :, :], ps[:, b, 0:NT * H2].rearrange("p (t h) -> p t h", t=NT), HEAD_SCALE, None, ALU.mult)\
           .then_inc(bank_empty(b), 1)
        read(dve, "wt")
        for j in range(len(index_units)):
            index_vector(dve, j)
            if j == 4 * (AT_KVA - AT_INDEX) + 1:
                b = full(dve, ("kva", 0))
                dve.wait_ge(S("va_ready"), 1)
                for z in range(2):
                    dve.tensor_tensor(ka_lo[64 * z:64 * z + 64, :], ps[0:64, b, :], ka_hi[0:64, :].bitcast(F32), ALU.subtract)\
                       .then_inc(S("ka_ready"), 1)
        index_end(dve)
        for h in range(4):
            lower_parts(dve, "qa", h, qa_views, A_SCALE)
            if h < EARLY_ROUNDS:
                topk_round(dve)

    def proj2_scalar(act):
        for i, (name, h, _) in enumerate(chunks_2):
            b = full(act, (name, h))
            split_slots(act, second["g_proj"] + i + 2)
            if name in ("qi", "qa"):
                for z in range(2):
                    src, hi, _ = (qi_views if name == "qi" else qa_views)(b, h, z)
                    act.activation(hi, src, ACT.Copy, scale=1.0 if name == "qi" else A_SCALE).then_inc(S(name + "_hi"), 1)
            elif name == "ki":
                act.activation(ki_hi[:, :], ps[:, b, :], ACT.Copy).then_inc(S("ki_hi"), 1)
            elif name == "kva":
                for z in range(2):
                    act.activation(ka_hi[64 * z:64 * z + 64, :], ps[0:64, b, :], ACT.Copy).then_inc(S("ka_hi"), 1)
                act.activation(kva[64:128, :], ps[64:128, b, :], ACT.Copy).then_inc(S("va_ready"), 1)
            else:
                to = {"wkr": wkr[:, :], "cq": cq[:, h % 3, :], "ckv": ckv[:, h % 2, :]}[name]
                act.activation(to, ps[:, b, :], ACT.Copy).then_inc(bank_empty(b), 1)
            if i == AT_INDEX - 1:
                rope2_scalar(act)
            if 0 <= i - AT_INDEX < len(index_units) // 4:
                for j in range(4 * (i - AT_INDEX), 4 * (i - AT_INDEX) + 4):
                    index_scalar(act, j)

    PI_A = 6.28125
    PI_B = math.floor((2 * math.pi - PI_A) * 2.0 ** 21) / 2.0 ** 21
    TWO_PI = (PI_A, PI_B, 2 * math.pi - PI_A - PI_B)
    ROUND = 1.5 * 2.0 ** 23
    rot_rows = slice(64, 96)

    def rope2_vector(dve):
        mark("rope2", dve.tensor_copy(posf[:, :], posi[:, :]))
        mark("rope2", dve.tensor_copy(qfrom[:, :], qposi[:, :]))
        settle(dve, "rope2")
        mark("rope2", dve.tensor_scalar(qfrom[:, :], qfrom[:, :], c("bucket_from"), None, ALU.add))
        ang, turns = sinr[rot_rows, :], t1[1][rot_rows, 0:N]
        for shift, to in ((0.25, cosr[rot_rows, :]), (0.0, sinr[rot_rows, :])):
            if shift:
                mark("rope2", dve.tensor_scalar(ang, posf[rot_rows, :], c("freq")[rot_rows, :], None, ALU.mult))
                settle(dve, "rope2")
            mark("rope2", dve.tensor_scalar(turns, ang, 1 / (2 * math.pi), shift, ALU.mult, ALU.add))
            settle(dve, "rope2")
            mark("rope2", dve.tensor_scalar(turns, turns, ROUND, None, ALU.add))
            settle(dve, "rope2")
            mark("rope2", dve.tensor_scalar(turns, turns, ROUND, None, ALU.subtract))
            settle(dve, "rope2")
            for i, part in enumerate(TWO_PI):
                mark("rope2", dve.scalar_tensor_tensor(out=to, in0=turns, scalar=-part, in1=ang if i == 0 else to,
                                                       op0=ALU.mult, op1=ALU.add))
                settle(dve, "rope2")
            if shift:
                mark("rope2", dve.tensor_scalar(to, to, math.pi / 2, None, ALU.add))
                settle(dve, "rope2")
            mark("rope2_angle", dve.tensor_scalar(to, to, 3.1415925, -3.1415925, ALU.min, ALU.max))

    def rope2_scalar(act):
        for i, to in enumerate((cosr, sinr)):
            act.wait_ge(S("rope2_angle"), i + 1)
            act.activation(to[rot_rows, :], to[rot_rows, :], ACT.Sin).then_inc(S("rope2_table"), 1)


    def index_tensor(pe, i):
        qt, h = index_units[i]
        b, keys = (2, 3, 6, 7)[i % 4], (qt + 1) * P
        claim(pe, b, ("dots", i))
        if i == 0:
            read(pe, ("ki", 0))
            read(pe, ("qi", 3))
        for k in (ki_hi, ki_lo):
            mm = pe.matmul(ps[:, b, 0:keys], qi[:, h, qt * P:(qt + 1) * P], k[:, 0:keys], start=k is ki_hi, stop=k is ki_lo)
        mm.then_inc(bank_full(b), 1)

    def index_scalar(act, i):
        keys = (index_units[i][0] + 1) * P
        if i >= 2:
            act.wait_ge(S("index_sum"), i - 1)
        b = full(act, ("dots", i))
        act.activation(sq[i % 2][:, 0:keys], ps[:, b, 0:keys], ACT.Relu, scale=IDX_SCALE).then_inc(bank_empty(b), 1)

    def index_vector(dve, i):
        qt, h = index_units[i]
        keys, to = (qt + 1) * P, score[qt - 1]
        read(dve, ("dots", i))
        if h == 0:
            ins = dve.tensor_scalar(to[:, :], sq[i % 2][:, 0:keys], wt[:, qt, h:h + 1], None, ALU.mult)
        else:
            dve.wait_ge(S("index_sum"), i)
            ins = dve.scalar_tensor_tensor(out=to[:, :], in0=sq[i % 2][:, 0:keys], scalar=wt[:, qt, h:h + 1], in1=to[:, :],
                                           op0=ALU.mult, op1=ALU.add)
        ins.then_inc(S("index_sum"), 1)

    def index_end(dve):
        dve.wait_ge(S("index_sum"), len(index_units))
        for qt in range(1, NT):
            mark("topk", dve.memset(score[qt - 1][0:64, qt * P + 64:(qt + 1) * P], NEG))
        settle(dve, "topk")

    EARLY_ROUNDS = 3

    def topk_round(dve):
        for qt in range(1, NT):
            mark("topk", dve.max(best[:, qt - 1, :], score[qt - 1][:, :]))
        settle(dve, "topk")
        for qt in range(1, NT):
            mark("topk", dve.match_replace(score[qt - 1][:, :], best[:, qt - 1, :], score[qt - 1][:, :], TAKEN))
        settle(dve, "topk")

    def topk_end(dve):
        mark("hide_ready", dve.memset(hide[0][:, :], 0.0))
        settle(dve, "hide_ready")
        mark("hide_ready", dve.memset(hide[0][0:64, 64:P], HIDE))
        for qt in range(1, NT):
            mark("hide_ready", dve.tensor_scalar(hide[qt][:, :], score[qt - 1][:, :], TAKEN, HIDE, ALU.is_gt, ALU.mult))

    def uq_tiles():
        tiles = [(k * P, P, ((h * QK2, (h + 1) * QK2, 0),)) for h in range(H2) for k in range(3)]
        return [("w_uq_2", tiles[i:i + 8]) for i in range(0, 24, 8)]

    def pair_tiles(name):
        return (name, [(k * P, P, ((i * P, (i + 1) * P, 0),)) for i in range(4) for k in range(2)])

    def lora_tensor(pe):
        norm_tensor(pe, "ncq", 3, N, 4, 4)
        norm_tensor(pe, "nckv", 2, N, 5, 5)
        second["g_uq"] = len(slot_of)
        turn = c("rot2")[rot_rows, :]

        def rotate_q(h):
            read(pe, ("uq", h))
            claim(pe, 2 + h % 2, ("rot2", h))
            pe.matmul(ps[rot_rows, 2 + h % 2, :], turn, qb[rot_rows, h, :], start=True, stop=True).then_inc(bank_full(2 + h % 2), 1)

        specs = uq_tiles()
        for h in range(H2):
            claim(pe, h % 2, ("uq", h))
            for k in range(3):
                if h == 0:
                    pe.wait_ge(*norm("ncq", "ready", k + 1))
                i = 3 * h + k
                if i % 8 == 0:
                    g = take_slot(pe, specs[i // 8])
                mm = three_passes(pe, ps[0:QK2, h % 2, :], g, i % 8, QK2, cqh[:, k, :], cql[:, k, :], k == 0, k == 2)
                if i % 8 == 7 and k < 2:
                    mark("slab_done", mm)
                    after[g] = (S("slab_done"), marks["slab_done"])
            mm.then_inc(bank_full(h % 2), 1)
            if 3 * h + 2 == 23:
                after[g] = (bank_full(h % 2), bank_uses[h % 2])
            if h:
                rotate_q(h - 1)
        rotate_q(H2 - 1)
        for name, key in (("w_uk_2", "uk"), ("w_uv_2", "uv")):
            g = take_slot(pe, pair_tiles(name))
            for i in range(4):
                claim(pe, i % 2, (key, i))
                for k in range(2):
                    if key == "uk" and i == 0:
                        pe.wait_ge(*norm("nckv", "ready", k + 1))
                    mm = three_passes(pe, ps[:, i % 2, :], g, 2 * i + k, P, ckvh[:, k, :], ckvl[:, k, :], k == 0, k == 1)
                mm.then_inc(bank_full(i % 2), 1)
                after[g] = (bank_full(i % 2), bank_uses[i % 2])
                if key == "uk" and i == 0:
                    claim(pe, 2, "rot2_k")
                    pe.matmul(ps[rot_rows, 2, :], turn, wkr[rot_rows, :], start=True, stop=True).then_inc(bank_full(2), 1)
                if key == "uv" and i:
                    to_tokens2(pe, i - 1)
        to_tokens2(pe, 3)

    def to_tokens2(pe, i):
        read(pe, ("uv", i))
        claim(pe, 4 + i % 2, ("vb", i))
        for t in range(NT):
            mm = pe.transpose(ps[:, 4 + i % 2, t * P:(t + 1) * P], sq[i % 2][:, t * P:(t + 1) * P], ident)
        mm.then_inc(bank_full(4 + i % 2), 1)

    def lora_scalar(act):
        act.wait_ge(S("index_sum"), len(index_units))
        norm_scalar(act, "ncq", cq, 3, N, Q_LORA, cqh, None, lambda e, k: read(e, ("cq", k)))
        norm_scalar(act, "nckv", ckv, 2, N, KV_LORA, ckvh, None, lambda e, k: read(e, ("ckv", k)))
        g0 = second["g_uq"]
        for h in range(H2):
            b = full(act, ("uq", h))
            act.activation(qb[:, h, :], ps[0:QK2, b, :], ACT.Copy, scale=B_SCALE).then_inc(bank_empty(b), 1)
            if 3 * h + 2 >= 7:
                split_slots(act, g0 + 2 + (3 * h + 2 - 7) // 8)
        for i in range(4):
            b = full(act, ("uk", i))
            act.activation(kb[0:64, 2 * i, :], ps[0:64, b, :], ACT.Copy)
            act.activation(kb[0:64, 2 * i + 1, :], ps[64:128, b, :], ACT.Copy).then_inc(bank_empty(b), 1)
        for i in range(4):
            if i >= 2:
                full(act, ("vb", i - 2))
            b = full(act, ("uv", i))
            act.activation(sq[i % 2][:, 0:N], ps[:, b, :], ACT.Copy).then_inc(bank_empty(b), 1)
        split_slots(act, second["g_gated_b"] + 1)

    def lora_vector(dve):
        b = full(dve, "vat")
        dve.tensor_copy(vat[:, :, :], ps[:, b, 0:NT * DH2].rearrange("p (t d) -> p t d", t=NT)).then_inc(bank_empty(b), 1)
        norm_vector(dve, "ncq", cq, 3, N, lambda k: v("g_cq", k, k + 1), cqh, cql, None)
        norm_vector(dve, "nckv", ckv, 2, N, lambda k: v("g_ckv", k, k + 1), ckvh, ckvl, None)
        dve.wait_ge(S("rope2_table"), 2)
        dve.wait_ge(*norm("nckv", "ready", 2))

        last_rotated = []

        def rotate(src, dst, key):
            b = full(dve, key)
            if last_rotated:
                read(dve, last_rotated.pop())
            last_rotated.append(key)
            mark("rope2_step", dve.tensor_tensor(t1[0][rot_rows, 0:N], ps[rot_rows, b, :], sinr[rot_rows, :], ALU.mult))
            mark("rope2_step", dve.tensor_tensor(t1[1][rot_rows, 0:N], src, cosr[rot_rows, :], ALU.mult))
            settle(dve, "rope2_step")
            dve.tensor_tensor(dst, t1[0][rot_rows, 0:N], t1[1][rot_rows, 0:N], ALU.add).then_inc(bank_empty(b), 1)

        for h in range(H2):
            rotate(qb[rot_rows, h, :], qb[rot_rows, h, :], ("rot2", h))
        rotate(wkr[rot_rows, :], kb[rot_rows, 0, :], "rot2_k")
        read(dve, "rot2_k")
        for h in range(1, H2):
            mark("kb_ready", dve.tensor_copy(kb[rot_rows, h, :], kb[rot_rows, 0, :]))
        for i in range(4):
            b = full(dve, ("vb", i))
            dve.tensor_copy(vbt[:, :, i * P:(i + 1) * P], ps[:, b, :].rearrange("p (t d) -> p t d", t=NT)).then_inc(bank_empty(b), 1)

    score_banks = (0, 1, 6)
    mla_units = [(h, qt) for h in range(H2) for qt in range(NT)]

    def mla_tensor(pe):
        read(pe, ("uk", 3))
        pe.wait_ge(S("kb_ready"), H2 - 1)
        read(pe, ("rot2", H2 - 1))
        read(pe, ("vb", 3))

        def scores(u):
            h, qt = mla_units[u]
            b = score_banks[u % 3]
            claim(pe, b, ("ms", u))
            pe.matmul(ps[:, b, 0:(qt + 1) * P], qb[:, h, qt * P:(qt + 1) * P], kb[:, h, 0:(qt + 1) * P], start=True, stop=True)\
              .then_inc(bank_full(b), 1)

        def turn(u):
            h, qt = mla_units[u]
            pe.wait_ge(S("mp_ready"), u + 1)
            b = 2 + u % 2
            claim(pe, b, ("mt", u))
            for t in range(qt + 1):
                mm = pe.transpose(ps[:, b, t * P:(t + 1) * P], mp[u % 2][:, t * P:(t + 1) * P], ident)
            mm.then_inc(bank_full(b), 1)

        def mix_values(u):
            h, qt = mla_units[u]
            read(pe, ("mt", u))
            ob = 4 + h // 2 % 2
            if h % 2 == 0 and qt == 0:
                claim(pe, ob, ("ob", h // 2), (S("ob_ready"), h // 2 + 1))
            rows = slice(64 * (h % 2), 64 * (h % 2) + 64)
            for t in range(qt + 1):
                mm = pe.matmul(ps[rows, ob, qt * P:(qt + 1) * P], vbt[:, t, h * DH2:(h + 1) * DH2], mpT[u % 2][:, t, :],
                               start=(t == 0), stop=(t == qt))
            if h % 2 and qt == NT - 1:
                mm.then_inc(bank_full(ob), 1)
            else:
                mm.then_inc(S("mla_pv"), 1)

        scores(0)
        scores(1)
        for u in range(len(mla_units)):
            if u + 2 < len(mla_units):
                scores(u + 2)
            turn(u)
            if u:
                mix_values(u - 1)
        mix_values(len(mla_units) - 1)

    def pv_done(u):
        return sum(not (h % 2 and qt == NT - 1) for h, qt in mla_units[:u + 1])

    def mla_scalar(act):
        def exps(u):
            h, qt = mla_units[u]
            keys = (qt + 1) * P
            if u >= 2:
                full(act, ("mt", u - 2))
            act.wait_ge(S("mla_max"), u + 1)
            b = held[("ms", u)][0]
            act.activation(mp[u % 2][:, 0:keys], ps[:, b, 0:keys], ACT.Exp, bias=sm["mla_max"][u % 2][:, :],
                           accum_out=sm["mla_sum"][u % 2][:, :]).then_inc(bank_empty(b), 1)

        def outputs(u):
            h, qt = mla_units[u]
            if h % 2 and qt == NT - 1:
                b = full(act, ("ob", h // 2))
                act.activation(obh[:, h // 2, :], ps[:, b, :], ACT.Copy).then_inc(S("ob_hi"), 1)

        exps(0)
        for u, (h, qt) in enumerate(mla_units):
            if u + 1 < len(mla_units):
                exps(u + 1)
            if u >= 2:
                ph, pqt = mla_units[u - 2]
                if ph % 2 and pqt == NT - 1:
                    full(act, ("ob", ph // 2))
                else:
                    act.wait_ge(S("mla_pv"), pv_done(u - 2))
            b = full(act, ("mt", u))
            act.activation(mpT[u % 2][:, 0:qt + 1, :], ps[:, b, 0:(qt + 1) * P].rearrange("p (t q) -> p t q", q=P), ACT.Copy)\
               .then_inc(bank_empty(b), 1)
            if u:
                outputs(u - 1)
        outputs(len(mla_units) - 1)

    def mla_vector(dve):
        def maxima(u):
            h, qt = mla_units[u]
            keys = (qt + 1) * P
            b = full(dve, ("ms", u))
            mark("mla_step", dve.memset(ps[0:64, b, keys - 64:keys], NEG))
            settle(dve, "mla_step")
            dve.tensor_reduce(sm["mla_max"][u % 2][:, :], ps[:, b, 0:keys], AX, ALU.max, negate=True).then_inc(S("mla_max"), 1)

        def outputs(u):
            h, qt = mla_units[u]
            if h % 2 and qt == NT - 1:
                b = full(dve, ("ob", h // 2))
                dve.wait_ge(S("ob_hi"), h // 2 + 1)
                dve.tensor_tensor(obl[:, h // 2, :], ps[:, b, :], obh[:, h // 2, :].bitcast(F32), ALU.subtract).then_inc(S("ob_ready"), 1)

        maxima(0)
        maxima(1)
        for u, (h, qt) in enumerate(mla_units):
            keys = (qt + 1) * P
            read(dve, ("ms", u))
            mark("mla_step", dve.reciprocal(sm["mla_inv"][u % 2][:, :], sm["mla_sum"][u % 2][:, :]))
            settle(dve, "mla_step")
            dve.tensor_scalar(mp[u % 2][:, 0:keys], mp[u % 2][:, 0:keys], sm["mla_inv"][u % 2][:, :], None, ALU.mult)\
               .then_inc(S("mp_ready"), 1)
            if u + 2 < len(mla_units):
                maxima(u + 2)
            if u:
                outputs(u - 1)
        outputs(len(mla_units) - 1)

    dsa_units = list(range(N // QG))

    def dsa_tensor(pe):
        pe.wait_ge(S("table_ready"), 4)
        pe.wait_ge(S("identb_ready"), 1)
        read(pe, ("qa", 3))
        read(pe, "vat")
        pe.wait_ge(S("hide_ready"), 2 + NT - 1)

        def scores(u):
            qt, b = u // 8, score_banks[u % 3]
            keys = (qt + 1) * P
            claim(pe, b, ("ds", u))
            out = ps[:, b, 0:keys]
            for k in (ka_hi, ka_lo):
                pe.matmul(out, qa[:, u, :, :].rearrange("p h q -> p (h q)"), k[:, 0:keys], start=k is ka_hi, stop=False)
            pe.matmul(out, identb[:, u % 8, :, :].rearrange("p h q -> p (h q)"), hide[qt][:, :], start=False, stop=False)
            for j in range(4):
                i = 4 * u + j
                pe.wait_ge(S("step_ready"), i + 1)
                pe.matmul(out, table_hi[:, j, :], step[i % NSTEP][:, 0:keys], start=False, stop=False)
                mm = pe.matmul(out, table_lo[:, j, :], step[i % NSTEP][:, 0:keys], start=False, stop=(j == 3))
            mm.then_inc(bank_full(b), 1)

        def turn(u):
            qt = u // 8
            pe.wait_ge(S("pp_ready"), u + 1)
            b = 2 + u % 2
            claim(pe, b, ("dt", u))
            for t in range(qt + 1):
                mm = pe.transpose(ps[:, b, t * P:(t + 1) * P], pp[u % 2][:, t * P:(t + 1) * P], ident)
            mm.then_inc(bank_full(b), 1)

        def mix_values(u):
            qt = u // 8
            read(pe, ("dt", u))
            ob = 4 + u // 4 % 2
            if u % 4 == 0:
                claim(pe, ob, ("oa", u // 4), (S("oa_ready"), 2 * (u // 4 + 1)))
            for t in range(qt + 1):
                mm = pe.matmul(ps[0:64, ob, (u % 4) * P:(u % 4 + 1) * P], vat[:, t, :], ppT[u % 2][:, t, :],
                               start=(t == 0), stop=(t == qt))
            mm.then_inc(bank_full(ob) if u % 4 == 3 else S("dsa_pv"), 1)

        scores(0)
        scores(1)
        for u in dsa_units:
            if u + 2 < len(dsa_units):
                scores(u + 2)
            turn(u)
            if u:
                mix_values(u - 1)
        mix_values(dsa_units[-1])

    def oa_views(i, half):
        src = ps[0:64, held[("oa", i)][0], :].rearrange("p (u c z q) -> p c z u q", u=4, c=4, z=2)[:, :, half, :, :]
        rows, cols = slice(64 * half, 64 * half + 64), slice(i * 4 * QG, (i + 1) * 4 * QG)
        return src, oah[rows, :, cols].rearrange("p c (u q) -> p c u q", u=4), oal[rows, :, cols].rearrange("p c (u q) -> p c u q", u=4)

    def table_scalar(act):
        act.activation(identb[:, :, :, :], ident.rearrange("p (u q) -> p u q", q=QG).unsqueeze(2).broadcast_to([P, P // QG, H2, QG]), ACT.Copy)\
           .then_inc(S("identb_ready"), 1)
        for j in range(4):
            act.wait_ge(S("table_full"), j + 1)
            act.activation(table_hi[:, j, :], table[:, j, :], ACT.Copy).then_inc(S("table_hi"), 1)

    def dsa_scalar(act):
        def exps(u):
            keys = (u // 8 + 1) * P
            if u >= 2:
                full(act, ("dt", u - 2))
            act.wait_ge(S("dsa_max"), u + 1)
            b = held[("ds", u)][0]
            act.activation(pp[u % 2][:, 0:keys], ps[:, b, 0:keys], ACT.Exp, bias=sm["dsa_max"][u % 2][:, :],
                           accum_out=sm["dsa_sum"][u % 2][:, :]).then_inc(bank_empty(b), 1)

        def outputs(u):
            if u % 4 == 3:
                full(act, ("oa", u // 4))
                for half in range(2):
                    src, hi, _ = oa_views(u // 4, half)
                    act.activation(hi, src, ACT.Copy).then_inc(S("oa_hi"), 1)

        exps(0)
        for u in dsa_units:
            qt = u // 8
            if u + 1 < len(dsa_units):
                exps(u + 1)
            if u >= 2:
                if (u - 2) % 4 == 3:
                    full(act, ("oa", (u - 2) // 4))
                else:
                    act.wait_ge(S("dsa_pv"), 3 * ((u - 2) // 4) + (u - 2) % 4 + 1)
            b = full(act, ("dt", u))
            act.activation(ppT[u % 2][:, 0:qt + 1, :], ps[:, b, 0:(qt + 1) * P].rearrange("p (t q) -> p t q", q=P), ACT.Copy)\
               .then_inc(bank_empty(b), 1)
            if u:
                outputs(u - 1)
        outputs(dsa_units[-1])

    def table_vector(dve):
        mark("table_step", dve.tensor_tensor(delta[:, :], v("bias_at"), v("bias_before"), ALU.subtract))
        settle(dve, "table_step")
        for j in range(4):
            dve.tensor_tensor(table[:, j, :].rearrange("p (h q) -> p h q", h=H2), delta[:, :].unsqueeze(2).broadcast_to([P, H2, QG]),
                              c("own_query", j * QG, (j + 1) * QG).unsqueeze(1).broadcast_to([P, H2, QG]), ALU.mult)\
               .then_inc(S("table_full"), 1)
        for j in range(4):
            dve.wait_ge(S("table_hi"), j + 1)
            dve.tensor_tensor(table_lo[:, j, :], table[:, j, :], table_hi[:, j, :].bitcast(F32), ALU.subtract).then_inc(S("table_ready"), 1)

    def dsa_vector(dve):
        def steps(u):
            keys = (u // 8 + 1) * P
            if u >= 2:
                full(dve, ("ds", u - 2))
            for i in range(4 * u, 4 * u + 4):
                dve.tensor_scalar(step[i % NSTEP][:, 0:keys], posf[:, 0:keys], qfrom[:, i:i + 1], None, ALU.is_ge).then_inc(S("step_ready"), 1)

        def maxima(u):
            b = full(dve, ("ds", u))
            dve.tensor_reduce(sm["dsa_max"][u % 2][:, :], ps[:, b, 0:(u // 8 + 1) * P], AX, ALU.max, negate=True).then_inc(S("dsa_max"), 1)

        def outputs(u):
            if u % 4 == 3:
                full(dve, ("oa", u // 4))
                for half in range(2):
                    src, hi, lo = oa_views(u // 4, half)
                    dve.wait_ge(S("oa_hi"), 2 * (u // 4) + 2)
                    dve.tensor_tensor(lo, src, hi.bitcast(F32), ALU.subtract).then_inc(S("oa_ready"), 1)

        steps(0)
        steps(1)
        maxima(0)
        steps(2)
        maxima(1)
        for u in dsa_units:
            keys = (u // 8 + 1) * P
            read(dve, ("ds", u))
            mark("dsa_step", dve.reciprocal(sm["dsa_inv"][u % 2][:, :], sm["dsa_sum"][u % 2][:, :]))
            settle(dve, "dsa_step")
            dve.tensor_scalar(pp[u % 2][:, 0:keys], pp[u % 2][:, 0:keys], sm["dsa_inv"][u % 2][:, :], None, ALU.mult)\
               .then_inc(S("pp_ready"), 1)
            if u + 3 < len(dsa_units):
                steps(u + 3)
            if u + 2 < len(dsa_units):
                maxima(u + 2)
            if u:
                outputs(u - 1)
        outputs(dsa_units[-1])

    def gated_tensor(pe, x, hi, lo, ready):
        second["g_gated_" + x] = len(slot_of)
        for pair in range(KD // 2):
            for z in range(2):
                m, b = 2 * pair + z, 4 * (pair % 2) + z
                at = IN2["g" + x] + m * P
                g = take_slot(pe, in2((at, at + P, 0)))
                claim(pe, b, ("g" + x, m))
                for k in range(KD):
                    mm = three_passes(pe, ps[:, b, :], g, k, P, hh[:, k, :], hl[:, k, :], k == 0, k == KD - 1)
                mm.then_inc(bank_full(b), 1)
                after[g] = (bank_full(b), bank_uses[b])
            g = take_slot(pe, ("w_o_" + x + "_2", [(k * P, P, ((m * P, m * P + P, 0),)) for m in (2 * pair, 2 * pair + 1) for k in range(4)]))
            if pair == 0:
                pe.wait_ge(*ready)
            for z in range(2):
                m, b = 2 * pair + z, 4 * (pair % 2) + 2 + z
                claim(pe, b, ("p" + x, m))
                for k in range(4):
                    mm = three_passes(pe, ps[:, b, :], g, 4 * z + k, P, hi[:, k, :], lo[:, k, :], k == 0, k == 3)
                mm.then_inc(bank_full(b), 1)
                after[g] = (bank_full(b), bank_uses[b])

    def gated_scalar(act, x):
        g0 = second["g_gated_" + x]
        for pair in range(KD // 2):
            for z in range(2):
                m = 2 * pair + z
                b = full(act, ("g" + x, m))
                split_slots(act, g0 + 3 * pair + z + 2)
                if m >= 4:
                    if x == "a":
                        act.wait_ge(S("y_ready"), m - 3)
                    else:
                        read(act, ("pb", m - 4))
                act.activation(sig[m % 4][:, :], ps[:, b, :], ACT.Sigmoid).then_inc(bank_empty(b), 1)
            full(act, ("p" + x, 2 * pair + 1))
            split_slots(act, g0 + 3 * pair + 4)
            if x == "a":
                for m in (2 * pair, 2 * pair + 1):
                    act.wait_ge(S("y_sum"), m + 1)
                    act.activation(yh[:, m, :], sig[m % 4][:, :], ACT.Copy).then_inc(S("y_hi"), 1)

    def gated_vector_b(dve):
        late = ROUNDS - EARLY_ROUNDS
        for m in range(KD):
            for _ in range(min(late, m * late // (KD - 1)), min(late, (m + 1) * late // (KD - 1))):
                topk_round(dve)
            if m == KD - 1:
                topk_end(dve)
            read(dve, ("gb", m))
            b = full(dve, ("pb", m))
            dve.tensor_tensor(y_b[:, m, :], sig[m % 4][:, :], ps[:, b, :], ALU.mult).then_inc(bank_empty(b), 1)
        read(dve, ("pb", KD - 1))

    def gated_vector_a(dve):
        for m in range(KD):
            read(dve, ("ga", m))
            b = full(dve, ("pa", m))
            dve.tensor_tensor(sig[m % 4][:, :], sig[m % 4][:, :], ps[:, b, :], ALU.mult).then_inc(bank_empty(b), 1)
            read(dve, ("pa", m))
            dve.tensor_tensor(sig[m % 4][:, :], sig[m % 4][:, :], y_b[:, m, :], ALU.add).then_inc(S("y_sum"), 1)
            dve.wait_ge(S("y_hi"), m + 1)
            dve.tensor_tensor(yl[:, m, :], sig[m % 4][:, :], yh[:, m, :].bitcast(F32), ALU.subtract).then_inc(S("y_ready"), 1)

    def scaled(dve, to, scale, gains):
        mark("gain_ready", dve.scalar_tensor_tensor(out=to[:, :], in0=scale, scalar=1.0, in1=gains, op0=ALU.add, op1=ALU.mult))

    def half_gain(dve, n, at):
        mark("gain_ready", dve.tensor_scalar(half_gate[n][:, :], ada[:, at:at + KD], 0.5, None, ALU.mult))
        settle(dve, "gain_ready")

    def gains_1(dve):
        scaled(dve, gain["x1"], mod[:, 8:16, 0], v("norm1_g"))
        settle(dve, "gain_ready")

    def gains_2(dve):
        scaled(dve, gain["x2"], mod[:, 32:40, 0], v("norm2_g"))
        settle(dve, "gain_ready")

    def gains_3(dve):
        scaled(dve, gain["f1"], ada[:, 8:16], v("g_ffn1"))
        scaled(dve, gain["mx"], ada[:, 32:40], v("g_mix"))
        scaled(dve, gain["f2"], ada[:, 56:64], v("g_ffn2"))
        half_gain(dve, "f1", 16)

    def of(t):
        return lambda k: t[:, k:k + 1]

    def x_shift(at, which=0):
        return lambda k: mod[:, at + k, which:which + 1]

    def after_chunk(key):
        return lambda e, k: e.wait_ge(*residual(key, k + 1))

    def x_loaded(e, k):
        e.wait_ge(S(f"x_loaded{k // 4}"), 16)

    def c_loaded(e, k):
        e.wait_ge(S("c_loaded"), 16)

    block = ctx.enter_context(nc.Block())

    @block.tensor
    def _(pe):
        pe.wait_ge(S("cst_loaded"), 16)
        pe.wait_ge(S("vec_loaded"), 16)
        modulation_slots(2 * KD)
        norm_tensor(pe, "nx", KD, N, 4, 4)
        projections_tensor(pe)
        diff_tensor(pe)
        gla_tensor(pe)
        firsts["mix1"] = len(slot_of)
        for pair in range(4):
            new_slot(half_slots(pair, 0))
        half_mixed_tensor(pe, "mix1", 0, firsts["mix1"], 0, "ng", "n2")
        norm_tensor(pe, "n2", KD, N, 4, 5, KD - SUM_LAG)
        ffn_tensor(pe, "ffn1", "n2", "w_ffn_in", "w_ffn_out")
        norm_tensor(pe, "nf1", KD, N, 4, 5)
        ffn_tensor(pe, "ffn2", "nf1", "w_ffn1_in_2", "w_ffn1_down_2")
        norm_tensor(pe, "nm", KD, N, 4, 5)
        proj2_tensor(pe)
        lora_tensor(pe)
        mla_tensor(pe)
        gated_tensor(pe, "b", obh, obl, (S("ob_ready"), HEADS))
        dsa_tensor(pe)
        gated_tensor(pe, "a", oah, oal, (S("oa_ready"), 2 * N // (4 * QG)))
        firsts["mix2"] = len(slot_of)
        mixed_tensor(pe, "mix2", "w_out_2", yh, yl, [(S("y_ready"), k + 1) for k in range(KD)], "nf2")
        norm_tensor(pe, "nf2", KD, N, 4, 5, KD - SUM_LAG)
        ffn_tensor(pe, "ffn3", "nf2", "w_ffn2_in_2", "w_ffn2_down_2")
        norm_tensor(pe, "nfin", KD, N, 4, 5)

    @block.scalar
    def _(act):
        act.wait_ge(S("vec_loaded"), 16)
        act.wait_ge(S("cst_loaded"), 16)
        act.wait_ge(S("cond_loaded"), 16)
        act.activation(cond[:, :], cond[:, :], ACT.Silu).then_inc(S("cond_ready"), 1)
        act.wait_ge(S("cond_ctx_loaded"), 16)
        act.activation(cond_ctx[:, :], cond_ctx[:, :], ACT.Silu).then_inc(S("cond_ready"), 1)
        act.wait_ge(S("cond_ada_loaded"), 16)
        act.activation(cond_ada[:, :], cond_ada[:, :], ACT.Silu).then_inc(S("cond_ready"), 1)
        norm_scalar(act, "nx", xT, KD, N, D, hh, x_shift(0), x_loaded, lambda: split_slots(act, 1))
        projections_scalar(act)
        diff_scalar(act, lambda: split_slots(act, firsts["mix1_diff"] + 1))
        gla_scalar(act)
        split_slots(act, firsts["mix1"] + 1)
        half_mixed_scalar(act, "mix1", firsts["mix1"], "n2")
        norm_scalar(act, "n2", xT, KD, N, D, hh, x_shift(24), None)
        ffn_scalar(act, "ffn1")
        norm_scalar(act, "nf1", xT, KD, N, D, hh, of(ada), after_chunk("ffn1"), lambda: split_slots(act, ffns["ffn2"]["g0"] + 1))
        ffn_scalar(act, "ffn2")
        norm_scalar(act, "nm", xT, KD, N, D, hh, lambda k: ada[:, 24 + k:25 + k], after_chunk("ffn2"),
                    lambda: split_slots(act, second["g_proj"] + 1))
        act.dma_start(posi[:, :], A["posi"]).then_inc(S("posi_loaded"), 16)
        act.dma_start(qposi[:, :], A["qposi"]).then_inc(S("qposi_loaded"), 16)
        proj2_scalar(act)
        lora_scalar(act)
        mla_scalar(act)
        table_scalar(act)
        gated_scalar(act, "b")
        dsa_scalar(act)
        gated_scalar(act, "a")
        mixed_scalar(act, "mix2", firsts["mix2"], "nf2")
        norm_scalar(act, "nf2", xT, KD, N, D, hh, lambda k: ada[:, 48 + k:49 + k], None)
        ffn_scalar(act, "ffn3")
        norm_scalar(act, "nfin", xT, KD, N, D, None, None, after_chunk("ffn3"))

    @block.vector
    def _(dve):
        dve.wait_ge(S("vec_loaded"), 16)
        dve.wait_ge(S("cst_loaded"), 16)
        modulations(dve, [("w_mod", j) for j in range(2 * KD)])
        norm_modulation(dve, "w_mod", 0)
        gains_1(dve)
        x_loaded(dve, 0)
        x_loaded(dve, KD - 1)
        norm_vector(dve, "nx", xT, KD, N, of(gain["x1"]), hh, hl, x_shift(0))
        projections_vector(dve)
        diff_vector(dve)
        gla_vector(dve)
        mixed_vector(dve, "mix1", mix_gate)
        modulation_biases(dve, "w_ada_2")
        gains_2(dve)
        norm_vector(dve, "n2", xT, KD, N, of(gain["x2"]), hh, hl, x_shift(24))
        ffn_vector(dve, "ffn1", lambda m: mod[:, 40 + m, 0:1])
        gains_3(dve)
        norm_vector(dve, "nf1", xT, KD, N, of(gain["f1"]), hh, hl, of(ada))
        ffn_vector(dve, "ffn2", of(half_gate["f1"]))
        norm_vector(dve, "nm", xT, KD, N, of(gain["mx"]), hh, hl, lambda k: ada[:, 24 + k:25 + k])
        dve.wait_ge(S("posi_loaded"), 16)
        dve.wait_ge(S("qposi_loaded"), 16)
        proj2_vector(dve)
        lora_vector(dve)
        mla_vector(dve)
        table_vector(dve)
        gated_vector_b(dve)
        dsa_vector(dve)
        gated_vector_a(dve)
        mixed_vector(dve, "mix2", lambda m: ada[:, 40 + m:41 + m])
        norm_vector(dve, "nf2", xT, KD, N, of(gain["f2"]), hh, hl, lambda k: ada[:, 48 + k:49 + k])
        ffn_vector(dve, "ffn3", of(half_gate["f2"]))
        norm_vector(dve, "nfin", xT, KD, N, lambda k: v("g_final", k, k + 1), None, None, None, out=fin)

    @block.gpsimd
    def _(pool):
        split_lows(pool, 0, len(chunks_a))
        diff_gpsimd(pool)
        split_lows(pool, len(chunks_a), len(chunks_a) + 4)
        gla_gpsimd(pool)
        split_lows(pool, len(chunks_a) + 4, ffns["ffn1"]["g0"])
        ffn_gpsimd(pool, "ffn1")
        ffn_gpsimd(pool, "ffn2")
        split_lows(pool, ffns["ffn2"]["g1"] + KF, ffns["ffn3"]["g0"])
        ffn_gpsimd(pool, "ffn3")

    @block.sync
    def _(sp):
        sp.dma_start(vec[:, :], A["vec"]).then_inc(S("vec_loaded"), 16)
        sp.dma_start(cst[:, :], A["cst"]).then_inc(S("cst_loaded"), 16)
        sp.dma_start(cond[:, :], A["cond"][:, 0, :]).then_inc(S("cond_loaded"), 16)
        sp.dma_start(cond_ctx[:, :], A["cond_ctx"]).then_inc(S("cond_ctx_loaded"), 16)
        for s in range(RING):
            sp.dma_start(raw[s][:, :], A["stream"][s * P:(s + 1) * P, :]).then_inc(S(f"landed{s}"), 16)
        for i in range(2):
            sp.dma_start(xT[:, 4 * i:4 * i + 4, :], A["xT"][:, 4 * i:4 * i + 4, :]).then_inc(S(f"x_loaded{i}"), 16)
        sp.dma_start(cond_ada[:, :], A["cond"][:, 1, :]).then_inc(S("cond_ada_loaded"), 16)
        sp.dma_start(cT[:, :, :], A["cT"]).then_inc(S("c_loaded"), 16)
        sp.dma_start(csta[:, :], A["csta"]).then_inc(S("csta_loaded"), 16)
        with sp.Fori(1, len(stream) // RING) as it:
            for s in range(RING):
                sp.wait_ge(S(f"spent{s}"), it)
                sp.dma_start(raw[s][:, :], A["stream"][bass.ds(it * (RING * P) + s * P, P), :]).then_inc(S(f"landed{s}"), 16)
        for k in range(KD):
            sp.wait_ge(*norm("nfin", "t1", k + 1))
            sp.dma_start(A["out"][:, k, :], fin[:, k, :]).then_inc(S("stored"), 16)
        sp.wait_ge(S("stored"), 16 * KD)

    assert len(stream) == N_SLOTS and len(stream) % RING == 0
    ctx.close()
    return stream


def constants():
    p = np.arange(P)
    stay = np.zeros((P, NCST), np.float32)
    first = np.zeros((P, NCSTA), np.float32)

    def put(to, table, name, value):
        o, w = table[name]
        to[:, o:o + w] = value

    put(stay, CST, "ident", np.eye(P))
    put(stay, CST, "one", 1.0)
    put(stay, CST, "comp", p[:, None] // DIFF_DH == np.arange(2))
    put(stay, CST, "eps", EPS)
    half = ROPE2 // 2
    turn = np.zeros((P, ROPE2))
    for i in range(half):
        turn[DH2 + half + i, i] = -1.0
        turn[DH2 + i, half + i] = 1.0
    put(stay, CST, "rot2", turn)
    freq = np.float32(10000.0) ** (np.float32(-2.0) * np.arange(half, dtype=np.float32) / np.float32(ROPE2))
    put(stay, CST, "freq", freq[p % half][:, None])
    put(stay, CST, "bucket_from", np.array(BUCKET_FROM)[p % 32][:, None])
    put(stay, CST, "own_query", np.concatenate([np.arange(QG) == 4 * j + p[:, None] // 32 for j in range(4)], axis=1))

    rot = np.zeros((P, P))
    for o in range(0, P, 32):
        for i in range(16):
            rot[o + 16 + i, o + i] = -1.0
            rot[o + i, o + 16 + i] = 1.0
    put(first, CSTA, "rot", rot)
    t = np.arange(N)
    inv_freq = np.float32(10000.0) ** (-np.arange(16, dtype=np.float32) / np.float32(16))
    axis = (p % DIFF_DH) // 32
    at = np.where(axis[:, None] == 0, t // GRID_W, t % GRID_W).astype(np.float32)
    angle = at * inv_freq[p % 16][:, None]
    put(first, CSTA, "cos", np.cos(angle))
    put(first, CSTA, "sin", np.sin(angle))
    put(first, CSTA, "carry", (t % P != 0)[None, :])
    levels = [2.0 * np.eye(P)] + [(p[:, None] // (2 * s) == p // (2 * s)) & (p[:, None] // s != p // s) for s in LEVELS]
    put(first, CSTA, "levels", np.concatenate(levels, axis=1))
    return stay, first


def small_vectors(a):
    out = np.zeros((P, NVEC), np.float32)

    def put(name, value):
        o, w = VEC[name]
        out[:value.shape[0], o:o + w] = value

    def columns(w):
        return w.reshape(-1, P).T

    for name, src in (("norm1_g", "norm1_g"), ("norm2_g", "norm2_g"), ("g_ffn1", "g_ffn1_2"), ("g_mix", "g_mix_2"), ("g_ffn2", "g_ffn2_2"),
                      ("g_final", "g_final_2"), ("b_mod", "b_mod"), ("b_ada", "b_ada_2"), ("gla_g", "gla_norm_g"),
                      ("dn_g", "diff_norm_g"), ("g_cq", "g_cq_2"), ("g_ckv", "g_ckv_2"), ("gate_b", "gla_gate_bias")):
        put(name, columns(a[src]))
    put("dq_g", columns(np.tile(a["diff_q_norm_g"].reshape(-1), 2)))
    put("dk_g", columns(np.tile(a["diff_k_norm_g"].reshape(-1), 2)))
    put("lam_q", np.tile(a["diff_lambda_q"].reshape(1, -1), (P, 1)))
    put("lam_k", np.tile(a["diff_lambda_k"].reshape(1, -1), (P, 1)))
    up = np.zeros((32, 512), np.float32)
    for z in range(2):
        up[16 * z:16 * z + 16, 256 * z:256 * z + 256] = a["gla_gate_up"][0, z]
    put("gate_up", up)
    bias_at, bias_before = np.zeros((P, H2), np.float32), np.zeros((P, H2), np.float32)
    for p in range(P):
        if p % 32 < 31:
            bias_at[p] = a["rel_bias_2"][BUCKETS[p % 32]]
        if 1 <= p % 32 < 31:
            bias_before[p] = a["rel_bias_2"][BUCKETS[p % 32 - 1]]
    put("bias_at", bias_at)
    put("bias_before", bias_before)
    return out


def stream_array(a, stream):
    out = np.zeros((len(stream), P, KD, P), np.float32)
    for n, (name, tiles) in enumerate(stream):
        if isinstance(tiles, int):
            w = a[name].reshape(D, -1)
            out[n] = w[:, tiles * P:(tiles + 1) * P].T.reshape(P, KD, P)
            continue
        for i, tile in enumerate(tiles):
            source, row, rows, cuts = tile if not name else (name,) + tile
            w = a[source].reshape(a[source].shape[-2:])
            for c0, c1, to in cuts:
                out[n, :rows, i, to:to + c1 - c0] = w[row:row + rows, c0:c1]
    return out.reshape(len(stream) * P, KD * P)


def kernel(**inputs):
    import concourse.bacc as bacc
    from concourse.bass_utils import run_bass_kernel_spmd

    a = {name: np.asarray(value) for name, value in inputs.items()}
    positions = a["positions_2"].reshape(N)
    cst, csta = constants()
    arrays = {
        "vec": small_vectors(a), "cst": cst, "csta": csta,
        "xT": np.ascontiguousarray(a["x"].reshape(N, KD, P).transpose(2, 1, 0)),
        "cT": np.ascontiguousarray(a["ctx"].reshape(NCTX, KD, P).transpose(2, 1, 0)),
        "cond": np.ascontiguousarray(np.broadcast_to(np.stack([a["c"].reshape(D), a["c_2"].reshape(D)]), (P, 2, D))),
        "cond_ctx": np.ascontiguousarray(np.broadcast_to(a["c_ctx"], (P, D))),
        "posi": np.ascontiguousarray(np.broadcast_to(positions, (P, N))),
        "qposi": np.ascontiguousarray(np.repeat(positions.reshape(P, 4).T, 32, axis=0)),
    }
    nc = bacc.Bacc("TRN2", target_bir_lowering=False, num_devices=1)
    A = {name: nc.dram_tensor(name, v.shape, mybir.dt.from_np(v.dtype), kind="ExternalInput").ap() for name, v in arrays.items()}
    A["stream"] = nc.dram_tensor("stream", (N_SLOTS * P, SLOT), F32, kind="ExternalInput").ap()
    A["out"] = nc.dram_tensor("out", (P, KD, N), F32, kind="ExternalOutput").ap()
    arrays["stream"] = stream_array(a, build(nc, A))
    r = run_bass_kernel_spmd(nc, [arrays], core_ids=[0])
    return r.results[0]["out"].transpose(2, 1, 0).reshape(1, N, D)
```
